# Optimizing a Trainium2 kernel written in Bass

```python
import math
import jax, jax.numpy as jnp
from jax import lax
import numpy as np
import jax
import jax.numpy as jnp

D_MODEL = 2048
BATCH = 1
SEQ = 256
DEPTH = 1

HEAD_DIM = 128
MOBA_HEADS = D_MODEL // (2 * HEAD_DIM)
MOBA_BLOCK = 256
MOBA_TOPK = 3
MOBA_Q_CHUNK = 64
DIFF_HEADS = D_MODEL // (4 * HEAD_DIM)
DIFF_V_DIM = 2 * HEAD_DIM
DIFF_Q_BLOCK = 128
ROT_DIM = HEAD_DIM // 4
ROPE_THETA = 500000.0
D_FF = 4 * D_MODEL
PLE_DIM = 256
NORM_EPS = 1e-6
MOBA_WIDTH = MOBA_HEADS * HEAD_DIM
DIFF_QK_WIDTH = DIFF_HEADS * 2 * HEAD_DIM
DIFF_V_WIDTH = DIFF_HEADS * DIFF_V_DIM
IN_WIDTH = 3 * MOBA_WIDTH + 2 * DIFF_QK_WIDTH + DIFF_V_WIDTH + 2 * D_MODEL


F32 = jnp.float32

def rmsnorm(x, g):
    xf = x.astype(F32)
    y = xf * lax.rsqrt(jnp.mean(xf * xf, axis=-1, keepdims=True) + NORM_EPS)
    return (y * g.astype(F32)).astype(x.dtype)

def partial_rope(x, pos_f):
    half = ROT_DIM // 2
    inv_freq = 1.0 / (ROPE_THETA ** (jnp.arange(half, dtype=F32) * 2.0 / ROT_DIM))
    ang = pos_f[:, None] * inv_freq[None, :]
    cos, sin = jnp.cos(ang), jnp.sin(ang)
    xf = x.astype(F32)
    x1 = xf[..., :half]
    x2 = xf[..., half:ROT_DIM]
    out = jnp.concatenate([x1 * cos - x2 * sin, x2 * cos + x1 * sin, xf[..., ROT_DIM:]], axis=-1)
    return out.astype(x.dtype)

def moba_attention(q, k, v):
    B, H, S, Dh = q.shape
    nb = -(-S // MOBA_BLOCK)
    topk = min(MOBA_TOPK, nb)
    pad = nb * MOBA_BLOCK - S
    k_p = jnp.pad(k, ((0, 0), (0, 0), (0, pad), (0, 0)))
    v_p = jnp.pad(v, ((0, 0), (0, 0), (0, pad), (0, 0)))
    k_blk = k_p.reshape(B, H, nb, MOBA_BLOCK, Dh)
    v_blk = v_p.reshape(B, H, nb, MOBA_BLOCK, Dh)
    k_mean = jnp.mean(k_blk.astype(F32), axis=3)
    nc = S // MOBA_Q_CHUNK
    q_ch = jnp.moveaxis(q.reshape(B, H, nc, MOBA_Q_CHUNK, Dh), 2, 0)
    bi = jnp.arange(B)[:, None, None, None]
    hi = jnp.arange(H)[None, :, None, None]
    blk_ids = jnp.arange(nb)
    scale = Dh ** -0.5

    def chunk(args):
        ci, qc = args
        q_start = ci * MOBA_Q_CHUNK
        cur = q_start // MOBA_BLOCK
        gate = jnp.einsum('bhqd,bhnd->bhqn', qc.astype(F32), k_mean)
        gate = jnp.where(blk_ids < cur, gate, -jnp.inf)
        _, idx = lax.top_k(gate, topk)
        valid = idx < cur
        k_sel = k_blk[bi, hi, idx]
        v_sel = v_blk[bi, hi, idx]
        s_sel = jnp.einsum('bhqd,bhqjkd->bhqjk', qc, k_sel).astype(F32) * scale
        s_sel = jnp.where(valid[..., None], s_sel, -jnp.inf)
        s_sel = s_sel.reshape(B, H, MOBA_Q_CHUNK, topk * MOBA_BLOCK)
        own0 = cur * MOBA_BLOCK
        k_own = lax.dynamic_slice_in_dim(k_p, own0, MOBA_BLOCK, axis=2)
        v_own = lax.dynamic_slice_in_dim(v_p, own0, MOBA_BLOCK, axis=2)
        s_own = jnp.einsum('bhqd,bhkd->bhqk', qc, k_own).astype(F32) * scale
        q_pos = q_start + jnp.arange(MOBA_Q_CHUNK)
        k_pos = own0 + jnp.arange(MOBA_BLOCK)
        s_own = jnp.where(k_pos[None, :] <= q_pos[:, None], s_own, -jnp.inf)
        probs = jax.nn.softmax(jnp.concatenate([s_sel, s_own], axis=-1), axis=-1).astype(v.dtype)
        p_sel = probs[..., :topk * MOBA_BLOCK].reshape(B, H, MOBA_Q_CHUNK, topk, MOBA_BLOCK)
        p_own = probs[..., topk * MOBA_BLOCK:]
        return (jnp.einsum('bhqjk,bhqjkd->bhqd', p_sel, v_sel)
                + jnp.einsum('bhqk,bhkd->bhqd', p_own, v_own))

    out = lax.map(chunk, (jnp.arange(nc), q_ch))
    return jnp.moveaxis(out, 0, 2).reshape(B, H, S, Dh)

def diff_attention(q, k, v, lam, sub_g, lambda_init):
    B, H, _, S, Dh = q.shape
    nq = S // DIFF_Q_BLOCK
    q_bl = jnp.moveaxis(q.reshape(B, H, 2, nq, DIFF_Q_BLOCK, Dh), 3, 0)
    k_pos = jnp.arange(S)
    scale = Dh ** -0.5

    def block(args):
        bidx, qb = args
        s = jnp.einsum('bhcqd,bhckd->bhcqk', qb, k).astype(F32) * scale
        q_pos = bidx * DIFF_Q_BLOCK + jnp.arange(DIFF_Q_BLOCK)
        s = jnp.where(k_pos[None, :] <= q_pos[:, None], s, -jnp.inf)
        pr = jax.nn.softmax(s, axis=-1)
        attn = (pr[:, :, 0] - lam * pr[:, :, 1]).astype(v.dtype)
        return jnp.einsum('bhqk,bhkd->bhqd', attn, v)

    out = lax.map(block, (jnp.arange(nq), q_bl))
    out = jnp.moveaxis(out, 0, 2).reshape(B, H, S, DIFF_V_DIM)
    return (rmsnorm(out, sub_g) * (1.0 - lambda_init)).astype(v.dtype)

def first_inputs(seed: int = 0) -> dict:
    key = jax.random.key(seed)
    ks = jax.random.split(key, 24)
    n = lambda k_, shape, s: jax.random.normal(k_, shape, F32) * s
    gain = lambda k_, dim: 1.0 + 0.02 * jax.random.normal(k_, (DEPTH, dim), F32)
    return {
        "x": n(ks[0], (BATCH, SEQ, D_MODEL), 1.0),
        "p": n(ks[1], (DEPTH, BATCH, SEQ, PLE_DIM), 1.0),
        "w_in": n(ks[2], (DEPTH, D_MODEL, IN_WIDTH), D_MODEL ** -0.5),
        "w_br_moba": n(ks[3], (DEPTH, MOBA_WIDTH, D_MODEL), MOBA_WIDTH ** -0.5),
        "w_br_diff": n(ks[4], (DEPTH, DIFF_V_WIDTH, D_MODEL), DIFF_V_WIDTH ** -0.5),
        "w_out": n(ks[5], (DEPTH, D_MODEL, D_MODEL), D_MODEL ** -0.5),
        "lambda_q1": n(ks[6], (DEPTH, HEAD_DIM), 0.1),
        "lambda_k1": n(ks[7], (DEPTH, HEAD_DIM), 0.1),
        "lambda_q2": n(ks[8], (DEPTH, HEAD_DIM), 0.1),
        "lambda_k2": n(ks[9], (DEPTH, HEAD_DIM), 0.1),
        "diff_subln_g": gain(ks[10], DIFF_V_DIM),
        "g_mix_pre": gain(ks[11], D_MODEL),
        "g_mix_post": gain(ks[12], D_MODEL),
        "w_up": n(ks[13], (DEPTH, D_MODEL, D_FF), D_MODEL ** -0.5),
        "w_down": n(ks[14], (DEPTH, D_FF, D_MODEL), D_FF ** -0.5),
        "g_mlp_pre": gain(ks[15], D_MODEL),
        "g_mlp_post": gain(ks[16], D_MODEL),
        "w_ple_proj": n(ks[17], (DEPTH, PLE_DIM, D_MODEL), PLE_DIM ** -0.5),
        "w_ple_gate": n(ks[18], (DEPTH, D_MODEL, D_MODEL), D_MODEL ** -0.5),
        "g_ple_pre": gain(ks[19], D_MODEL),
        "g_ple_post": gain(ks[20], D_MODEL),
    }

def first_block(x, p, w_in, w_br_moba, w_br_diff, w_out, lambda_q1, lambda_k1, lambda_q2, lambda_k2,
              diff_subln_g, g_mix_pre, g_mix_post, w_up, w_down, g_mlp_pre, g_mlp_post,
              w_ple_proj, w_ple_gate, g_ple_pre, g_ple_post):
    B, S, _ = x.shape
    pos_f = jnp.arange(S, dtype=F32)
    widths = [MOBA_WIDTH, MOBA_WIDTH, MOBA_WIDTH, DIFF_QK_WIDTH, DIFF_QK_WIDTH, DIFF_V_WIDTH, D_MODEL]
    split_points = [int(v) for v in np.cumsum(widths)]
    h = x
    for i in range(DEPTH):
        lambda_init = 0.8 - 0.6 * math.exp(-0.3 * i)
        u = rmsnorm(h, g_mix_pre[i])
        proj = u @ w_in[i]
        qa, ka, va, qb, kb, vb, ga, gb = jnp.split(proj, split_points, axis=-1)
        to_heads = lambda t: t.reshape(B, S, MOBA_HEADS, HEAD_DIM).transpose(0, 2, 1, 3)
        qa = partial_rope(to_heads(qa), pos_f)
        ka = partial_rope(to_heads(ka), pos_f)
        va = to_heads(va)
        oa = moba_attention(qa, ka, va)
        to_sub = lambda t: t.reshape(B, S, DIFF_HEADS, 2, HEAD_DIM).transpose(0, 2, 3, 1, 4)
        qb = partial_rope(to_sub(qb), pos_f)
        kb = partial_rope(to_sub(kb), pos_f)
        vb = vb.reshape(B, S, DIFF_HEADS, DIFF_V_DIM).transpose(0, 2, 1, 3)
        lam = (jnp.exp(jnp.sum(lambda_q1[i].astype(F32) * lambda_k1[i].astype(F32)))
               - jnp.exp(jnp.sum(lambda_q2[i].astype(F32) * lambda_k2[i].astype(F32)))
               + lambda_init)
        ob = diff_attention(qb, kb, vb, lam, diff_subln_g[i], lambda_init)
        ya = oa.transpose(0, 2, 1, 3).reshape(B, S, MOBA_WIDTH) @ w_br_moba[i]
        yb = ob.transpose(0, 2, 1, 3).reshape(B, S, DIFF_V_WIDTH) @ w_br_diff[i]
        mixed = jax.nn.sigmoid(ga) * ya + jax.nn.sigmoid(gb) * yb
        h = h + rmsnorm(mixed @ w_out[i], g_mix_post[i])
        u2 = rmsnorm(h, g_mlp_pre[i])
        ff = jnp.square(jax.nn.relu(u2 @ w_up[i])) @ w_down[i]
        h = h + rmsnorm(ff, g_mlp_post[i])
        gate = jax.nn.sigmoid(rmsnorm(h, g_ple_pre[i]) @ w_ple_gate[i])
        e = (p[i] @ w_ple_proj[i]) * gate
        h = h + rmsnorm(e, g_ple_post[i])
    return h


DEPTH_2 = 2

N_MIXERS = 2
N_RET_LAYERS = (DEPTH_2 + 1) // 2
N_MLA_LAYERS = DEPTH_2 // 2
EPS = 1e-6
ROPE_BASE = 10000.0
BLOCK = 128

RET_HEADS = 8
RET_DK = D_MODEL // RET_HEADS
RET_DV = 2 * RET_DK
RET_WIDTH = RET_HEADS * RET_DV
RET_QK = RET_HEADS * RET_DK
RET_IN = 2 * RET_QK + 2 * RET_WIDTH

MLA_HEADS = 16
MLA_NOPE = 128
MLA_ROPE = 64
MLA_V = 128
MLA_Q_RANK = 512
MLA_KV_RANK = 512
MLA_WIDTH = MLA_HEADS * MLA_V
MLA_IN = MLA_Q_RANK + MLA_KV_RANK + MLA_ROPE + MLA_WIDTH


def rmsnorm_2(x, g):
    xf = x.astype(jnp.float32)
    y = xf * lax.rsqrt(jnp.mean(xf * xf, axis=-1, keepdims=True) + EPS)
    return (y * g.astype(jnp.float32)).astype(x.dtype)

def rope(x, pos):
    d = x.shape[-1]
    inv_freq = ROPE_BASE ** (-jnp.arange(0, d, 2, dtype=jnp.float32) / d)
    ang = pos.astype(jnp.float32)[:, :, None, None] * inv_freq
    cos = jnp.cos(ang).astype(x.dtype)
    sin = jnp.sin(ang).astype(x.dtype)
    x1, x2 = x[..., : d // 2], x[..., d // 2:]
    return jnp.concatenate([x1 * cos - x2 * sin, x2 * cos + x1 * sin], axis=-1)

def chunkwise_retention(q, k, v):
    B, S, H, _ = q.shape
    nc = S // BLOCK
    log_gamma = jnp.log1p(-jnp.exp2(-5.0 - jnp.arange(H, dtype=jnp.float32)))
    idx = jnp.arange(BLOCK, dtype=jnp.float32)
    diff = idx[:, None] - idx[None, :]
    d_intra = jnp.where(diff >= 0, jnp.exp(log_gamma[:, None, None] * jnp.maximum(diff, 0.0)), 0.0)
    xi = jnp.exp(log_gamma[:, None] * (idx + 1.0))[None, :, :, None]
    zeta = jnp.exp(log_gamma[:, None] * (BLOCK - 1.0 - idx))[None, :, :, None]
    chunk_decay = jnp.exp(log_gamma * BLOCK)[None, :, None, None]

    def to_chunks(t):
        return t.astype(jnp.float32).reshape(B, nc, BLOCK, H, t.shape[-1]).transpose(1, 0, 3, 2, 4)

    def step(state, inp):
        qi, ki, vi = inp
        scores = jnp.einsum('bhnd,bhmd->bhnm', qi, ki) * d_intra
        inner = jnp.einsum('bhnm,bhmv->bhnv', scores, vi)
        cross = jnp.einsum('bhnd,bhdv->bhnv', qi, state) * xi
        state = state * chunk_decay + jnp.einsum('bhmd,bhmv->bhdv', ki, vi * zeta)
        return state, inner + cross

    state0 = jnp.zeros((B, H, q.shape[-1], v.shape[-1]), jnp.float32)
    _, out = lax.scan(step, state0, (to_chunks(q), to_chunks(k), to_chunks(v)))
    return out.transpose(1, 0, 3, 2, 4).reshape(B, S, H, v.shape[-1])

def retention_branch(h, pos, w_in, gn_g, w_out):
    B, S, _ = h.shape
    proj = h @ w_in
    q, k, v, g = jnp.split(proj, [RET_QK, 2 * RET_QK, 2 * RET_QK + RET_WIDTH], axis=-1)
    q = rope(q.reshape(B, S, RET_HEADS, RET_DK), pos)
    k = rope(k.reshape(B, S, RET_HEADS, RET_DK), pos) * (RET_DK ** -0.5)
    v = v.reshape(B, S, RET_HEADS, RET_DV)
    y = chunkwise_retention(q, k, v)
    mu = jnp.mean(y, axis=-1, keepdims=True)
    var = jnp.mean(jnp.square(y - mu), axis=-1, keepdims=True)
    y = (y - mu) * lax.rsqrt(var + EPS)
    y = (y.reshape(B, S, RET_WIDTH) * gn_g.astype(jnp.float32)).astype(h.dtype)
    return (jax.nn.silu(g) * y) @ w_out

def causal_block_attention(q, k, v):
    B, S, H, dq = q.shape
    nb = S // BLOCK
    scale = dq ** -0.5
    qb = q.reshape(B, nb, BLOCK, H, dq).transpose(1, 0, 3, 2, 4)
    kt = k.transpose(0, 2, 1, 3)
    vt = v.transpose(0, 2, 1, 3)
    key_pos = jnp.arange(S)

    def one_block(args):
        i, qi = args
        s = jnp.einsum('bhqd,bhkd->bhqk', qi, kt).astype(jnp.float32) * scale
        qpos = i * BLOCK + jnp.arange(BLOCK)
        s = jnp.where(key_pos[None, :] <= qpos[:, None], s, -1e30)
        p = jax.nn.softmax(s, axis=-1).astype(vt.dtype)
        return jnp.einsum('bhqk,bhkd->bhqd', p, vt)

    o = lax.map(one_block, (jnp.arange(nb), qb))
    return o.transpose(1, 0, 3, 2, 4).reshape(B, S, H, v.shape[-1])

def mla_branch(h, pos, w_in, q_norm_g, w_uq, kv_norm_g, w_ukv, w_out):
    B, S, _ = h.shape
    proj = h @ w_in
    cq, ckv, k_rope, g = jnp.split(
        proj, [MLA_Q_RANK, MLA_Q_RANK + MLA_KV_RANK, MLA_Q_RANK + MLA_KV_RANK + MLA_ROPE], axis=-1)
    q = (rmsnorm_2(cq, q_norm_g) @ w_uq).reshape(B, S, MLA_HEADS, MLA_NOPE + MLA_ROPE)
    q = jnp.concatenate([q[..., :MLA_NOPE], rope(q[..., MLA_NOPE:], pos)], axis=-1)
    kv = (rmsnorm_2(ckv, kv_norm_g) @ w_ukv).reshape(B, S, MLA_HEADS, MLA_NOPE + MLA_V)
    k_nope, v = kv[..., :MLA_NOPE], kv[..., MLA_NOPE:]
    k_rope = rope(k_rope[:, :, None, :], pos)
    k = jnp.concatenate([k_nope, jnp.broadcast_to(k_rope, (B, S, MLA_HEADS, MLA_ROPE))], axis=-1)
    o = causal_block_attention(q, k, v).reshape(B, S, MLA_WIDTH)
    return (jax.nn.silu(g) * o) @ w_out

def second_inputs(seed: int = 0) -> dict:
    key = jax.random.key(seed)
    ks = jax.random.split(key, 18)

    def w(k, shape, fan_in, gain=1.0):
        return jax.random.normal(k, shape, jnp.float32) * (gain * fan_in ** -0.5)

    def gain(k, shape):
        return 1.0 + 0.05 * jax.random.normal(k, shape, jnp.float32)

    x = jax.random.normal(ks[0], (BATCH, SEQ, D_MODEL), jnp.float32)
    c = jax.random.normal(ks[1], (BATCH, D_MODEL), jnp.float32)
    start = jax.random.randint(ks[2], (BATCH, 1), 0, 1024, dtype=jnp.int32)
    positions = start + jnp.arange(SEQ, dtype=jnp.int32)[None, :]
    return {
        "x": x,
        "c": c,
        "positions": positions,
        "ada_w": w(ks[3], (DEPTH_2, D_MODEL, 3 * D_MODEL), D_MODEL, 0.5),
        "ada_b": 0.01 * jax.random.normal(ks[4], (DEPTH_2, 3 * D_MODEL), jnp.float32),
        "norm_g": gain(ks[5], (DEPTH_2, D_MODEL)),
        "ret_w_in": w(ks[6], (N_RET_LAYERS, D_MODEL, RET_IN), D_MODEL),
        "ret_gn_g": gain(ks[7], (N_RET_LAYERS, RET_WIDTH)),
        "ret_w_out": w(ks[8], (N_RET_LAYERS, RET_WIDTH, D_MODEL), RET_WIDTH),
        "mla_w_in": w(ks[9], (N_MLA_LAYERS, D_MODEL, MLA_IN), D_MODEL),
        "mla_q_norm_g": gain(ks[10], (N_MLA_LAYERS, MLA_Q_RANK)),
        "mla_w_uq": w(ks[11], (N_MLA_LAYERS, MLA_Q_RANK, MLA_HEADS * (MLA_NOPE + MLA_ROPE)), MLA_Q_RANK),
        "mla_kv_norm_g": gain(ks[12], (N_MLA_LAYERS, MLA_KV_RANK)),
        "mla_w_ukv": w(ks[13], (N_MLA_LAYERS, MLA_KV_RANK, MLA_HEADS * (MLA_NOPE + MLA_V)), MLA_KV_RANK),
        "mla_w_out": w(ks[14], (N_MLA_LAYERS, MLA_WIDTH, D_MODEL), MLA_WIDTH),
        "final_norm_g": gain(ks[15], (D_MODEL,)),
    }

def second_block(x, c, positions, ada_w, ada_b, norm_g, ret_w_in, ret_gn_g, ret_w_out,
              mla_w_in, mla_q_norm_g, mla_w_uq, mla_kv_norm_g, mla_w_ukv, mla_w_out,
              final_norm_g):
    c_act = jax.nn.silu(c)
    for i in range(DEPTH_2):
        mod = (c_act @ ada_w[i] + ada_b[i])[:, None, :]
        shift, scale, gate = jnp.split(mod, 3, axis=-1)
        h = rmsnorm_2(x, norm_g[i]) * (1.0 + scale) + shift
        j = i // N_MIXERS
        if i % N_MIXERS == 0:
            y = retention_branch(h, positions, ret_w_in[j], ret_gn_g[j], ret_w_out[j])
        else:
            y = mla_branch(h, positions, mla_w_in[j], mla_q_norm_g[j], mla_w_uq[j],
                           mla_kv_norm_g[j], mla_w_ukv[j], mla_w_out[j])
        x = x + gate * y
    return rmsnorm_2(x, final_norm_g)


def setup_inputs(seed=0):
    out = dict(first_inputs(seed))
    for name, value in second_inputs(seed + 1).items():
        if name != "x":
            out[name + "_2"] = value
    return out


def reference(
    x, p, w_in, w_br_moba, w_br_diff, w_out, lambda_q1, lambda_k1, lambda_q2, lambda_k2,
    diff_subln_g, g_mix_pre, g_mix_post, w_up, w_down, g_mlp_pre, g_mlp_post, w_ple_proj,
    w_ple_gate, g_ple_pre, g_ple_post, c_2, positions_2, ada_w_2, ada_b_2, norm_g_2, ret_w_in_2,
    ret_gn_g_2, ret_w_out_2, mla_w_in_2, mla_q_norm_g_2, mla_w_uq_2, mla_kv_norm_g_2,
    mla_w_ukv_2, mla_w_out_2, final_norm_g_2,
):
    x = first_block(
        x, p, w_in, w_br_moba, w_br_diff, w_out, lambda_q1, lambda_k1, lambda_q2, lambda_k2,
        diff_subln_g, g_mix_pre, g_mix_post, w_up, w_down, g_mlp_pre, g_mlp_post, w_ple_proj,
        w_ple_gate, g_ple_pre, g_ple_post,
    )
    return second_block(
        x, c_2, positions_2, ada_w_2, ada_b_2, norm_g_2, ret_w_in_2, ret_gn_g_2, ret_w_out_2,
        mla_w_in_2, mla_q_norm_g_2, mla_w_uq_2, mla_kv_norm_g_2, mla_w_ukv_2, mla_w_out_2,
        final_norm_g_2,
    )


_drawn_inputs = setup_inputs


def setup_inputs(seed=0):
    import zlib

    import numpy as np

    out = dict(_drawn_inputs(seed))
    spreads = {}
    factors = {'diff_subln_g': 4.156,
     'g_mix_post': 4.267,
     'g_mlp_pre': 4.552,
     'g_mlp_post': 5.508,
     'g_ple_pre': 8.0,
     'g_ple_post': 5.71,
     'ada_b_2': 8.0,
     'norm_g_2': 5.385,
     'ret_gn_g_2': 8.0,
     'mla_q_norm_g_2': 8.0,
     'mla_w_uq_2': 4.691,
     'mla_kv_norm_g_2': 8.0}
    for name, (base, spread) in spreads.items():
        noise = np.random.default_rng([zlib.crc32(name.encode()), seed]).standard_normal(out[name].shape)
        drawn = base * np.exp(spread * noise) if base else spread * noise
        out[name] = jnp.asarray(drawn.astype(out[name].dtype))
    for name, factor in factors.items():
        out[name] = (out[name] * factor).astype(out[name].dtype)
    return out
```

```python
from contextlib import ExitStack, contextmanager

import concourse.bass as bass
from concourse import mybir

F32 = mybir.dt.float32
F32R = mybir.dt.float32r
I32 = mybir.dt.int32
ACT = mybir.ActivationFunctionType
ALU = mybir.AluOpType
AXIS_X = mybir.AxisListType.X

P = 128
TOKENS = 256
TILES = TOKENS // P
D = 2048
KT = D // P
EPS = 1e-6
HALF_TURN = 3.1415925
TURN = 6.283185307179586
TURN_PARTS = (6.28125, 2.0 ** -19 * 1014, TURN - 6.28125 - 2.0 ** -19 * 1014)
MANY = 4096.0
ROUND = 1.5 * 2.0 ** 23

HEAD = 128
ROT_HALF = 16
MOBA_W = 1024
DIFF_V = 256
FF = 8192
FF_BLOCK = 1024
LAMBDA_INIT = 0.2

RET_HEADS = 8
RET_DK = 256
RET_DV = 512
MLA_HEADS = 16
MLA_NOPE = 128
MLA_ROPE = 64
MLA_RANK = 512
MLA_QW = 2 * (MLA_NOPE + MLA_ROPE)

RAW_SLOTS = 4
CHUNK = 1024
RAW_CHUNKS = 2 * RAW_SLOTS
HI_CHUNKS = 4
AHEAD = 3
LANDED = 32
N = 512

ADA_W = 3 * D
ADA_CHUNK = 1024
ADA_CHUNKS = ADA_W // ADA_CHUNK
ADA_STEPS = KT * ADA_CHUNKS
ADA_SLOTS = 2
ADA_LANDED = 16
N_SETUP = 20

COL_MIX, COL_MLP, COL_PLE, COL_NORM, COL_C = 0, 16, 32, 48, 80
COL_Q, COL_KV, COL_SUB, VEC_ROWS = 96, 100, 104, 106
COL_GN = VEC_ROWS
COLS = VEC_ROWS + RET_HEADS * RET_DV // P


class Tally:

    def __init__(self, engine):
        self.engine, self.seen, self.i, self.per = engine, {}, None, {}

    def now(self, sem, ahead=0):
        n = self.seen.get(sem.name, 0) + ahead
        if self.i is None:
            return n
        per = self.per[sem.name]
        return self.i * per + n if per else n

    def nth(self, sem, k=1):
        self.seen[sem.name] = self.seen.get(sem.name, 0) + k
        return self.now(sem)

    def count(self, sem):
        return self.seen.get(sem.name, 0)

    @contextmanager
    def rounds(self, n, per):
        per = {sem.name: k for sem, k in per}
        before = dict(self.seen)
        with self.engine.Fori(0, n) as i:
            self.i, self.per = i, per
            yield i
            self.i = None
        for name in self.seen:
            once = self.seen[name] - before.get(name, 0)
            assert once in (0, per.get(name, 0)), (name, once, per.get(name))
            self.seen[name] = before.get(name, 0) + n * once


def build(nc, a, out):
    w_in, w_br_moba, w_br_diff, w_out = a["w_in"][0], a["w_br_moba"][0], a["w_br_diff"][0], a["w_out"][0]
    w_up, w_down, w_ple_proj, w_ple_gate = a["w_up"][0], a["w_down"][0], a["w_ple_proj"][0], a["w_ple_gate"][0]
    ret_in, ret_out = a["ret_w_in_2"][0], a["ret_w_out_2"][0]
    mla_in, mla_uq, mla_ukv, mla_out = a["mla_w_in_2"][0], a["mla_w_uq_2"][0], a["mla_w_ukv_2"][0], a["mla_w_out_2"][0]
    ada_w = a["ada_w_2"]

    with ExitStack() as ctx:
        def sb(name, shape, dt=F32):
            return ctx.enter_context(nc.sbuf_tensor(name, shape, dt))

        def sem(name):
            return ctx.enter_context(nc.semaphore(name))

        raw = sb("raw", [P, RAW_SLOTS, 2 * CHUNK])
        hi = sb("hi", [P, HI_CHUNKS, CHUNK], F32R)
        lo = sb("lo", [P, HI_CHUNKS, CHUNK], F32R)
        xT_hi, xT_lo = sb("xT_hi", [P, KT, TOKENS], F32R), sb("xT_lo", [P, KT, TOKENS], F32R)
        yT_hi = [sb(f"yT{i}_hi", [P, 8, TOKENS], F32R) for i in range(2)]
        yT_lo = [sb(f"yT{i}_lo", [P, 8, TOKENS], F32R) for i in range(2)]
        pT_hi, pT_lo = sb("pT_hi", [P, 2, TOKENS], F32R), sb("pT_lo", [P, 2, TOKENS], F32R)
        h = sb("h", [P, TILES, D])
        acc = sb("acc", [P, TILES, D])
        row = sb("row", [P, D])
        WORK = 10240
        work = sb("work", [P, WORK])
        ident = sb("ident", [P, P])
        ones = sb("ones", [P, P])
        mask = sb("mask", [P, 3 * P])
        cols = sb("cols", [P, COLS])
        mods = sb("mods", [P, 3, KT])
        c_act = sb("c_act", [P, KT])
        rope1 = sb("rope1", [P, 2, 2 * 8 * ROT_HALF])
        trig = sb("trig", [P, 2, 640])
        stats = sb("stats", [P, 96])
        neg_half, eps = sb("neg_half", [P, 4]), sb("eps", [P, 4])

        def carve(at, *shape):
            n = 1
            for s in shape:
                n *= s
            assert at + n <= WORK, (at, shape)
            piece = work[:, at:at + n]
            if len(shape) == 2:
                return piece.rearrange("p (a b) -> p a b", b=shape[1])
            if len(shape) == 3:
                return piece.rearrange("p (a b c) -> p a b c", b=shape[1], c=shape[2])
            return piece

        panels = ctx.enter_context(nc.psum_tensor("panels", [P, 2 * TILES, N], F32))
        panel = [panels[:, 0:TILES, :], panels[:, TILES:2 * TILES, :]]
        spare = ctx.enter_context(nc.psum_tensor("spare", [P, 4, N], F32))
        turn = [spare[:, 0, :], spare[:, 1, :]]
        score = [spare[:, 2, :], spare[:, 3, :]]

        setup_landed, x_landed = sem("setup_landed"), sem("x_landed")
        raw_landed = [sem(f"raw_landed{i}") for i in range(RAW_SLOTS)]
        multiplied, hi_ready, lo_ready = sem("multiplied"), sem("hi_ready"), sem("lo_ready")
        panel_taken = [sem("panel_taken0"), sem("panel_taken1")]
        turned, turn_taken = [sem("turned0"), sem("turned1")], [sem("turn_taken0"), sem("turn_taken1")]
        scored, score_taken = [sem("scored0"), sem("scored1")], [sem("score_taken0"), sem("score_taken1")]
        turn_hi = sem("turn_hi")
        sums_ready, rstd_ready = sem("sums_ready"), sem("rstd_ready")
        h_ready, xs_ready = sem("h_ready"), sem("xs_ready")
        sp_waited, pe_waited, dve_waited, pool_step, dve_step, act_step = sem("sp_waited"), sem("pe_waited"), sem("dve_waited"), sem("pool_step"), sem("dve_step"), sem("act_step")
        vec_ready, lam_sums, lam_exps = sem("vec_ready"), sem("lam_sums"), sem("lam_exps")
        angles_ready, trig_ready, c_ready = sem("angles_ready"), sem("trig_ready"), sem("c_ready")
        roped = sem("roped")
        max_ready, exp_ready, probs_ready = sem("max_ready"), sem("exp_ready"), sem("probs_ready")
        mixed_ready, squares_done = sem("mixed_ready"), sem("squares_done")
        ada_landed = [sem(f"ada_landed{i}") for i in range(ADA_SLOTS)]
        ada_set, ada_row, ada_taken, mods_ready = sem("ada_set"), sem("ada_row"), sem("ada_taken"), sem("mods_ready")
        row_landed, diag_ready = sem("row_landed"), sem("diag_ready")
        ple_ready, dm_landed, yg_ready = sem("ple_ready"), sem("dm_landed"), sem("yg_ready")
        out_ready, out_landed = sem("out_ready"), sem("out_landed")

        vec, vec2 = acc[:, 0, 0:P], acc[:, 0, P:2 * P]
        lambdas = acc[:, 0, 896:896 + 4 * HEAD].rearrange("p (a b d) -> p a b d", a=2, d=HEAD)
        lam_prods = acc[:, 0, 1536:1536 + 2 * HEAD].rearrange("p (a d) -> p a d", d=HEAD)
        p_in = acc[:, 1, 0:512].rearrange("p (m d) -> p m d", m=TILES)
        freq, turns_all, turns_hi = carve(8192, 640), carve(5120, 640), carve(5760, 640)
        qk = carve(0, TILES, 8 * HEAD)
        v_sb = carve(2048, TILES, N)
        qkT = carve(3072, 4, 4 * P)
        sm = carve(5120, 4, 3 * P)
        pr = carve(6656, 4, 3 * P)
        pT = carve(8192, 4, 3 * P)
        ob = acc[:, 0, 0:1024].rearrange("p (m h d) -> p m h d", m=TILES, d=DIFF_V)
        ob_squares = acc[:, 0, 1024:2048].rearrange("p (h m d) -> p h m d", m=TILES, d=DIFF_V)
        rope_tmp = acc[:, 1, 0:1024].rearrange("p (n h r) -> p n h r", n=4, r=ROT_HALF)
        sig = [carve(0, TILES, N), carve(1024, TILES, N)]
        gated = carve(2048, TILES, N)
        ada_acc = carve(0, ADA_W)
        ada_ring = carve(ADA_W, ADA_SLOTS, ADA_CHUNK)
        relu = carve(8192, TILES, N)
        e_sb = carve(6144, TILES, D)
        diag = carve(6144, D)
        shift_tmp = carve(8192, 2, N)
        ret_qk = carve(8192, TILES, N)
        ret_v = ret_qk
        ret_yn = ret_qk
        ret_sT = carve(9216, 3 * P)
        ret_dm = carve(9600, 3 * P)
        ret_sg = row[:, 0:1024].rearrange("p (m n) -> p m n", n=N)
        ret_qkT = row[:, 1024:2048].rearrange("p (c d t) -> p c d t", c=2, t=TOKENS)
        sgm = acc
        q_sb = [carve(i * 768, TILES, MLA_QW) for i in range(2)]
        kv_sb = [carve(1536 + i * 1024, TILES, N) for i in range(2)]
        lat = carve(3584, TILES, N)
        nT = carve(4608, 2, 4 * P)
        rT = work[0:MLA_ROPE, 5632:5632 + 2 * TOKENS].rearrange("p (h t) -> p h t", t=TOKENS)
        krT = work[0:MLA_ROPE, 6144:6144 + TOKENS]
        kr = carve(6400, TILES, MLA_ROPE)
        m_sm = carve(6528, 2, 3 * P)
        m_pr = carve(7296, 2, 3 * P)
        m_pT = carve(8064, 2, 3 * P)
        og = carve(8832, TILES, 2 * P)
        mla_tmp = carve(9344, 2, 128)
        lat_squares = [carve(9728, N), carve(4608, N)]
        final_row = carve(0, D)

        st_sum = stats[:, 0:2]
        st_rstd = stats[:, 2:4]
        st_parts = stats[:, 8:16].rearrange("p (m n) -> p m n", n=4)
        st_max = stats[:, 16:24].rearrange("p (h q) -> p h q", q=2)
        st_neg = stats[:, 24:32].rearrange("p (h q) -> p h q", q=2)
        st_den = stats[:, 32:40].rearrange("p (h q) -> p h q", q=2)
        st_inv = stats[:, 40:48].rearrange("p (h q) -> p h q", q=2)
        st_lam = stats[:, 48:50]
        neg_lam = stats[:, 50:51]
        st_pos = stats[:, 52:54]
        st_ipos = stats[:, 54:56].bitcast(I32)
        st_bn = stats[:, 60:72].rearrange("p (m s) -> p m s", s=6)
        st_mv = stats[:, 72:76].rearrange("p (m s) -> p m s", s=2)
        st_dsum = stats[:, 76:80].rearrange("p (h m) -> p h m", m=TILES)
        st_drstd = stats[:, 80:84].rearrange("p (h m) -> p h m", m=TILES)

        def per_round(chunks, panels=(0, 0), turns=(0, 0), scores=(0, 0), ada=0, more=()):
            assert chunks % RAW_CHUNKS == 0
            base = [(multiplied, chunks), (hi_ready, chunks), (lo_ready, chunks)]
            base += [(s, chunks // RAW_CHUNKS * LANDED) for s in raw_landed]
            for b in range(2):
                base += [(panel_taken[b], panels[b]), (turned[b], turns[b]), (turn_taken[b], turns[b]),
                         (scored[b], scores[b]), (score_taken[b], scores[b])]
            base += [(s, ada // ADA_SLOTS * ADA_LANDED) for s in ada_landed] + [(ada_taken, ada)]
            return base + list(more)

        ATTENTION = per_round(48, (3, 3), (8, 8), (6, 6), 0, (
            (roped, 2), (max_ready, 4), (exp_ready, 4), (probs_ready, 3), (turn_hi, 4), (sums_ready, 1),
            (rstd_ready, 1), (dve_step, 14), (pool_step, 1)))
        MIX = per_round(24, (2, 2), more=((mixed_ready, 1),))
        WIDE = per_round(16, (1, 1), more=((squares_done, 2), (ple_ready, 2), (mixed_ready, 2)))
        FEED = per_round(64, (6, 6), (4, 4), ada=24, more=((act_step, 4), (turn_hi, 8)))
        RETAIN = per_round(32, (4, 3), (2, 2), (2, 1), 12, (
            (roped, 1), (sums_ready, 1), (rstd_ready, 1), (yg_ready, 1), (turn_hi, 2), (dm_landed, 16),
            (dve_step, 1), (pool_step, 1)))
        LATENT = per_round(8, (2, 2), (6, 6), (4, 2), 0, (
            (roped, 2), (max_ready, 2), (exp_ready, 2), (probs_ready, 2), (turn_hi, 2), (dve_step, 4)))

        def ada_at(slots):
            return [n * slots // (2 * ADA_CHUNKS) for n in range(2 * ADA_CHUNKS)]

        block = ctx.enter_context(nc.Block())

        @block.sync
        def _(sp):
            t = Tally(sp)
            n_setup = 0

            def setup(dst, src):
                nonlocal n_setup
                sp.dma_start(dst, src).then_inc(setup_landed, 16)
                n_setup += 1

            def unit(*parts):
                slot = t.count(multiplied) // 2 % RAW_SLOTS
                sp.wait_ge(multiplied, t.nth(multiplied, 2))
                if t.i is not None:
                    sp.sem_inc(sp_waited, 1)
                for dst, src in parts:
                    sp.dma_start(dst(raw[:, slot, :]), src).then_inc(raw_landed[slot], LANDED // len(parts))

            def plain(w, row0, col0, kts=4, ncols=N):
                src = w[row0, col0] if kts else None
                half = kts * ncols // 2
                if half == CHUNK:
                    return unit((lambda r: r.rearrange("p (k n) -> p k n", n=ncols),
                                 src.rearrange("(k p) n -> p k n", p=P)))
                s = src.rearrange("(c k p) n -> c p k n", c=2, p=P)
                return unit(*[((lambda r, c=c: r[:, c * CHUNK:c * CHUNK + half].rearrange("p (k n) -> p k n", n=ncols)),
                               s[c]) for c in range(2)])

            def rows(k0, kts=4):
                return slice(k0 * P, (k0 + kts) * P)

            def wide(w, col0, k_tiles=KT, row0=0):
                for k in range(0, k_tiles, 4):
                    plain(w, rows(row0 + k), bass.ds(col0, N))

            sp.dma_start(h[:], a["x"][0].rearrange("(m p) d -> p m d", p=P)).then_inc(x_landed, 16)
            for at, name, n in ((COL_MIX, "g_mix_pre", KT), (COL_MLP, "g_mlp_pre", KT), (COL_PLE, "g_ple_pre", KT),
                                (COL_NORM, "norm_g_2", 2 * KT), (COL_C, "c_2", KT), (COL_Q, "mla_q_norm_g_2", 4),
                                (COL_KV, "mla_kv_norm_g_2", 4), (COL_SUB, "diff_subln_g", 2)):
                setup(vec[at:at + n, :], a[name].rearrange("l (k p) -> (l k) p", p=P))
            setup(vec2[0:COLS - COL_GN, :], a["ret_gn_g_2"].rearrange("l (k p) -> (l k) p", p=P))
            setup(ident[:], a["k_ident"])
            setup(mask[:], a["k_mask"])
            setup(rope1[:], a["k_rope1"])
            setup(freq, a["k_freq"].partition_broadcast(P))
            for m in range(TILES):
                setup(st_ipos[:, m:m + 1], a["positions_2"][0, m * P:(m + 1) * P].rearrange("(p o) -> p o", o=1))
            for n, name in enumerate(("lambda_q1", "lambda_k1", "lambda_q2", "lambda_k2")):
                setup(lambdas[:, n // 2, n % 2, :], a[name][0].partition_broadcast(P))
            setup(p_in, a["p"][0, 0].rearrange("(m p) d -> p m d", p=P))
            assert n_setup == N_SETUP, n_setup

            with t.rounds(2, ATTENTION) as g:
                for at in (3 * MOBA_W, 4 * MOBA_W, 0, MOBA_W, 5 * MOBA_W, 2 * MOBA_W):
                    wide(w_in, g * N + at)
            with t.rounds(4, MIX) as n:
                wide(w_in, n * N + 6 * MOBA_W)
                wide(w_br_moba, n * N, 8)
                wide(w_in, n * N + 6 * MOBA_W + D)
                wide(w_br_diff, n * N, 8)
            with t.rounds(2, WIDE) as n:
                for j in range(2):
                    wide(w_out, n * 2 * N + j * N)

            def up(col0):
                for j in range(2):
                    wide(w_up, col0 + j * N)

            def down(row0):
                for n in range(4):
                    for k in range(2):
                        plain(w_down, bass.ds(row0 + k * 4 * P, 4 * P), slice(n * N, (n + 1) * N))

            up(0)
            with t.rounds(3, FEED) as i:
                for j in range(2):
                    up(i * 2 * FF_BLOCK + (j + 1) * FF_BLOCK)
                    down(i * 2 * FF_BLOCK + j * FF_BLOCK)
            up(7 * FF_BLOCK)
            down(6 * FF_BLOCK)
            down(7 * FF_BLOCK)
            for n in range(4):
                plain(w_ple_proj, slice(0, 2 * P), slice(n * N, (n + 1) * N), 2)
            with t.rounds(2, WIDE) as n:
                for j in range(2):
                    wide(w_ple_gate, n * 2 * N + j * N)

            def ret_qk_unit(head):
                for k in range(0, KT, 4):
                    unit(*[((lambda r, c=c: r.rearrange("p (k c n) -> p k c n", c=2, n=RET_DK)[:, :, c, :]),
                            ret_in[rows(k), bass.ds(head * RET_DK + c * D, RET_DK)].rearrange("(k p) n -> p k n", p=P))
                           for c in range(2)])

            def ret_out_units(head):
                for n in range(4):
                    plain(ret_out, bass.ds(head * RET_DV, RET_DV), slice(n * N, (n + 1) * N))

            def ret_vg(head):
                wide(ret_in, head * RET_DV + 2 * D)
                wide(ret_in, head * RET_DV + 4 * D)

            ret_qk_unit(0)
            ret_vg(0)
            with t.rounds(RET_HEADS - 1, RETAIN) as i:
                ret_qk_unit(i + 1)
                ret_out_units(i)
                ret_vg(i + 1)
            ret_out_units(RET_HEADS - 1)

            wide(mla_in, MLA_RANK)
            plain(mla_in, slice(0, D), slice(2 * MLA_RANK, 2 * MLA_RANK + MLA_ROPE), KT, MLA_ROPE)
            wide(mla_in, 0)
            with t.rounds(2, WIDE) as n:
                for j in range(2):
                    wide(mla_in, n * 2 * N + (2 * MLA_RANK + MLA_ROPE + j * N))

            def pair(p):
                plain(mla_uq, rows(0), bass.ds(p * MLA_QW, MLA_QW), 4, MLA_QW)
                plain(mla_ukv, rows(0), bass.ds(p * N, N))

            pair(0)
            pair(1)
            with t.rounds(3, LATENT) as i:
                pair(i * 2 + 2)
                pair(i * 2 + 3)
            with t.rounds(2, WIDE) as n:
                for j in range(2):
                    wide(mla_out, n * 2 * N + j * N)
            for m in range(TILES):
                sp.wait_ge(out_ready, m + 1)
                sp.dma_start(out[0, m * P:(m + 1) * P, :], acc[:, m, :]).then_inc(out_landed, 16)
            sp.wait_ge(out_landed, 16 * TILES)

        @block.tensor
        def _(pe):
            t = Tally(pe)
            XT, PT_X = (xT_hi, xT_lo), (pT_hi, pT_lo)
            YT = [(yT_hi[i], yT_lo[i]) for i in range(2)]

            pe.sem_inc(multiplied, RAW_CHUNKS)
            for b in range(2):
                pe.sem_inc(panel_taken[b], 1)
                pe.sem_inc(turn_taken[b], 1)
                pe.sem_inc(score_taken[b], 1)

            def open_panel(b):
                pe.wait_ge(panel_taken[b], t.nth(panel_taken[b]))

            def panel_closed(b):
                pe.wait_ge(panel_taken[b], t.now(panel_taken[b], 1))

            def turn_closed(b):
                pe.wait_ge(turn_taken[b], t.now(turn_taken[b], 1))

            def score_closed(b):
                pe.wait_ge(score_taken[b], t.now(score_taken[b], 1))

            def chunk(b, x, kt0, first, last, ncols=N, kts=2):
                x_hi, x_lo = x
                slot = t.count(lo_ready) % HI_CHUNKS
                pe.wait_ge(lo_ready, t.nth(lo_ready))
                for j in range(kts):
                    w_hi, w_lo = (w[:, slot, j * ncols:(j + 1) * ncols] for w in (hi, lo))
                    for m in range(TILES):
                        o, ms = panel[b][:, m, 0:ncols], slice(m * P, (m + 1) * P)
                        pe.matmul(o, x_hi[:, kt0 + j, ms], w_hi, start=first and j == 0, stop=False)
                        pe.matmul(o, x_hi[:, kt0 + j, ms], w_lo, start=False, stop=False)
                        done = pe.matmul(o, x_lo[:, kt0 + j, ms], w_hi, start=False, stop=last and j == kts - 1)
                done.then_inc(multiplied, 1)
                t.nth(multiplied)

            def wide_chunk(s, b, x, chunks=8, k0=0):
                if s == 0:
                    open_panel(b)
                chunk(b, x, k0 + 2 * s, s == 0, s == chunks - 1)

            def turn_batch(b, *pieces):
                pe.wait_ge(turn_taken[b], t.nth(turn_taken[b]))
                if pieces[0][0].shape[1] < P and t.i is not None:
                    pe.sem_inc(pe_waited, 1)
                for src, at in pieces:
                    rows, n = src.shape
                    done = pe.transpose(turn[b][0:n, at:at + rows], src, ident[0:rows, 0:rows])
                done.then_inc(turned[b], 1)
                t.nth(turned[b])

            def turn_tokens(b, src):
                turn_batch(b, *[(src(m)[:, k * P:(k + 1) * P], k * TOKENS + m * P) for k in range(2) for m in range(TILES)])

            def turn_xs(c):
                turn_tokens(c % 2, lambda m: acc[:, m, c * 2 * P:(c + 1) * 2 * P])

            def turn_probs(b, src):
                turn_batch(b, *[(src[:, n * P:(n + 1) * P], n * P) for n in range(3)])

            def open_score(b):
                pe.wait_ge(score_taken[b], t.nth(score_taken[b]))

            def scores_of(b, parts):
                open_score(b)
                for at, n, q in ((0, P, slice(0, P)), (P, 2 * P, slice(P, 2 * P))):
                    for i, (qT, kT) in enumerate(parts):
                        done = pe.matmul(score[b][:, at:at + n], qT[:, q], kT[:, 0:n], start=i == 0,
                                         stop=i == len(parts) - 1)
                done.then_inc(scored[b], 1)
                t.nth(scored[b])

            def weighted(out0, out1, pT3, v0, v1):
                pe.matmul(out0, pT3[:, 0:P], v0, start=True, stop=True)
                pe.matmul(out1, pT3[:, P:2 * P], v0, start=True, stop=False)
                return pe.matmul(out1, pT3[:, 2 * P:3 * P], v1, start=False, stop=True)

            def turned_panel(s, b):
                if s == 0:
                    pe.wait_ge(xs_ready, t.nth(xs_ready, TILES))
                    turn_xs(0)
                if s < 7:
                    turn_xs(s + 1)
                turn_closed(s % 2)
                wide_chunk(s, b, XT)

            pe.wait_ge(setup_landed, 16 * N_SETUP)
            pe.wait_ge(score_taken[0], t.nth(score_taken[0]))
            pe.transpose(score[0][:, 0:VEC_ROWS], vec[0:VEC_ROWS, :], ident[0:VEC_ROWS, 0:VEC_ROWS])
            pe.transpose(score[0][:, COL_GN:COLS], vec2[0:COLS - COL_GN, :],
                         ident[0:COLS - COL_GN, 0:COLS - COL_GN]).then_inc(scored[0], 1)
            t.nth(scored[0])
            turn_tokens(1, lambda m: p_in[:, m, :])
            pe.wait_ge(xs_ready, t.nth(xs_ready, TILES))
            for c in range(8):
                turn_xs(c)
            turn_closed(0)
            turn_closed(1)

            def turn_heads(j):
                turn_batch(j % 2, *[(qk[:, m, (4 * c + j) * HEAD:(4 * c + j + 1) * HEAD], (2 * c + m) * P)
                                    for c in range(2) for m in range(TILES)])

            def head_scores(j):
                scores_of(j % 2, [(qkT[:, j, 0:2 * P], qkT[:, j, 2 * P:4 * P])])

            with t.rounds(2, ATTENTION) as g:
                for s in range(48):
                    if s in (18, 34):
                        pe.wait_ge(roped, t.nth(roped))
                        turn_heads(0)
                        turn_heads(1)
                    if s in (19, 35):
                        turn_heads(2)
                        turn_heads(3)
                    if s in (21, 37):
                        head_scores(0)
                        head_scores(1)
                    if s in (22, 38):
                        turn_closed(0)
                        turn_closed(1)
                        head_scores(2)
                        head_scores(3)
                    if s == 27:
                        pe.wait_ge(probs_ready, t.nth(probs_ready))
                        for hh in range(2):
                            turn_probs(hh, pr[:, 2 * hh, :])
                    if s == 42:
                        panel_closed(0)
                        turn_closed(0)
                        turn_closed(1)
                        for hh in range(2):
                            open_score(hh)
                            vs = [v_sb[:, m, hh * DIFF_V:(hh + 1) * DIFF_V] for m in range(TILES)]
                            weighted(score[hh][:, 0:DIFF_V], score[hh][:, DIFF_V:2 * DIFF_V], pT[:, hh, :],
                                     *vs).then_inc(scored[hh], 1)
                            t.nth(scored[hh])
                    if s in (43, 44):
                        pe.wait_ge(probs_ready, t.nth(probs_ready))
                        for j in range(2):
                            turn_probs(j, pr[:, 2 * (s - 43) + j, :])
                    if s == 47:
                        score_closed(0)
                        score_closed(1)
                        for hh in range(2):
                            turn_tokens(hh, lambda m: ob[:, m, hh, :])
                    wide_chunk(s % 8, s // 8 % 2, XT)
                panel_closed(1)
                for b in range(2):
                    open_score(b)
                    for j in (2 * b, 2 * b + 1):
                        at = (j % 2) * TOKENS
                        v0, v1 = (v_sb[:, m, j * HEAD:(j + 1) * HEAD] for m in range(TILES))
                        pe.matmul(score[b][:, at:at + P], v0, pT[:, j, 0:P], start=True, stop=True)
                        pe.matmul(score[b][:, at + P:at + 2 * P], v0, pT[:, j, P:2 * P], start=True, stop=False)
                        done = pe.matmul(score[b][:, at + P:at + 2 * P], v1, pT[:, j, 2 * P:3 * P], start=False, stop=True)
                    done.then_inc(scored[b], 1)
                    t.nth(scored[b])

            with t.rounds(4, MIX) as n:
                for s in range(24):
                    if s < 8:
                        wide_chunk(s, 0, XT)
                    elif s < 12:
                        if s == 8:
                            score_closed(0)
                            score_closed(1)
                        wide_chunk(s - 8, 1, YT[0], 4)
                    elif s < 20:
                        wide_chunk(s - 12, 0, XT)
                    else:
                        if s == 20:
                            turn_closed(0)
                            turn_closed(1)
                        wide_chunk(s - 20, 1, YT[1], 4)
            pe.wait_ge(mixed_ready, t.nth(mixed_ready, D // N))
            for c in range(8):
                turn_xs(c)
            turn_closed(0)
            turn_closed(1)

            def four_panels(b0, x):
                with t.rounds(2, WIDE) as n:
                    for s in range(16):
                        wide_chunk(s % 8, (b0 + s // 8) % 2, x)

            four_panels(0, XT)

            def up_turns(s, k):
                if s in (10, 18):
                    b = s // 18
                    panel_closed(b)
                    for j in range(2):
                        turn_tokens(j, lambda m: relu[:, m, j * 2 * P:(j + 1) * 2 * P])

            def up_chunk(s):
                wide_chunk(s % 8, s // 8, XT)

            def down_chunk(s, k):
                wide_chunk(s % 4, s // 4 % 2, YT[k % 2], 4)

            for s in range(16):
                up_turns(s, 0)
                if s < 8:
                    turned_panel(s, 0)
                else:
                    up_chunk(s)
            up_turns(18, 0)
            with t.rounds(3, FEED) as i:
                for half in range(2):
                    for s in range(32):
                        up_turns(s, half + 1)
                        if s < 16:
                            up_chunk(s)
                        else:
                            down_chunk(s - 16, half)
            for s in range(48):
                up_turns(s, 7)
                if s < 16:
                    up_chunk(s)
                else:
                    down_chunk(s - 16, s // 32)

            for s in range(8):
                if s % 2 == 0:
                    open_panel(s // 2 % 2)
                chunk(s // 2 % 2, PT_X, s % 2, s % 2 == 0, s % 2 == 1, N, 1)
            pe.wait_ge(xs_ready, t.nth(xs_ready, TILES))
            for c in range(8):
                turn_xs(c)
            turn_closed(0)
            turn_closed(1)
            four_panels(0, XT)

            def mod_sums(layer):
                open_score(0)
                pe.wait_ge(ada_taken, ADA_SLOTS + ADA_STEPS * (layer + 1))
                for n in range(ADA_W // P):
                    done = pe.matmul(score[0][:, n:n + 1], ada_acc[:, n * P:(n + 1) * P], ones[:, 0:1], start=True, stop=True)
                done.then_inc(scored[0], 1)
                t.nth(scored[0])

            def gate_rows():
                pe.wait_ge(diag_ready, t.nth(diag_ready))
                for n in range(4):
                    open_score(n % 2)
                    pe.matmul(score[n % 2], ones[:], diag[:, n * N:(n + 1) * N], start=True, stop=True).then_inc(scored[n % 2], 1)
                    t.nth(scored[n % 2])

            mod_sums(0)

            def ret_y_turns():
                pe.wait_ge(yg_ready, t.nth(yg_ready))
                for j in range(2):
                    turn_tokens(j, lambda m: ret_sg[:, m, j * 2 * P:(j + 1) * 2 * P])

            def ret_out_chunk(s):
                if s == 0:
                    turn_closed(0)
                    turn_closed(1)
                wide_chunk(s % 2, (1 + s // 2) % 2, YT[0], 2)

            def ret_qk_turns():
                pe.wait_ge(roped, t.nth(roped))
                for c in range(2):
                    turn_tokens(c, lambda m: ret_qk[:, m, c * RET_DK:(c + 1) * RET_DK])

            def ret_scores():
                turn_closed(0)
                turn_closed(1)
                open_score(0)
                for at, n, k0, q0 in ((0, 2 * P, 0, 0), (2 * P, P, P, P)):
                    for d in range(2):
                        done = pe.matmul(score[0][:, at:at + n], ret_qkT[:, 1, d, k0:k0 + P], ret_qkT[:, 0, d, q0:q0 + n],
                                         start=d == 0, stop=d == 1)
                done.then_inc(scored[0], 1)
                t.nth(scored[0])

            def ret_y():
                score_closed(0)
                panel_closed(1)
                open_score(0)
                pe.matmul(score[0], ret_sT[:, 0:P], ret_v[:, 0, :], start=True, stop=True).then_inc(scored[0], 1)
                t.nth(scored[0])
                open_score(1)
                pe.matmul(score[1], ret_sT[:, P:2 * P], ret_v[:, 0, :], start=True, stop=False)
                pe.matmul(score[1], ret_sT[:, 2 * P:3 * P], ret_v[:, 1, :], start=False, stop=True).then_inc(scored[1], 1)
                t.nth(scored[1])

            for s in range(24):
                if s == 11:
                    ret_qk_turns()
                if s == 14:
                    ret_scores()
                if s == 18:
                    ret_y()
                if s < 8:
                    turned_panel(s, 0)
                else:
                    wide_chunk(s % 8, s // 8 % 2, XT)
            with t.rounds(RET_HEADS - 1, RETAIN) as i:
                for s in range(32):
                    if s == 2:
                        ret_y_turns()
                    if s == 11:
                        ret_qk_turns()
                    if s == 14:
                        ret_scores()
                    if s == 26:
                        ret_y()
                    if s < 8:
                        wide_chunk(s, 0, XT)
                    elif s < 16:
                        ret_out_chunk(s - 8)
                    elif s < 24:
                        wide_chunk(s - 16, 1, XT)
                    else:
                        wide_chunk(s - 24, 0, XT)
            ret_y_turns()
            gate_rows()
            for s in range(8):
                ret_out_chunk(s)
            mod_sums(1)

            for s in range(18):
                if s == 9:
                    gate_rows()
                if s == 13:
                    for j in range(2):
                        turn_tokens(j, lambda m: lat[:, m, j * 2 * P:(j + 1) * 2 * P])
                if s == 15:
                    pe.wait_ge(roped, t.nth(roped))
                    turn_batch(0, *[(kr[:, m, :], m * P) for m in range(TILES)])
                if s < 8:
                    turned_panel(s, 0)
                elif s < 10:
                    if s == 8:
                        open_panel(1)
                    chunk(1, XT, 8 * (s - 8), s == 8, s == 9, MLA_ROPE, 8)
                else:
                    wide_chunk(s - 10, 0, XT)
            four_panels(1, XT)
            for j in range(2):
                turn_tokens(j, lambda m: lat[:, m, j * 2 * P:(j + 1) * 2 * P])
            turn_closed(0)
            turn_closed(1)

            def pair_chunk(s):
                if s < 2:
                    if s == 0:
                        open_panel(0)
                    chunk(0, YT[0], 2 * s, s == 0, s == 1, MLA_QW)
                else:
                    wide_chunk(s - 2, 1, (yT_hi[0][:, 4:8, :], yT_lo[0][:, 4:8, :]), 2)

            def pair_step(s, q, r):
                if s == 1 and q is not None:
                    pe.wait_ge(roped, t.nth(roped))
                    panel_closed(1)
                    for hh in range(2):
                        k0 = hh * 2 * MLA_NOPE
                        q0 = hh * (MLA_NOPE + MLA_ROPE)
                        turn_batch(hh, *[(q_sb[q][:, m, q0:q0 + MLA_NOPE], m * P) for m in range(TILES)],
                                   *[(kv_sb[q][:, m, k0:k0 + MLA_NOPE], (2 + m) * P) for m in range(TILES)])
                if s == 2 and r is not None:
                    pe.wait_ge(probs_ready, t.nth(probs_ready))
                    for hh in range(2):
                        turn_probs(hh, m_pr[:, hh, :])
                if s == 3:
                    if r is not None:
                        turn_closed(0)
                        turn_closed(1)
                    if q is not None:
                        q1 = MLA_NOPE
                        turn_batch(0, *[(q_sb[q][:, m, hh * (MLA_NOPE + MLA_ROPE) + q1:(hh + 1) * (MLA_NOPE + MLA_ROPE)],
                                         hh * TOKENS + m * P) for hh in range(2) for m in range(TILES)])
                    if r is not None:
                        open_score(0)
                        for hh in range(2):
                            vs = [kv_sb[r][:, m, (2 * hh + 1) * P:(2 * hh + 2) * P] for m in range(TILES)]
                            done = weighted(score[0][:, hh * P:(hh + 1) * P], score[0][:, (2 + hh) * P:(3 + hh) * P],
                                            m_pT[:, hh, :], *vs)
                        done.then_inc(scored[0], 1)
                        t.nth(scored[0])
                if s == 4:
                    if q is not None:
                        turn_closed(0)
                        turn_closed(1)
                        scores_of(1, [(nT[:, 0, 0:2 * P], nT[:, 0, 2 * P:4 * P]), (rT[:, 0, :], krT)])
                    if r is not None:
                        score_closed(0)
                        turn_batch(1, *[(og[:, m, hh * P:(hh + 1) * P], hh * TOKENS + m * P)
                                        for hh in range(2) for m in range(TILES)])
                    if q is not None:
                        scores_of(0, [(nT[:, 1, 0:2 * P], nT[:, 1, 2 * P:4 * P]), (rT[:, 1, :], krT)])

            for p in range(2):
                for s in range(5):
                    pair_step(s, 0 if p else None, None)
                    if s < 4:
                        pair_chunk(s)
            with t.rounds(3, LATENT) as i:
                for p in range(2):
                    for s in range(5):
                        pair_step(s, 1 - p, p)
                        if s < 4:
                            pair_chunk(s)
            for s in range(5):
                pair_step(s, 1, 0)
            for s in range(5):
                pair_step(s, None, 1)
            turn_closed(1)
            four_panels(0, XT)

        @block.scalar
        def _(act):
            t = Tally(act)
            copy = ACT.Copy

            def split_hi():
                k = t.count(hi_ready)
                slot = k // 2 % RAW_SLOTS
                if k % 2 == 0:
                    act.wait_ge(raw_landed[slot], t.nth(raw_landed[slot], LANDED))
                act.wait_ge(multiplied, t.nth(multiplied) + RAW_CHUNKS - HI_CHUNKS)
                act.activation(hi[:, k % HI_CHUNKS, :], raw[:, slot, k % 2 * CHUNK:(k % 2 + 1) * CHUNK],
                               copy).then_inc(hi_ready, 1)
                t.nth(hi_ready)

            def chunks_done():
                act.wait_ge(multiplied, t.now(multiplied, RAW_CHUNKS - AHEAD))

            def wait_turned(b):
                act.wait_ge(turned[b], t.nth(turned[b]))

            def squares(junk, src, sums, shared=False):
                for m in range(TILES):
                    if shared and m:
                        done.then_inc(act_step, 1)
                        act.wait_ge(act_step, t.nth(act_step))
                    done = act.activation(junk(m), src(m), ACT.Square, accum_out=sums[:, m:m + 1])
                done.then_inc(sums_ready, 1)
                t.nth(sums_ready)

            def h_squares(n):
                act.wait_ge(h_ready, t.nth(h_ready, n))
                squares(lambda m: acc[:, m, :], lambda m: h[:, m, :], st_sum)

            def hi_plain(c, dst, kt):
                wait_turned(c % 2)
                act.activation(dst[:, kt, :], turn[c % 2].rearrange("p (k t) -> p k t", t=TOKENS), copy).then_inc(turn_hi, 1)

            def hi_scaled(b, dst, kt, gains, shifts=None):
                wait_turned(b)
                for k in range(2):
                    src = turn[b][:, k * TOKENS:(k + 1) * TOKENS]
                    if shifts:
                        done = act.activation(dst[:, kt + k, :], src, ACT.Identity, scale=gains(k), bias=shifts(k))
                    else:
                        done = act.activation(dst(k) if callable(dst) else dst[:, kt + k, :], src, copy, scale=gains(k))
                done.then_inc(turn_hi, 1)

            def hi_norm(c, col):
                hi_scaled(c % 2, xT_hi, 2 * c, lambda k: cols[:, col + 2 * c + k:col + 2 * c + k + 1])

            def hi_mod(c):
                hi_scaled(c % 2, xT_hi, 2 * c, lambda k: mods[:, 1, 2 * c + k:2 * c + k + 1],
                          lambda k: mods[:, 0, 2 * c + k:2 * c + k + 1])

            def copy_turned(b, dst, src=None):
                wait_turned(b)
                act.activation(dst, turn[b] if src is None else src, copy).then_inc(turn_taken[b], 1)

            def load_row(name):
                act.dma_start(row[:], a[name].partition_broadcast(P)).then_inc(row_landed, 16)

            def ada_load(layer, kt, c):
                slot = t.count(ada_taken) % ADA_SLOTS
                act.wait_ge(ada_taken, t.nth(ada_taken))
                act.dma_start(ada_ring[:, slot, :], ada_w[layer][kt, c * ADA_CHUNK:(c + 1) * ADA_CHUNK]).then_inc(ada_landed[slot], ADA_LANDED)

            def ada_loads(s, at, layer, k0):
                for n in range(2 * ADA_CHUNKS):
                    if at[n] == s:
                        ada_load(layer, k0(n // ADA_CHUNKS), n % ADA_CHUNKS)

            def exps(sm, pr, heads):
                act.wait_ge(max_ready, t.nth(max_ready))
                for j in heads:
                    act.activation(pr[:, j, 0:P], sm[:, j, 0:P], ACT.Exp, bias=st_neg[:, j, 0:1], accum_out=st_den[:, j, 0:1])
                    done = act.activation(pr[:, j, P:3 * P], sm[:, j, P:3 * P], ACT.Exp, bias=st_neg[:, j, 1:2],
                                          accum_out=st_den[:, j, 1:2])
                done.then_inc(exp_ready, 1)

            load_row("g_mix_post")
            act.wait_ge(x_landed, 16)
            squares(lambda m: panels[:].rearrange("p b n -> p (b n)"), lambda m: h[:, m, :], st_sum, True)
            act.wait_ge(lam_sums, 1)
            act.activation(st_lam, st_lam, ACT.Exp).then_inc(lam_exps, 1)
            t.nth(scored[0])
            hi_plain(1, pT_hi, slice(0, 2))
            for _ in range(AHEAD):
                split_hi()
            act.wait_ge(vec_ready, 1)
            for c in range(8):
                hi_norm(c, COL_MIX)
            act.activation(c_act[:], cols[:, COL_C:COL_C + KT], ACT.Silu).then_inc(c_ready, 1)
            act.wait_ge(angles_ready, 1)
            act.activation(trig[:], trig[:], ACT.Sin).then_inc(trig_ready, 1)

            with t.rounds(2, ATTENTION) as g:
                for s in range(48):
                    if s in (19, 20, 35, 36):
                        first = 0 if s in (19, 35) else 2
                        for j in (first, first + 1):
                            copy_turned(j % 2, qkT[:, j, :])
                    if s in (22, 23, 38, 39):
                        first = 0 if s in (22, 38) else 2
                        for b in range(2):
                            t.nth(scored[b])
                        exps(sm, pr, (first, first + 1))
                    if s == 28:
                        for hh in range(2):
                            copy_turned(hh, pT[:, hh, :], turn[hh][:, 0:3 * P])
                    if s == 43:
                        for hh in range(2):
                            act.wait_ge(scored[hh], t.nth(scored[hh]))
                            for m in range(TILES):
                                done = act.activation(ob_squares[:, hh, m, :], score[hh][:, m * DIFF_V:(m + 1) * DIFF_V], ACT.Square,
                                                      scale=DIFF_V ** -0.5, accum_out=st_dsum[:, hh, m:m + 1])
                        done.then_inc(sums_ready, 1)
                        t.nth(sums_ready)
                    if s in (44, 45):
                        for j in range(2):
                            copy_turned(j, pT[:, 2 * (s - 44) + j, :], turn[j][:, 0:3 * P])
                    split_hi()
                for hh in range(2):
                    hi_scaled(hh, lambda k: yT_hi[1][:, bass.ds(g * 4 + (hh * 2 + k), 1), :].rearrange("p a t -> p (a t)"), 0,
                              lambda k: cols[:, COL_SUB + k:COL_SUB + k + 1])
                for b in range(2):
                    act.wait_ge(scored[b], t.nth(scored[b]))
                    act.activation(yT_hi[0][:, bass.ds(g * 4 + 2 * b, 2), :], score[b].rearrange("p (j t) -> p j t", t=TOKENS),
                                   copy).then_inc(turn_hi, 1)

            def sigmoid(b, dst):
                chunks_done()
                act.activation(dst, panel[b], ACT.Sigmoid).then_inc(panel_taken[b], 1)
                t.nth(panel_taken[b])

            for b in range(2):
                t.nth(panel_taken[b], 1 + 3 * 2)
            with t.rounds(4, MIX) as n:
                for s in range(24):
                    if s == 8:
                        act.wait_ge(panel_taken[1], t.now(panel_taken[1]))
                        sigmoid(0, sig[0])
                    if s == 12:
                        t.nth(panel_taken[1])
                    if s == 20:
                        act.wait_ge(panel_taken[1], t.now(panel_taken[1]))
                        sigmoid(0, sig[1])
                    split_hi()
                t.nth(panel_taken[1])
            for c in range(8):
                hi_plain(c, xT_hi, slice(2 * c, 2 * c + 2))

            with t.rounds(2, WIDE) as n:
                for s in range(17):
                    if s in (8, 16):
                        j = s // 16
                        chunks_done()
                        for m in range(TILES):
                            done = act.activation(sig[0][:, m, :], panel[j][:, m, :], ACT.Square,
                                                  accum_out=st_parts[:, m, bass.ds(n * 2 + j, 1)])
                        done.then_inc(squares_done, 1)
                        t.nth(panel_taken[j])
                    if s < 16:
                        split_hi()

            h_squares(TILES)
            load_row("g_mlp_post")

            def ada_bias(layer):
                act.wait_ge(ada_set, layer + 1)
                act.dma_start(ada_acc[0:1, :], a["ada_b_2"][layer:layer + 1, :]).then_inc(ada_row, 16)

            def up_panel(s, k):
                if s in (8, 16):
                    b = s // 16
                    chunks_done()
                    act.activation(relu, panel[b], ACT.Relu).then_inc(act_step, 1)
                    act.wait_ge(act_step, t.nth(act_step))
                    act.activation(relu, relu, ACT.Square).then_inc(panel_taken[b], 1)
                    t.nth(panel_taken[b])
                if s in (11, 19):
                    for j in range(2):
                        kt = s // 19 * 4 + 2 * j
                        hi_plain(j, yT_hi[k % 2], slice(kt, kt + 2))

            for s in range(16):
                if s == 1:
                    ada_bias(0)
                if s < 8:
                    hi_norm(s, COL_MLP)
                ada_loads(s, ada_at(16), 0, lambda k: slice(k * P, (k + 1) * P))
                up_panel(s, 0)
                split_hi()
            up_panel(16, 0)
            up_panel(19, 0)
            with t.rounds(3, FEED) as i:
                for half in range(2):
                    for s in range(32):
                        ada_loads(s, ada_at(32), 0, lambda k: bass.ds(i * 4 * P + (2 + 2 * half + k) * P, P))
                        up_panel(s, half + 1)
                        if s >= 20 and s % 4 == 0:
                            t.nth(panel_taken[s // 4 % 2 ^ 1])
                        split_hi()
                    t.nth(panel_taken[1])
            for s in range(48):
                if s < 16:
                    ada_loads(s, ada_at(16), 0, lambda k: slice((14 + k) * P, (15 + k) * P))
                up_panel(s, 7)
                if s >= 20 and s % 4 == 0:
                    t.nth(panel_taken[s // 4 % 2 ^ 1])
                split_hi()
            t.nth(panel_taken[1])
            act.wait_ge(ada_taken, ADA_SLOTS + ADA_STEPS)
            for b in range(2):
                act.wait_ge(panel_taken[b], t.now(panel_taken[b]))
            squares(lambda m: e_sb[:, m, :], lambda m: acc[:, m, :], st_sum)

            for s in range(8):
                if s % 2 == 0 and s:
                    e_panel = s // 2 - 1
                    chunks_done()
                    if e_panel == 0:
                        act.wait_ge(sums_ready, t.now(sums_ready))
                    act.activation(e_sb[:, :, e_panel * N:(e_panel + 1) * N], panel[e_panel % 2], copy).then_inc(panel_taken[e_panel % 2], 1)
                    t.nth(panel_taken[e_panel % 2])
                split_hi()
            chunks_done()
            act.activation(e_sb[:, :, 3 * N:4 * N], panel[1], copy).then_inc(panel_taken[1], 1)
            t.nth(panel_taken[1])
            h_squares(TILES)
            load_row("g_ple_post")
            for c in range(8):
                hi_norm(c, COL_PLE)
            with t.rounds(2, WIDE) as n:
                for s in range(17):
                    if s in (8, 16):
                        j = s // 16
                        sigmoid(j, acc[:, :, bass.ds(n * 2 * N + j * N, N)])
                        act.wait_ge(ple_ready, t.nth(ple_ready))
                        for m in range(TILES):
                            done = act.activation(turn[m], acc[:, m, bass.ds(n * 2 * N + j * N, N)], ACT.Square,
                                                  accum_out=st_parts[:, m, bass.ds(n * 2 + j, 1)])
                        done.then_inc(squares_done, 1)
                    if s < 16:
                        split_hi()

            h_squares(TILES)
            act.wait_ge(mods_ready, 1)

            def load_decay(head):
                act.dma_start(ret_dm, a["k_decay"][head].rearrange("h p n -> p (h n)")).then_inc(dm_landed, 16)

            def ret_y_hi(head):
                for j in range(2):
                    hi_scaled(j, yT_hi[0], 2 * j, lambda k: cols[:, bass.ds(head * 4 + (COL_GN + 2 * j + k), 1)])

            def ret_copies():
                for c in range(2):
                    copy_turned(c, ret_qkT[:, c, :, :], turn[c].rearrange("p (d t) -> p d t", t=TOKENS))

            def ret_gate():
                chunks_done()
                act.activation(ret_sg, panel[0], ACT.Silu).then_inc(panel_taken[0], 1)
                t.nth(panel_taken[0])

            load_decay(slice(0, 1))
            for s in range(24):
                if s == 1:
                    ada_bias(1)
                if s < 8:
                    hi_mod(s)
                ada_loads(s, ada_at(24), 1, lambda k: slice(k * P, (k + 1) * P))
                if s == 8:
                    t.nth(panel_taken[0])
                if s == 12:
                    ret_copies()
                if s == 16:
                    t.nth(panel_taken[1])
                split_hi()
            ret_gate()
            with t.rounds(RET_HEADS - 1, RETAIN) as i:
                for s in range(32):
                    ada_loads(s, ada_at(32), 1, lambda k: bass.ds(i * 2 * P + (2 + k) * P, P))
                    if s == 3:
                        ret_y_hi(i)
                        load_decay(bass.ds(i + 1, 1))
                    if s == 8:
                        t.nth(panel_taken[0])
                    if s == 12:
                        ret_copies()
                    if s in (10, 14, 24):
                        t.nth(panel_taken[1])
                    if s in (12, 16):
                        t.nth(panel_taken[0])
                    split_hi()
                ret_gate()
            for j in range(2):
                kt = (RET_HEADS - 1) * 4 + 2 * j
                hi_scaled(j, yT_hi[0], 2 * j, lambda k: cols[:, COL_GN + kt + k:COL_GN + kt + k + 1])
            for s in range(8):
                split_hi()

            h_squares(TILES)
            act.wait_ge(mods_ready, 2)
            for b in range(2):
                t.nth(panel_taken[b], 2)

            def lat_sums():
                chunks_done()
                squares(lambda m: lat_squares[m], lambda m: panel[0][:, m, :], st_sum)

            def lat_hi(kt, col):
                for j in range(2):
                    hi_scaled(j, yT_hi[0], kt + 2 * j, lambda k: cols[:, col + 2 * j + k:col + 2 * j + k + 1])

            for s in range(18):
                if s < 8:
                    hi_mod(s)
                if s == 8:
                    lat_sums()
                if s == 14:
                    lat_hi(4, COL_KV)
                if s == 16:
                    copy_turned(0, krT, turn[0][0:MLA_ROPE, 0:TOKENS])
                split_hi()
            lat_sums()
            with t.rounds(2, WIDE) as n:
                for s in range(17):
                    if s in (8, 16):
                        j = s // 16
                        chunks_done()
                        act.activation(sgm[:, :, bass.ds(n * 2 * N + j * N, N)], panel[1 - j], ACT.Silu).then_inc(panel_taken[1 - j], 1)
                        t.nth(panel_taken[1 - j])
                    if s < 16:
                        split_hi()
            lat_hi(0, COL_Q)

            def pair_step(s, q, r, kt=None):
                if s == 1 and r is not None:
                    exps(m_sm, m_pr, range(2))
                if s == 2 and q is not None:
                    for hh in range(2):
                        copy_turned(hh, nT[:, hh, :])
                if s == 3 and r is not None:
                    for hh in range(2):
                        copy_turned(hh, m_pT[:, hh, :], turn[hh][:, 0:3 * P])
                if s == 4:
                    if q is not None:
                        copy_turned(0, rT, turn[0][0:MLA_ROPE, :].rearrange("p (h t) -> p h t", t=TOKENS))
                    if r is not None:
                        wait_turned(1)
                        act.activation(xT_hi[:, kt, :], turn[1].rearrange("p (k t) -> p k t", t=TOKENS), copy).then_inc(turn_hi, 1)

            for p in range(2):
                for s in range(5):
                    pair_step(s, 0 if p else None, None)
                    if s < 4:
                        split_hi()
            with t.rounds(3, LATENT) as i:
                for p in range(2):
                    for s in range(5):
                        pair_step(s, 1 - p, p, bass.ds(i * 4 + 2 * p, 2))
                        if s < 4:
                            split_hi()
            for s in range(5):
                pair_step(s, 1, 0, slice(12, 14))
            for s in range(5):
                pair_step(s, None, 1, slice(14, 16))
            act.dma_start(final_row, a["final_norm_g_2"].partition_broadcast(P)).then_inc(row_landed, 16)
            for _ in range(8 - AHEAD):
                split_hi()
            with t.rounds(3, per_round(8)):
                for _ in range(8):
                    split_hi()
            h_squares(4)

        @block.vector
        def _(dve):
            t = Tally(dve)
            dve.sem_inc(ada_taken, ADA_SLOTS)
            t.nth(ada_taken, ADA_SLOTS)
            for b in range(2):
                t.nth(panel_taken[b])
                t.nth(score_taken[b])

            def split_lo():
                k = t.count(lo_ready)
                dve.wait_ge(hi_ready, t.nth(hi_ready))
                t.nth(multiplied)
                dve.tensor_tensor(lo[:, k % HI_CHUNKS, :], raw[:, k // 2 % RAW_SLOTS, k % 2 * CHUNK:(k % 2 + 1) * CHUNK],
                                  hi[:, k % HI_CHUNKS, :].bitcast(F32), ALU.subtract).then_inc(lo_ready, 1)
                t.nth(lo_ready)

            def chunks_done():
                dve.wait_ge(multiplied, t.now(multiplied, RAW_CHUNKS - AHEAD))

            def panel_done(b):
                dve.wait_ge(panel_taken[b], t.now(panel_taken[b]))

            def panel_by_act(b):
                dve.wait_ge(panel_taken[b], t.nth(panel_taken[b]))

            def steps_done():
                dve.wait_ge(dve_step, t.now(dve_step))

            def wait_rstd():
                dve.wait_ge(rstd_ready, t.nth(rstd_ready))

            def wait_scored(b):
                dve.wait_ge(scored[b], t.nth(scored[b]))

            def normalised():
                wait_rstd()
                for m in range(TILES):
                    dve.tensor_scalar(acc[:, m, :], h[:, m, :], st_rstd[:, m:m + 1], None, ALU.mult).then_inc(xs_ready, 1)

            def turned_hi():
                dve.wait_ge(turn_hi, t.nth(turn_hi))

            def two(bank):
                return bank.rearrange("p (k t) -> p k t", t=TOKENS)

            def lo_plain(c, y_hi, y_lo, kt):
                turned_hi()
                dve.tensor_tensor(y_lo[:, kt, :], two(turn[c % 2]), y_hi[:, kt, :].bitcast(F32),
                                  ALU.subtract).then_inc(turn_taken[c % 2], 1)

            def lo_scaled(b, y_hi, y_lo, gains):
                turned_hi()
                for k in range(2):
                    done = dve.scalar_tensor_tensor(y_lo(k), turn[b][:, k * TOKENS:(k + 1) * TOKENS], gains(k),
                                                    y_hi(k).bitcast(F32), ALU.mult, ALU.subtract)
                done.then_inc(turn_taken[b], 1)

            def lo_norm(c, col):
                lo_scaled(c % 2, lambda k: xT_hi[:, 2 * c + k, :], lambda k: xT_lo[:, 2 * c + k, :],
                          lambda k: cols[:, col + 2 * c + k:col + 2 * c + k + 1])

            def lo_mod(c):
                turned_hi()
                b, kt = c % 2, slice(2 * c, 2 * c + 2)
                for k in range(2):
                    done = dve.tensor_scalar(shift_tmp[:, b, k * TOKENS:(k + 1) * TOKENS], turn[b][:, k * TOKENS:(k + 1) * TOKENS],
                                             mods[:, 1, 2 * c + k:2 * c + k + 1], mods[:, 0, 2 * c + k:2 * c + k + 1],
                                             ALU.mult, ALU.add)
                done.then_inc(dve_step, 1)
                dve.wait_ge(dve_step, t.nth(dve_step))
                dve.tensor_tensor(xT_lo[:, kt, :], two(shift_tmp[:, b, :]), xT_hi[:, kt, :].bitcast(F32),
                                  ALU.subtract).then_inc(turn_taken[b], 1)

            def residual():
                wait_rstd()
                for m in range(TILES):
                    dve.scalar_tensor_tensor(h[:, m, :], acc[:, m, :], st_rstd[:, m:m + 1], h[:, m, :],
                                             ALU.mult, ALU.add).then_inc(h_ready, 1)

            def row_of(ap):
                return ap.unsqueeze(1).broadcast_to([P, TILES, ap.shape[1]])

            def ada_step(kt, c):
                slot = t.count(ada_taken) % ADA_SLOTS
                dve.wait_ge(ada_landed[slot], t.nth(ada_landed[slot], ADA_LANDED))
                dve.wait_ge(ada_taken, t.now(ada_taken))
                piece = ada_acc[:, c * ADA_CHUNK:(c + 1) * ADA_CHUNK]
                dve.scalar_tensor_tensor(piece, ada_ring[:, slot, :], c_act[:, kt], piece, ALU.mult, ALU.add).then_inc(ada_taken, 1)
                t.nth(ada_taken)

            def ada_steps(s, at, late, k0):
                for n in range(2 * ADA_CHUNKS):
                    if min(at[n] + late, at[-1] + 1) == s:
                        ada_step(k0(n // ADA_CHUNKS), n % ADA_CHUNKS)

            def rotate(x1, x2, y1, y2, cos, sin, tmp, b):
                dve.tensor_tensor(y1, x1, cos, ALU.mult)
                dve.tensor_tensor(y2, x2, cos, ALU.mult)
                dve.tensor_tensor(tmp[0], x2, sin, ALU.mult)
                dve.tensor_tensor(tmp[1], x1, sin, ALU.mult).then_inc(panel_taken[b], 1)
                dve.wait_ge(panel_taken[b], t.nth(panel_taken[b]))
                dve.tensor_tensor(y1, y1, tmp[0], ALU.subtract)
                dve.tensor_tensor(y2, y2, tmp[1], ALU.add).then_inc(roped, 1)

            def masked_scores(j0, banks, sm, scale):
                for n, b in enumerate(banks):
                    wait_scored(b)
                    dve.scalar_tensor_tensor(sm[:, j0 + n, :], score[b][:, 0:3 * P], scale, mask[:], ALU.mult,
                                             ALU.add).then_inc(score_taken[b], 1)
                    t.nth(score_taken[b])
                for b in banks:
                    dve.wait_ge(score_taken[b], t.now(score_taken[b]))
                pair = slice(j0, j0 + 2)
                dve.tensor_reduce(st_max[:, pair, 0], sm[:, pair, 0:P], AXIS_X, ALU.max)
                dve.tensor_reduce(st_max[:, pair, 1], sm[:, pair, P:3 * P], AXIS_X, ALU.max).then_inc(dve_step, 1)
                dve.wait_ge(dve_step, t.nth(dve_step))
                dve.tensor_scalar(st_neg[:, pair, :], st_max[:, pair, :], -1.0, None, ALU.mult).then_inc(max_ready, 1)

            def normalise(j0, pr, ready):
                dve.wait_ge(exp_ready, t.nth(exp_ready))
                pair = slice(j0, j0 + 2)
                dve.reciprocal(st_inv[:, pair, :], st_den[:, pair, :]).then_inc(dve_step, 1)
                dve.wait_ge(dve_step, t.nth(dve_step))
                for q, at in ((0, slice(0, P)), (1, slice(P, 3 * P))):
                    part = pr[:, pair, at]
                    done = dve.tensor_tensor(part, part, st_inv[:, pair, q:q + 1].broadcast_to([P, 2, at.stop - at.start]), ALU.mult)
                done.then_inc(ready, 1)
                t.nth(ready)

            dve.wait_ge(setup_landed, 16 * N_SETUP)
            dve.tensor_copy(st_pos, st_ipos)
            dve.tensor_tensor(lam_prods, lambdas[:, :, 0, :], lambdas[:, :, 1, :], ALU.mult).then_inc(dve_step, 1)
            dve.wait_ge(dve_step, t.nth(dve_step))
            dve.tensor_reduce(st_lam, lam_prods, AXIS_X, ALU.add).then_inc(lam_sums, 1)
            wait_scored(0)
            dve.tensor_copy(cols[:, 0:VEC_ROWS], score[0][:, 0:VEC_ROWS]).then_inc(vec_ready, 1)
            dve.tensor_copy(cols[:, COL_GN:COLS], score[0][:, COL_GN:COLS]).then_inc(score_taken[0], 1)
            t.nth(score_taken[0])
            dve.wait_ge(vec_ready, 1)
            dve.tensor_scalar(cols[:, COL_SUB:COL_SUB + 2], cols[:, COL_SUB:COL_SUB + 2], 1.0 - LAMBDA_INIT, None, ALU.mult)
            lo_plain(1, pT_hi, pT_lo, slice(0, 2))
            dve.wait_ge(lam_exps, 1)
            dve.scalar_tensor_tensor(neg_lam, st_lam[:, 1:2], -LAMBDA_INIT, st_lam[:, 0:1], ALU.add, ALU.subtract)
            normalised()
            for _ in range(AHEAD):
                split_lo()
            for c in range(8):
                lo_norm(c, COL_MIX)

            angle, cos_in = trig[:, 1, :], trig[:, 0, :]
            for m in range(TILES):
                for at, n in ((0, RET_DK), (2 * RET_DK, MLA_ROPE)):
                    part = slice(at + m * n, at + (m + 1) * n)
                    done = dve.tensor_scalar(angle[:, part], freq[:, part], st_pos[:, m:m + 1], None, ALU.mult)
            done.then_inc(dve_step, 1)
            dve.wait_ge(dve_step, t.nth(dve_step))
            dve.tensor_scalar(turns_all, angle, 1.0 / TURN, ROUND, ALU.mult, ALU.add).then_inc(dve_step, 1)
            dve.wait_ge(dve_step, t.nth(dve_step))
            dve.tensor_scalar(turns_all, turns_all, -ROUND, None, ALU.add).then_inc(dve_step, 1)
            dve.wait_ge(dve_step, t.nth(dve_step))
            dve.tensor_scalar(turns_hi, turns_all, 1.0 / MANY, ROUND, ALU.mult, ALU.add).then_inc(dve_step, 1)
            dve.wait_ge(dve_step, t.nth(dve_step))
            dve.tensor_scalar(turns_hi, turns_hi, -ROUND, MANY, ALU.add, ALU.mult).then_inc(dve_step, 1)
            dve.wait_ge(dve_step, t.nth(dve_step))
            dve.tensor_tensor(turns_all, turns_all, turns_hi, ALU.subtract).then_inc(dve_step, 1)
            dve.wait_ge(dve_step, t.nth(dve_step))
            for part in TURN_PARTS:
                for turns in (turns_hi, turns_all):
                    dve.scalar_tensor_tensor(angle, turns, -part, angle, ALU.mult, ALU.add).then_inc(dve_step, 1)
                    dve.wait_ge(dve_step, t.nth(dve_step))
            dve.tensor_scalar(angle, angle, HALF_TURN, -HALF_TURN, ALU.min, ALU.max).then_inc(dve_step, 1)
            dve.wait_ge(dve_step, t.nth(dve_step))
            dve.scalar_tensor_tensor(cos_in, angle, -1.0, angle, ALU.mult, ALU.max).then_inc(dve_step, 1)
            dve.wait_ge(dve_step, t.nth(dve_step))
            dve.tensor_scalar(cos_in, cos_in, -1.0, TURN / 4, ALU.mult, ALU.add).then_inc(angles_ready, 1)

            def q_copy():
                chunks_done()
                dve.tensor_copy(qk[:, :, 0:N], panel[0]).then_inc(panel_taken[0], 1)
                t.nth(panel_taken[0])

            def k_copy_and_rotate():
                chunks_done()
                src = panel[1].rearrange("p m (h d) -> p m h d", d=HEAD)
                dst = qk[:, :, N:2 * N].rearrange("p m (h d) -> p m h d", d=HEAD)
                rot = 2 * ROT_HALF
                dve.tensor_copy(dst[:, :, :, 0:rot], src[:, :, :, 0:rot]).then_inc(dve_step, 1)
                dve.tensor_copy(dst[:, :, :, rot:HEAD], src[:, :, :, rot:HEAD]).then_inc(panel_taken[1], 1)
                t.nth(panel_taken[1])
                dve.wait_ge(dve_step, t.nth(dve_step))
                heads = qk.rearrange("p m (h d) -> p (m h) d", d=HEAD)
                x1, x2 = heads[:, :, 0:ROT_HALF], heads[:, :, ROT_HALF:rot]
                cos, sin = (rope1[:, i, :].rearrange("p (h r) -> p h r", r=ROT_HALF) for i in range(2))
                for n, (x, y) in enumerate(((x1, cos), (x2, sin), (x2, cos), (x1, sin))):
                    done = dve.tensor_tensor(rope_tmp[:, n], x, y, ALU.mult)
                done.then_inc(dve_step, 1)
                dve.wait_ge(dve_step, t.nth(dve_step))
                dve.tensor_tensor(x1, rope_tmp[:, 0], rope_tmp[:, 1], ALU.subtract)
                dve.tensor_tensor(x2, rope_tmp[:, 2], rope_tmp[:, 3], ALU.add).then_inc(roped, 1)

            def v_copy(b):
                chunks_done()
                dve.tensor_copy(v_sb, panel[b]).then_inc(panel_taken[b], 1)
                t.nth(panel_taken[b])

            with t.rounds(2, ATTENTION) as g:
                for s in range(48):
                    if s in (8, 24):
                        q_copy()
                    if s in (16, 32):
                        k_copy_and_rotate()
                    if s in (22, 23, 38, 39):
                        masked_scores(0 if s in (22, 38) else 2, (0, 1), sm, HEAD ** -0.5)
                    if s == 25:
                        for j0 in (0, 2):
                            normalise(j0, pr, dve_step)
                        steps_done()
                        maps = pr.rearrange("p (h c) n -> p h c n", c=2)
                        dve.scalar_tensor_tensor(maps[:, :, 0, :], maps[:, :, 1, :], neg_lam, maps[:, :, 0, :], ALU.mult,
                                                 ALU.add).then_inc(probs_ready, 1)
                        t.nth(probs_ready)
                    if s == 40:
                        v_copy(0)
                    if s == 41:
                        for j0 in (0, 2):
                            normalise(j0, pr, probs_ready)
                    if s == 44:
                        wait_rstd()
                        for hh in range(2):
                            wait_scored(hh)
                            dve.tensor_tensor(ob[:, :, hh, :], score[hh].rearrange("p (m d) -> p m d", d=DIFF_V),
                                              st_drstd[:, hh, :].unsqueeze(2).broadcast_to([P, TILES, DIFF_V]),
                                              ALU.mult).then_inc(score_taken[hh], 1)
                            t.nth(score_taken[hh])
                    split_lo()
                v_copy(1)
                for hh in range(2):
                    def kt(k):
                        return bass.ds(g * 4 + (hh * 2 + k), 1)
                    lo_scaled(hh, lambda k: yT_hi[1][:, kt(k), :].rearrange("p a t -> p (a t)"),
                              lambda k: yT_lo[1][:, kt(k), :].rearrange("p a t -> p (a t)"),
                              lambda k: cols[:, COL_SUB + k:COL_SUB + k + 1])
                for b in range(2):
                    turned_hi()
                    wait_scored(b)
                    pair = bass.ds(g * 4 + 2 * b, 2)
                    dve.tensor_tensor(yT_lo[0][:, pair, :], two(score[b]), yT_hi[0][:, pair, :].bitcast(F32),
                                      ALU.subtract).then_inc(score_taken[b], 1)
                    t.nth(score_taken[b])

            with t.rounds(4, MIX) as n:
                for s in range(24):
                    if s == 12:
                        panel_by_act(0)
                        chunks_done()
                        dve.tensor_tensor(gated, panel[1], sig[0], ALU.mult).then_inc(panel_taken[1], 1)
                        t.nth(panel_taken[1])
                    split_lo()
                panel_by_act(0)
                chunks_done()
                dve.tensor_tensor(sig[1], panel[1], sig[1], ALU.mult).then_inc(panel_taken[1], 1)
                t.nth(panel_taken[1])
                panel_done(1)
                dve.tensor_tensor(acc[:, :, bass.ds(n * N, N)], gated, sig[1], ALU.add).then_inc(mixed_ready, 1)
            for c in range(8):
                lo_plain(c, xT_hi, xT_lo, slice(2 * c, 2 * c + 2))

            dve.wait_ge(row_landed, 16)
            with t.rounds(2, WIDE) as n:
                for s in range(17):
                    if s in (8, 16):
                        j = s // 16
                        dve.wait_ge(squares_done, t.nth(squares_done))
                        at = bass.ds(n * 2 * N + j * N, N)
                        dve.tensor_tensor(acc[:, :, at], panel[j], row_of(row[:, at]), ALU.mult).then_inc(panel_taken[j], 1)
                        t.nth(panel_taken[j])
                    if s < 16:
                        split_lo()
            for b in range(2):
                panel_done(b)
            residual()

            def up_panel(s, k):
                if s in (8, 16):
                    t.nth(panel_taken[s // 16])
                if s in (11, 19):
                    for j in range(2):
                        kt = s // 19 * 4 + 2 * j
                        lo_plain(j, yT_hi[k % 2], yT_lo[k % 2], slice(kt, kt + 2))

            def down_panel(n):
                chunks_done()
                part = acc[:, :, n * N:(n + 1) * N]
                dve.tensor_tensor(part, panel[n % 2], part, ALU.add).then_inc(panel_taken[n % 2], 1)
                t.nth(panel_taken[n % 2])

            normalised()
            for s in range(16):
                if s < 8:
                    lo_norm(s, COL_MLP)
                if s == 8:
                    dve.memset(acc[:], 0.0)
                if s == 2:
                    dve.wait_ge(c_ready, 1)
                    dve.wait_ge(ada_row, 16)
                ada_steps(s, ada_at(16), 2, lambda k: slice(k, k + 1))
                up_panel(s, 0)
                split_lo()
            up_panel(16, 0)
            up_panel(19, 0)
            with t.rounds(3, FEED) as i:
                for half in range(2):
                    for s in range(32):
                        ada_steps(s, ada_at(32), 2, lambda k: bass.ds(i * 4 + (2 + 2 * half + k), 1))
                        up_panel(s, half + 1)
                        if s >= 20 and s % 4 == 0:
                            down_panel(s // 4 - 5)
                        split_lo()
                    down_panel(3)
            for s in range(48):
                if s < 16:
                    ada_steps(s, ada_at(16), 2, lambda k: slice(14 + k, 15 + k))
                up_panel(s, 7)
                if s >= 20 and s % 4 == 0:
                    down_panel((s // 4 - 5) % 4)
                split_lo()
            down_panel(3)

            dve.wait_ge(row_landed, 16 * 2)
            dve.wait_ge(sums_ready, 5)
            dve.tensor_tensor(acc[:], acc[:], row_of(row[:]), ALU.mult).then_inc(dve_step, 1)
            dve.wait_ge(dve_step, t.nth(dve_step))
            residual()
            for s in range(8):
                split_lo()
            for b in range(2):
                t.nth(panel_taken[b], 2)
            normalised()
            for c in range(8):
                lo_norm(c, COL_PLE)

            for b in range(2):
                panel_done(b)
            with t.rounds(2, WIDE) as n:
                for s in range(17):
                    if s in (8, 16):
                        j = s // 16
                        panel_by_act(j)
                        at = bass.ds(n * 2 * N + j * N, N)
                        dve.tensor_tensor(acc[:, :, at], acc[:, :, at], e_sb[:, :, at], ALU.mult).then_inc(ple_ready, 1)
                    if s < 16:
                        split_lo()
            dve.wait_ge(row_landed, 16 * 3)
            dve.wait_ge(squares_done, t.nth(squares_done, 4))
            dve.tensor_tensor(acc[:], acc[:], row_of(row[:]), ALU.mult).then_inc(dve_step, 1)
            dve.wait_ge(dve_step, t.nth(dve_step))
            residual()

            def modulation(layer):
                wait_scored(0)
                dve.tensor_copy(mods[:], score[0][:, 0:3 * KT].rearrange("p (a k) -> p a k", k=KT)).then_inc(score_taken[0], 1)
                dve.wait_ge(score_taken[0], t.nth(score_taken[0]))
                gain = cols[:, COL_NORM + layer * KT:COL_NORM + (layer + 1) * KT]
                dve.scalar_tensor_tensor(mods[:, 1, :], mods[:, 1, :], 1.0, gain, ALU.add, ALU.mult).then_inc(mods_ready, 1)

            def gate_row():
                for n in range(4):
                    wait_scored(n % 2)
                    dve.tensor_copy(row[:, n * N:(n + 1) * N], score[n % 2]).then_inc(score_taken[n % 2], 1)
                    t.nth(score_taken[n % 2])

            modulation(0)

            def ret_rotate():
                chunks_done()
                src, dst = (x.rearrange("p m (c x f) -> p (m c) x f", c=2, x=2) for x in (panel[0], ret_qk))
                cos, sin = (trig[:, i, 0:2 * RET_DK].rearrange("p (n f) -> p n f", f=RET_DK // 2) for i in range(2))
                tmp = [ret_sg[:, i, :].rearrange("p (n f) -> p n f", f=RET_DK // 2) for i in range(2)]
                rotate(src[:, :, 0, :], src[:, :, 1, :], dst[:, :, 0, :], dst[:, :, 1, :], cos, sin, tmp, 0)

            def ret_decay():
                wait_scored(0)
                dve.wait_ge(dm_landed, t.nth(dm_landed, 16))
                dve.tensor_tensor(ret_sT, score[0][:, 0:3 * P], ret_dm, ALU.mult).then_inc(score_taken[0], 1)
                t.nth(score_taken[0])

            def ret_v_copy():
                chunks_done()
                dve.tensor_copy(ret_v, panel[1]).then_inc(panel_taken[1], 1)
                t.nth(panel_taken[1])

            def ret_moments():
                for m in range(TILES):
                    wait_scored(m)
                    done = dve.bn_stats(st_bn[:, m, :], score[m])
                done.then_inc(dve_step, 1)
                dve.wait_ge(dve_step, t.nth(dve_step))
                if t.i is not None:
                    dve.sem_inc(dve_waited, 1)
                dve.bn_aggr(st_mv[:, 0, :], st_bn[:, 0, :])
                dve.bn_aggr(st_mv[:, 1, :], st_bn[:, 1, :]).then_inc(sums_ready, 1)

            def ret_group_norm():
                wait_rstd()
                for m in range(TILES):
                    dve.tensor_scalar(ret_yn[:, m, :], score[m], st_mv[:, m, 0:1], st_rstd[:, m:m + 1], ALU.subtract,
                                      ALU.mult).then_inc(score_taken[m], 1)
                    t.nth(score_taken[m])

            def ret_gated():
                panel_by_act(0)
                for b in range(2):
                    dve.wait_ge(score_taken[b], t.now(score_taken[b]))
                dve.tensor_tensor(ret_sg, ret_sg, ret_yn, ALU.mult).then_inc(yg_ready, 1)

            def ret_out_panel(n):
                chunks_done()
                b = (1 + n) % 2
                part = acc[:, :, n * N:(n + 1) * N]
                dve.tensor_tensor(part, panel[b], part, ALU.add).then_inc(panel_taken[b], 1)
                t.nth(panel_taken[b])

            def ret_y_lo(gains):
                for j in range(2):
                    lo_scaled(j, lambda k: yT_hi[0][:, 2 * j + k, :], lambda k: yT_lo[0][:, 2 * j + k, :],
                              lambda k: gains(2 * j + k))

            normalised()
            for s in range(24):
                if s < 8:
                    lo_mod(s)
                if s == 2:
                    dve.wait_ge(ada_row, 16 * 2)
                ada_steps(s, ada_at(24), 2, lambda k: slice(k, k + 1))
                if s == 8:
                    dve.wait_ge(trig_ready, 1)
                    ret_rotate()
                    dve.memset(acc[:], 0.0)
                if s == 15:
                    ret_decay()
                if s == 16:
                    ret_v_copy()
                if s == 19:
                    ret_moments()
                if s == 21:
                    ret_group_norm()
                split_lo()
            ret_gated()
            with t.rounds(RET_HEADS - 1, RETAIN) as i:
                for s in range(32):
                    ada_steps(s, ada_at(32), 2, lambda k: bass.ds(i * 2 + (2 + k), 1))
                    if s == 3:
                        ret_y_lo(lambda kt: cols[:, bass.ds(i * 4 + (COL_GN + kt), 1)])
                    if s == 8:
                        ret_rotate()
                    if s in (10, 12, 14, 16):
                        ret_out_panel((s - 10) // 2)
                    if s == 15:
                        ret_decay()
                    if s == 24:
                        ret_v_copy()
                    if s == 27:
                        ret_moments()
                    if s == 29:
                        ret_group_norm()
                    split_lo()
                ret_gated()
            ret_y_lo(lambda kt: cols[:, COL_GN + (RET_HEADS - 1) * 4 + kt:COL_GN + (RET_HEADS - 1) * 4 + kt + 1])
            gate_row()
            for s in range(9):
                if s in (2, 4, 6, 8):
                    n = s // 2 - 1
                    ret_out_panel(n)
                    panel_done((1 + n) % 2)
                    at = slice(n * N, (n + 1) * N)
                    dve.tensor_tensor(acc[:, :, at], acc[:, :, at], row_of(row[:, at]), ALU.mult).then_inc(dve_step, 1)
                    dve.wait_ge(dve_step, t.nth(dve_step))
                    for m in range(TILES):
                        done = dve.tensor_tensor(h[:, m, at], h[:, m, at], acc[:, m, at], ALU.add)
                        if n == 3:
                            done.then_inc(h_ready, 1)
                if s < 8:
                    split_lo()
            modulation(1)

            def latent():
                wait_rstd()
                for m in range(TILES):
                    done = dve.tensor_scalar(lat[:, m, :], panel[0][:, m, :], st_rstd[:, m:m + 1], None, ALU.mult)
                done.then_inc(panel_taken[0], 1)
                t.nth(panel_taken[0])

            def lat_lo(kt, col):
                for j in range(2):
                    lo_scaled(j, lambda k: yT_hi[0][:, kt + 2 * j + k, :], lambda k: yT_lo[0][:, kt + 2 * j + k, :],
                              lambda k: cols[:, col + 2 * j + k:col + 2 * j + k + 1])

            mla_cos, mla_sin = (trig[:, i, 2 * RET_DK:640].rearrange("p (m h f) -> p m h f", m=TILES, h=2) for i in range(2))
            half = MLA_ROPE // 2
            normalised()
            for s in range(18):
                if s < 8:
                    lo_mod(s)
                if s == 8:
                    latent()
                if s == 9:
                    gate_row()
                if s == 10:
                    chunks_done()
                    tmp = [mla_tmp[:, i, 0:TILES * half].rearrange("p (m f) -> p m f", f=half) for i in range(2)]
                    rotate(panel[1][:, :, 0:half], panel[1][:, :, half:2 * half], kr[:, :, 0:half], kr[:, :, half:2 * half],
                           mla_cos[:, :, 0, :], mla_sin[:, :, 0, :], tmp, 1)
                if s == 14:
                    lat_lo(4, COL_KV)
                split_lo()
            latent()
            with t.rounds(2, WIDE) as n:
                for s in range(16):
                    split_lo()
                for b in range(2):
                    t.nth(panel_taken[b])
            lat_lo(0, COL_Q)

            def q_copy_and_rotate(p):
                chunks_done()
                src, dst = (x.rearrange("p m (h d) -> p m h d", h=2) for x in (panel[0][:, :, 0:MLA_QW], q_sb[p]))
                dve.tensor_copy(dst[:, :, :, 0:MLA_NOPE], src[:, :, :, 0:MLA_NOPE])
                x1, x2 = slice(MLA_NOPE, MLA_NOPE + half), slice(MLA_NOPE + half, MLA_NOPE + 2 * half)
                tmp = [mla_tmp[:, i, :].rearrange("p (m h f) -> p m h f", m=TILES, h=2) for i in range(2)]
                rotate(src[:, :, :, x1], src[:, :, :, x2], dst[:, :, :, x1], dst[:, :, :, x2], mla_cos, mla_sin, tmp, 0)

            def pair_step(s, p, r, cols_r=None, kt=None):
                if s == 0 and r is not None:
                    masked_scores(0, (1, 0), m_sm, (MLA_NOPE + MLA_ROPE) ** -0.5)
                if s == 1 and r is not None:
                    normalise(0, m_pr, probs_ready)
                if s == 2 and p is not None:
                    q_copy_and_rotate(p)
                if s == 4:
                    if r is not None:
                        wait_scored(0)
                        dve.tensor_tensor(og, score[0].rearrange("p (m d) -> p m d", m=TILES), sgm[:, :, cols_r],
                                          ALU.mult).then_inc(score_taken[0], 1)
                        t.nth(score_taken[0])
                    if p is not None:
                        chunks_done()
                        dve.tensor_copy(kv_sb[p], panel[1]).then_inc(panel_taken[1], 1)
                        t.nth(panel_taken[1])
                    if r is not None:
                        lo_plain(1, xT_hi, xT_lo, kt)

            for p in range(2):
                for s in range(5):
                    pair_step(s, p, None)
                    if s < 4:
                        split_lo()
            for b in range(2):
                panel_done(b)
            with t.rounds(3, LATENT) as i:
                for p in range(2):
                    for s in range(5):
                        pair_step(s, p, p, bass.ds(i * 4 * P + 2 * p * P, 2 * P), bass.ds(i * 4 + 2 * p, 2))
                        if s < 4:
                            split_lo()
            for p in range(2):
                pair = 6 + p
                for s in range(5):
                    pair_step(s, None, p, slice(pair * 2 * P, (pair + 1) * 2 * P), slice(2 * pair, 2 * pair + 2))

            for n in range(4):
                for s in range(8):
                    if n * 8 + s < 32 - AHEAD:
                        split_lo()
                dve.wait_ge(multiplied, t.now(multiplied, RAW_CHUNKS - (AHEAD if n < 3 else 0)))
                at, b = slice(n * N, (n + 1) * N), n % 2
                dve.tensor_tensor(acc[:, :, at], panel[b], row_of(row[:, at]), ALU.mult).then_inc(panel_taken[b], 1)
                t.nth(panel_taken[b])
                panel_done(b)
                dve.tensor_tensor(h[:, :, at], h[:, :, at], acc[:, :, at], ALU.add).then_inc(h_ready, 1)
            dve.wait_ge(row_landed, 16 * 4)
            wait_rstd()
            for m in range(TILES):
                dve.scalar_tensor_tensor(acc[:, m, :], h[:, m, :], st_rstd[:, m:m + 1], final_row, ALU.mult,
                                         ALU.mult).then_inc(out_ready, 1)

        @block.gpsimd
        def _(pool):
            t = Tally(pool)
            pool.memset(ones[:], 1.0)
            pool.memset(eps[:], EPS)
            pool.memset(neg_half[:], -0.5).then_inc(pool_step, 1)
            pool.wait_ge(pool_step, t.nth(pool_step))

            def rstd_of(dst, mean):
                pool.tensor_tensor(dst, mean, eps[:, 0:dst.shape[1]], ALU.add).then_inc(pool_step, 1)
                pool.wait_ge(pool_step, t.nth(pool_step))
                pool.tensor_tensor(dst, dst, neg_half[:, 0:dst.shape[1]], ALU.pow).then_inc(rstd_ready, 1)

            def mean_of(sums, width):
                pool.tensor_scalar(sums, sums, 1.0 / width, None, ALU.mult).then_inc(pool_step, 1)
                pool.wait_ge(pool_step, t.nth(pool_step))

            def rstd(width):
                pool.wait_ge(sums_ready, t.nth(sums_ready))
                mean_of(st_sum, width)
                rstd_of(st_rstd, st_sum)

            def rstd_parts():
                pool.wait_ge(squares_done, t.nth(squares_done, 4))
                pool.tensor_tensor(st_parts[:, :, 0:2], st_parts[:, :, 0:2], st_parts[:, :, 2:4], ALU.add).then_inc(pool_step, 1)
                pool.wait_ge(pool_step, t.nth(pool_step))
                pool.tensor_tensor(st_sum, st_parts[:, :, 0], st_parts[:, :, 1], ALU.add).then_inc(pool_step, 1)
                pool.wait_ge(pool_step, t.nth(pool_step))
                mean_of(st_sum, D)
                rstd_of(st_rstd, st_sum)

            def gate_diagonals():
                for k in range(KT):
                    done = pool.tensor_scalar(diag[:, k * P:(k + 1) * P], ident[:], mods[:, 2, k:k + 1], None, ALU.mult)
                done.then_inc(diag_ready, 1)

            rstd(D)
            with t.rounds(2, ATTENTION):
                pool.wait_ge(sums_ready, t.nth(sums_ready))
                rstd_of(stats[:, 80:84], stats[:, 76:80])
            rstd_parts()
            rstd(D)
            pool.memset(ada_acc, 0.0).then_inc(ada_set, 1)
            rstd(D)
            rstd(D)
            rstd_parts()
            rstd(D)
            pool.wait_ge(mods_ready, 1)
            pool.memset(ada_acc, 0.0).then_inc(ada_set, 1)

            def group_rstd():
                pool.wait_ge(sums_ready, t.nth(sums_ready))
                rstd_of(st_rstd, st_mv[:, :, 1])

            group_rstd()
            with t.rounds(RET_HEADS - 1, RETAIN):
                group_rstd()
            pool.wait_ge(ada_taken, ADA_SLOTS + 2 * ADA_STEPS)
            gate_diagonals()
            rstd(D)
            pool.wait_ge(mods_ready, 2)
            gate_diagonals()
            rstd(MLA_RANK)
            rstd(MLA_RANK)
            rstd(D)


def constants():
    import numpy as np

    i = np.arange(P)
    causal = np.where(i[None, :] <= i[:, None], 0.0, -3e38)
    mask = np.concatenate([causal, np.zeros((P, P)), causal], 1)
    theta = 1.0 / 500000.0 ** (np.arange(ROT_HALF) * 2.0 / (2 * ROT_HALF))
    angle = (np.arange(TOKENS, dtype=np.float32)[:, None] * theta.astype(np.float32)[None, :]).astype(np.float64)
    rope1 = np.stack([np.cos(angle), np.sin(angle)])
    rope1 = np.broadcast_to(rope1.reshape(2, TILES, P, 1, ROT_HALF), (2, TILES, P, 8, ROT_HALF))
    rope1 = rope1.transpose(2, 0, 1, 3, 4).reshape(P, 2, TILES * 8 * ROT_HALF)
    freq = [10000.0 ** (-np.arange(0, d, 2) / d) for d in (RET_DK, MLA_ROPE)]
    freq = np.concatenate([np.tile(f, 2 * TILES) for f in freq])
    log_gamma = np.log1p(-np.exp2(-5.0 - np.arange(RET_HEADS)))
    n, m = np.arange(TOKENS)[None, :], np.arange(TOKENS)[:, None]
    decay = np.where(n >= m, np.exp(log_gamma[:, None, None] * np.maximum(n - m, 0)), 0.0) * RET_DK ** -0.5
    decay = np.concatenate([decay[:, 0:P, :], decay[:, P:2 * P, P:2 * P]], 2)
    made = {"k_ident": np.eye(P), "k_mask": mask, "k_rope1": rope1, "k_freq": freq, "k_decay": decay}
    return {name: np.ascontiguousarray(x.astype(np.float32)) for name, x in made.items()}


INPUTS = ["x", "p", "w_in", "w_br_moba", "w_br_diff", "w_out", "lambda_q1", "lambda_k1", "lambda_q2", "lambda_k2",
          "diff_subln_g", "g_mix_pre", "g_mix_post", "w_up", "w_down", "g_mlp_pre", "g_mlp_post", "w_ple_proj",
          "w_ple_gate", "g_ple_pre", "g_ple_post", "c_2", "positions_2", "ada_w_2", "ada_b_2", "norm_g_2", "ret_w_in_2",
          "ret_gn_g_2", "ret_w_out_2", "mla_w_in_2", "mla_q_norm_g_2", "mla_w_uq_2", "mla_kv_norm_g_2",
          "mla_w_ukv_2", "mla_w_out_2", "final_norm_g_2"]


def kernel(**inputs):
    import concourse.bacc as bacc
    import numpy as np
    from concourse.bass_utils import run_bass_kernel_spmd

    nc = bacc.Bacc("TRN2", target_bir_lowering=False, num_devices=1, dynamic_dma_scratch_size=1024)
    arrays = {name: np.ascontiguousarray(inputs[name]) for name in INPUTS}
    arrays.update(constants())
    aps = {name: nc.dram_tensor(name, x.shape, mybir.dt.from_np(x.dtype), kind="ExternalInput").ap()
           for name, x in arrays.items()}
    out = nc.dram_tensor("out_0", (1, TOKENS, D), F32, kind="ExternalOutput").ap()
    build(nc, aps, out)
    r = run_bass_kernel_spmd(nc, [arrays], core_ids=[0])
    return r.results[0]["out_0"]
```

```python
from contextlib import ExitStack, contextmanager

import concourse.bass as bass
from concourse import mybir

F32 = mybir.dt.float32
F32R = mybir.dt.float32r
I32 = mybir.dt.int32
ACT = mybir.ActivationFunctionType
ALU = mybir.AluOpType
AXIS_X = mybir.AxisListType.X

P = 128
TOKENS = 256
TILES = TOKENS // P
D = 2048
KT = D // P
EPS = 1e-6
HALF_TURN = 3.1415925
TURN = 6.283185307179586
TURN_PARTS = (6.28125, 2.0 ** -19 * 1014, TURN - 6.28125 - 2.0 ** -19 * 1014)
MANY = 4096.0
ROUND = 1.5 * 2.0 ** 23

HEAD = 128
ROT_HALF = 16
MOBA_W = 1024
DIFF_V = 256
FF = 8192
FF_BLOCK = 1024
LAMBDA_INIT = 0.2

RET_HEADS = 8
RET_DK = 256
RET_DV = 512
MLA_HEADS = 16
MLA_NOPE = 128
MLA_ROPE = 64
MLA_RANK = 512
MLA_QW = 2 * (MLA_NOPE + MLA_ROPE)

RAW_SLOTS = 4
CHUNK = 1024
RAW_CHUNKS = 2 * RAW_SLOTS
HI_CHUNKS = 4
AHEAD = 3
LANDED = 32
N = 512

ADA_W = 3 * D
ADA_CHUNK = 1024
ADA_CHUNKS = ADA_W // ADA_CHUNK
ADA_STEPS = KT * ADA_CHUNKS
ADA_SLOTS = 2
ADA_LANDED = 16
N_VECTORS = 8
N_EARLY = 6
N_LATE = 4

COL_MIX, COL_MLP, COL_PLE, COL_NORM, COL_C = 0, 16, 32, 48, 80
COL_Q, COL_KV, COL_SUB, VEC_ROWS = 96, 100, 104, 106
COL_GN = VEC_ROWS
COLS = VEC_ROWS + RET_HEADS * RET_DV // P


class Tally:

    def __init__(self, engine):
        self.engine, self.seen, self.i, self.per = engine, {}, None, {}

    def now(self, sem, ahead=0):
        n = self.seen.get(sem.name, 0) + ahead
        if self.i is None:
            return n
        per = self.per[sem.name]
        return self.i * per + n if per else n

    def nth(self, sem, k=1):
        self.seen[sem.name] = self.seen.get(sem.name, 0) + k
        return self.now(sem)

    def count(self, sem):
        return self.seen.get(sem.name, 0)

    @contextmanager
    def rounds(self, n, per):
        per = {sem.name: k for sem, k in per}
        before = dict(self.seen)
        with self.engine.Fori(0, n) as i:
            self.i, self.per = i, per
            yield i
            self.i = None
        for name in self.seen:
            once = self.seen[name] - before.get(name, 0)
            assert once in (0, per.get(name, 0)), (name, once, per.get(name))
            self.seen[name] = before.get(name, 0) + n * once


def build(nc, a, out):
    w_in, w_br_moba, w_br_diff, w_out = a["w_in"][0], a["w_br_moba"][0], a["w_br_diff"][0], a["w_out"][0]
    w_up, w_down, w_ple_proj, w_ple_gate = a["w_up"][0], a["w_down"][0], a["w_ple_proj"][0], a["w_ple_gate"][0]
    ret_in, ret_out = a["ret_w_in_2"][0], a["ret_w_out_2"][0]
    mla_in, mla_uq, mla_ukv, mla_out = a["mla_w_in_2"][0], a["mla_w_uq_2"][0], a["mla_w_ukv_2"][0], a["mla_w_out_2"][0]
    ada_w = a["ada_w_2"]

    with ExitStack() as ctx:
        def sb(name, shape, dt=F32):
            return ctx.enter_context(nc.sbuf_tensor(name, shape, dt))

        def sem(name):
            return ctx.enter_context(nc.semaphore(name))

        raw = sb("raw", [P, RAW_SLOTS, 2 * CHUNK])
        hi = sb("hi", [P, HI_CHUNKS, CHUNK], F32R)
        lo = sb("lo", [P, HI_CHUNKS, CHUNK], F32R)
        xT_hi, xT_lo = sb("xT_hi", [P, KT, TOKENS], F32R), sb("xT_lo", [P, KT, TOKENS], F32R)
        yT_hi = [sb(f"yT{i}_hi", [P, 8, TOKENS], F32R) for i in range(2)]
        yT_lo = [sb(f"yT{i}_lo", [P, 8, TOKENS], F32R) for i in range(2)]
        pT_hi, pT_lo = sb("pT_hi", [P, 2, TOKENS], F32R), sb("pT_lo", [P, 2, TOKENS], F32R)
        h = sb("h", [P, TILES, D])
        acc = sb("acc", [P, TILES, D])
        row = sb("row", [P, D])
        WORK = 10240
        work = sb("work", [P, WORK])
        ident = sb("ident", [P, P])
        ones = sb("ones", [P, P])
        mask = sb("mask", [P, 3 * P])
        cols = sb("cols", [P, COLS])
        mods = sb("mods", [P, 3, KT])
        c_act = sb("c_act", [P, KT])
        rope1 = sb("rope1", [P, 2, 2 * 8 * ROT_HALF])
        trig = sb("trig", [P, 2, 640])
        stats = sb("stats", [P, 96])
        neg_half, eps = sb("neg_half", [P, 4]), sb("eps", [P, 4])

        def carve(at, *shape):
            n = 1
            for s in shape:
                n *= s
            assert at + n <= WORK, (at, shape)
            piece = work[:, at:at + n]
            if len(shape) == 2:
                return piece.rearrange("p (a b) -> p a b", b=shape[1])
            if len(shape) == 3:
                return piece.rearrange("p (a b c) -> p a b c", b=shape[1], c=shape[2])
            return piece

        panels = ctx.enter_context(nc.psum_tensor("panels", [P, 2 * TILES, N], F32))
        spare = ctx.enter_context(nc.psum_tensor("spare", [P, 4, N], F32))
        panel = [panels[:, 0:TILES, :], panels[:, TILES:2 * TILES, :], spare[:, 0:TILES, :]]
        turn = [spare[:, 0, :], spare[:, 1, :]]
        score = [spare[:, 2, :], spare[:, 3, :]]

        first_landed, vec_landed, late_landed = sem("first_landed"), sem("vec_landed"), sem("late_landed")
        ones_set = sem("ones_set")
        x_landed = [sem(f"x_landed{n}") for n in range(4)]
        raw_landed = [sem(f"raw_landed{i}") for i in range(RAW_SLOTS)]
        multiplied, hi_ready, lo_ready = sem("multiplied"), sem("hi_ready"), sem("lo_ready")
        panel_taken = [sem("panel_taken0"), sem("panel_taken1")]
        turned, turn_taken = [sem("turned0"), sem("turned1")], [sem("turn_taken0"), sem("turn_taken1")]
        scored, score_taken = [sem("scored0"), sem("scored1")], [sem("score_taken0"), sem("score_taken1")]
        turn_hi = sem("turn_hi")
        sums_ready, rstd_ready = sem("sums_ready"), sem("rstd_ready")
        h_ready, xs_ready = sem("h_ready"), sem("xs_ready")
        sp_waited, pe_waited, dve_waited, pool_step, dve_step, act_step = sem("sp_waited"), sem("pe_waited"), sem("dve_waited"), sem("pool_step"), sem("dve_step"), sem("act_step")
        lam_sums, lam_exps = sem("lam_sums"), sem("lam_exps")
        angles_ready, trig_ready, c_ready = sem("angles_ready"), sem("trig_ready"), sem("c_ready")
        roped = sem("roped")
        max_ready, exp_ready, probs_ready = sem("max_ready"), sem("exp_ready"), sem("probs_ready")
        pair_exps_ready = sem("pair_exps_ready")
        mixed_ready, squares_done = sem("mixed_ready"), sem("squares_done")
        ada_landed = [sem(f"ada_landed{i}") for i in range(ADA_SLOTS)]
        acc_zeroed, ada_set, ada_row, ada_taken, mods_ready = sem("acc_zeroed"), sem("ada_set"), sem("ada_row"), sem("ada_taken"), sem("mods_ready")
        row_landed, silu_ready = sem("row_landed"), sem("silu_ready")
        ple_ready, dm_landed, yg_ready = sem("ple_ready"), sem("dm_landed"), sem("yg_ready")
        out_ready, out_landed = sem("out_ready"), sem("out_landed")

        vec_mix, vec, vec_gn = (acc[:, 0, i * P:(i + 1) * P] for i in range(3))
        lambdas = acc[:, 0, 896:896 + 4 * HEAD].rearrange("p (a b d) -> p a b d", a=2, d=HEAD)
        lam_prods = acc[:, 0, 1536:1536 + 2 * HEAD].rearrange("p (a d) -> p a d", d=HEAD)
        x_squares = carve(0, TILES, D)
        freq, turns_all, turns_hi = carve(8192, 640), carve(6656, 640), carve(7296, 640)
        p_in = carve(8832, TILES, 256)
        qk = carve(0, TILES, 8 * HEAD)
        v_sb = carve(2048, TILES, N)
        qkT = carve(3072, 4, 4 * P)
        sm = carve(5120, 4, 3 * P)
        pr = carve(6656, 4, 3 * P)
        pT = carve(8192, 4, 3 * P)
        ob = acc[:, 0, 0:1024].rearrange("p (m h d) -> p m h d", m=TILES, d=DIFF_V)
        ob_squares = acc[:, 0, 1024:2048].rearrange("p (h m d) -> p h m d", m=TILES, d=DIFF_V)
        rope_tmp = acc[:, 1, 0:1024].rearrange("p (n h r) -> p n h r", n=4, r=ROT_HALF)
        sig = [carve(0, TILES, N), carve(1024, TILES, N)]
        gated = carve(2048, TILES, N)
        ada_acc = carve(0, ADA_W)
        ada_ring = carve(ADA_W, ADA_SLOTS, ADA_CHUNK)
        relu = carve(8192, TILES, N)
        e_sb = carve(6144, TILES, D)
        shift_tmp = carve(8192, 2, N)
        ret_qk = carve(8192, TILES, N)
        ret_v = ret_qk
        ret_yn = ret_qk
        ret_sT = carve(9216, 3 * P)
        ret_dm = carve(9600, 3 * P)
        ret_sg = row[:, 0:1024].rearrange("p (m n) -> p m n", n=N)
        ret_qkT = row[:, 1024:2048].rearrange("p (c d t) -> p c d t", c=2, t=TOKENS)
        sgm = acc
        q_sb = [carve(i * 768, TILES, MLA_QW) for i in range(2)]
        kv_sb = [carve(1536 + i * 1024, TILES, N) for i in range(2)]
        lat = carve(6528, TILES, N)
        nT = carve(4608, 2, 4 * P)
        rT = work[0:MLA_ROPE, 5632:5632 + 2 * TOKENS].rearrange("p (h t) -> p h t", t=TOKENS)
        krT = work[0:MLA_ROPE, 6144:6144 + TOKENS]
        kr = carve(6400, TILES, MLA_ROPE)
        kr_in = carve(7808, TILES, MLA_ROPE)
        krF = work[0:MLA_ROPE, 7552:7552 + TOKENS]
        m_sm = carve(6528, 2, 3 * P)
        m_exps = carve(7296, 2, 3 * P)
        m_pT = carve(8064, 2, 3 * P)
        og = carve(8832, TILES, 2 * P)
        mla_tmp = carve(9344, 2, 128)
        lat_squares = [carve(9728, N), carve(9216, N)]
        final_row = carve(0, D)

        st_sum = stats[:, 0:2]
        st_rstd = stats[:, 2:4]
        st_parts = stats[:, 8:16].rearrange("p (m n) -> p m n", n=4)
        st_max = stats[:, 16:24].rearrange("p (h q) -> p h q", q=2)
        st_neg = stats[:, 24:32].rearrange("p (h q) -> p h q", q=2)
        st_den = stats[:, 32:40].rearrange("p (h q) -> p h q", q=2)
        st_inv = stats[:, 40:48].rearrange("p (h q) -> p h q", q=2)
        st_lam = stats[:, 48:50]
        neg_lam = stats[:, 50:51]
        st_pos = stats[:, 52:54]
        st_ipos = stats[:, 54:56].bitcast(I32)
        st_bn = stats[:, 60:72].rearrange("p (m s) -> p m s", s=6)
        st_mv = stats[:, 72:76].rearrange("p (m s) -> p m s", s=2)
        st_dsum = stats[:, 76:80].rearrange("p (h m) -> p h m", m=TILES)
        st_drstd = stats[:, 80:84].rearrange("p (h m) -> p h m", m=TILES)

        def per_round(chunks, panels=(0, 0), turns=(0, 0), scores=(0, 0), ada=0, more=()):
            assert chunks % RAW_CHUNKS == 0
            base = [(multiplied, chunks), (hi_ready, chunks), (lo_ready, chunks)]
            base += [(s, chunks // RAW_CHUNKS * LANDED) for s in raw_landed]
            for b in range(2):
                base += [(panel_taken[b], panels[b]), (turned[b], turns[b]), (turn_taken[b], turns[b]),
                         (scored[b], scores[b]), (score_taken[b], scores[b])]
            base += [(s, ada // ADA_SLOTS * ADA_LANDED) for s in ada_landed] + [(ada_taken, ada)]
            return base + list(more)

        ATTENTION = per_round(48, (3, 3), (8, 8), (6, 6), 0, (
            (roped, 2), (max_ready, 4), (exp_ready, 4), (probs_ready, 3), (turn_hi, 4), (sums_ready, 1),
            (rstd_ready, 1), (dve_step, 14), (pool_step, 1)))
        MIX = per_round(24, (2, 2), more=((mixed_ready, 1),))
        WIDE = per_round(16, (1, 1), more=())
        FEED = per_round(64, (6, 6), (4, 4), ada=24, more=((act_step, 4), (turn_hi, 8)))
        RETAIN = per_round(32, (3, 3), (2, 2), (2, 1), 12, (
            (roped, 1), (silu_ready, 1), (sums_ready, 1), (rstd_ready, 1), (yg_ready, 1), (turn_hi, 2), (dm_landed, 16),
            (dve_step, 1), (pool_step, 1)))
        LATENT = per_round(8, (2, 2), (6, 6), (4, 2), 0, (
            (roped, 2), (max_ready, 2), (pair_exps_ready, 2), (turn_hi, 2), (dve_step, 4)))

        def ada_at(slots):
            return [n * slots // (2 * ADA_CHUNKS) for n in range(2 * ADA_CHUNKS)]

        ADA_FIRST = [6 + at for at in ada_at(16)]

        block = ctx.enter_context(nc.Block())

        @block.sync
        def _(sp):
            t = Tally(sp)

            def unit(*parts):
                slot = t.count(multiplied) // 2 % RAW_SLOTS
                sp.wait_ge(multiplied, t.nth(multiplied, 2))
                if t.i is not None:
                    sp.sem_inc(sp_waited, 1)
                for dst, src in parts:
                    sp.dma_start(dst(raw[:, slot, :]), src).then_inc(raw_landed[slot], LANDED // len(parts))

            def plain(w, row0, col0, kts=4, ncols=N):
                src = w[row0, col0] if kts else None
                half = kts * ncols // 2
                if half == CHUNK:
                    return unit((lambda r: r.rearrange("p (k n) -> p k n", n=ncols),
                                 src.rearrange("(k p) n -> p k n", p=P)))
                s = src.rearrange("(c k p) n -> c p k n", c=2, p=P)
                return unit(*[((lambda r, c=c: r[:, c * CHUNK:c * CHUNK + half].rearrange("p (k n) -> p k n", n=ncols)),
                               s[c]) for c in range(2)])

            def rows(k0, kts=4):
                return slice(k0 * P, (k0 + kts) * P)

            def wide(w, col0, k_tiles=KT, row0=0):
                for k in range(0, k_tiles, 4):
                    plain(w, rows(row0 + k), bass.ds(col0, N))

            sp.dma_start(vec_mix[0:KT, :], a["g_mix_pre"].rearrange("l (k p) -> (l k) p", p=P)).then_inc(first_landed, 16)
            sp.dma_start(ident[:], a["k_ident"]).then_inc(first_landed, 16)
            for n in range(4):
                at = slice(n * N, (n + 1) * N)
                sp.dma_start(h[:, :, at], a["x"][0][:, at].rearrange("(m p) d -> p m d", p=P)).then_inc(x_landed[n], 16)
                plain(w_in, rows(4 * n), slice(3 * MOBA_W, 3 * MOBA_W + N))

            with t.rounds(2, ATTENTION) as g:
                for at in (4 * MOBA_W, 0, MOBA_W, 5 * MOBA_W, 2 * MOBA_W):
                    wide(w_in, g * N + at)
                wide(w_in, g * (3 * MOBA_W - N) + (3 * MOBA_W + N))

            def mix(n):
                wide(w_br_moba, n * N, 8)
                wide(w_in, n * N + (6 * MOBA_W + D))
                wide(w_br_diff, n * N, 8)

            with t.rounds(3, MIX) as n:
                mix(n)
                wide(w_in, n * N + (6 * MOBA_W + N))
            mix(3)
            with t.rounds(2, WIDE) as n:
                for j in range(2):
                    wide(w_out, n * 2 * N + j * N)

            def up(col0):
                for j in range(2):
                    wide(w_up, col0 + j * N)

            def down(row0):
                for n in range(4):
                    for k in range(2):
                        plain(w_down, bass.ds(row0 + k * 4 * P, 4 * P), slice(n * N, (n + 1) * N))

            up(0)
            up(FF_BLOCK)
            with t.rounds(3, FEED) as i:
                for j in range(2):
                    down(i * 2 * FF_BLOCK + j * FF_BLOCK)
                    up(i * 2 * FF_BLOCK + (j + 2) * FF_BLOCK)
            down(6 * FF_BLOCK)
            down(7 * FF_BLOCK)
            for n in range(4):
                plain(w_ple_proj, slice(0, 2 * P), slice(n * N, (n + 1) * N), 2)
            with t.rounds(2, WIDE) as n:
                for j in range(2):
                    wide(w_ple_gate, n * 2 * N + j * N)

            def ret_qk_unit(head):
                for k in range(0, KT, 4):
                    unit(*[((lambda r, c=c: r.rearrange("p (k c n) -> p k c n", c=2, n=RET_DK)[:, :, c, :]),
                            ret_in[rows(k), bass.ds(head * RET_DK + c * D, RET_DK)].rearrange("(k p) n -> p k n", p=P))
                           for c in range(2)])

            def ret_out_units(head):
                for n in range(4):
                    plain(ret_out, bass.ds(head * RET_DV, RET_DV), slice(n * N, (n + 1) * N))

            def ret_vg(head):
                wide(ret_in, head * RET_DV + 2 * D)
                wide(ret_in, head * RET_DV + 4 * D)

            ret_qk_unit(0)
            ret_vg(0)
            with t.rounds(RET_HEADS - 1, RETAIN) as i:
                ret_qk_unit(i + 1)
                ret_out_units(i)
                ret_vg(i + 1)
            ret_out_units(RET_HEADS - 1)

            wide(mla_in, MLA_RANK)
            plain(mla_in, slice(0, D), slice(2 * MLA_RANK, 2 * MLA_RANK + MLA_ROPE), KT, MLA_ROPE)
            wide(mla_in, 0)
            with t.rounds(2, WIDE) as n:
                for j in range(2):
                    wide(mla_in, n * 2 * N + (2 * MLA_RANK + MLA_ROPE + j * N))

            def pair(p):
                plain(mla_uq, rows(0), bass.ds(p * MLA_QW, MLA_QW), 4, MLA_QW)
                plain(mla_ukv, rows(0), bass.ds(p * N, N))

            pair(0)
            pair(1)
            with t.rounds(3, LATENT) as i:
                pair(i * 2 + 2)
                pair(i * 2 + 3)
            wide(mla_out, 0, KT - 4)
            plain(mla_out, rows(0), slice(N, 2 * N))
            plain(mla_out, rows(KT - 4), slice(0, N))
            wide(mla_out, N, KT - 4, 4)
            for n in (2, 3):
                wide(mla_out, n * N)
            for m in range(TILES):
                for half in range(2):
                    at = slice(half * D // 2, (half + 1) * D // 2)
                    sp.wait_ge(out_ready, 2 * m + half + 1)
                    sp.dma_start(out[0, m * P:(m + 1) * P, at], acc[:, m, at]).then_inc(out_landed, 16)
            sp.wait_ge(out_landed, 16 * 2 * TILES)

        @block.tensor
        def _(pe):
            t = Tally(pe)
            XT, PT_X = (xT_hi, xT_lo), (pT_hi, pT_lo)
            YT = [(yT_hi[i], yT_lo[i]) for i in range(2)]

            pe.sem_inc(multiplied, RAW_CHUNKS)
            for b in range(2):
                pe.sem_inc(panel_taken[b], 1)
                pe.sem_inc(turn_taken[b], 1)
                pe.sem_inc(score_taken[b], 1)

            def open_panel(b):
                pe.wait_ge(panel_taken[b], t.nth(panel_taken[b]))

            def panel_closed(b):
                pe.wait_ge(panel_taken[b], t.now(panel_taken[b], 1))

            def turn_closed(b):
                pe.wait_ge(turn_taken[b], t.now(turn_taken[b], 1))

            def score_closed(b):
                pe.wait_ge(score_taken[b], t.now(score_taken[b], 1))

            def chunk(b, x, kt0, first, last, ncols=N, kts=2):
                x_hi, x_lo = x
                slot = t.count(lo_ready) % HI_CHUNKS
                pe.wait_ge(lo_ready, t.nth(lo_ready))
                for j in range(kts):
                    w_hi, w_lo = (w[:, slot, j * ncols:(j + 1) * ncols] for w in (hi, lo))
                    for m in range(TILES):
                        o, ms = panel[b][:, m, 0:ncols], slice(m * P, (m + 1) * P)
                        pe.matmul(o, x_hi[:, kt0 + j, ms], w_hi, start=first and j == 0, stop=False)
                        pe.matmul(o, x_hi[:, kt0 + j, ms], w_lo, start=False, stop=False)
                        done = pe.matmul(o, x_lo[:, kt0 + j, ms], w_hi, start=False, stop=last and j == kts - 1)
                done.then_inc(multiplied, 1)
                t.nth(multiplied)

            def wide_chunk(s, b, x, chunks=8, k0=0):
                if s == 0 and b < 2:
                    open_panel(b)
                elif s == 0:
                    turn_closed(0)
                    turn_closed(1)
                chunk(b, x, k0 + 2 * s, s == 0, s == chunks - 1)

            def turn_batch(b, *pieces):
                pe.wait_ge(turn_taken[b], t.nth(turn_taken[b]))
                if pieces[0][0].shape[1] < P and t.i is not None:
                    pe.sem_inc(pe_waited, 1)
                for src, at in pieces:
                    rows, n = src.shape
                    done = pe.transpose(turn[b][0:n, at:at + rows], src, ident[0:rows, 0:rows])
                done.then_inc(turned[b], 1)
                t.nth(turned[b])

            def turn_tokens(b, src):
                turn_batch(b, *[(src(m)[:, k * P:(k + 1) * P], k * TOKENS + m * P) for k in range(2) for m in range(TILES)])

            def turn_x(c, src):
                turn_tokens(c % 2, lambda m: src[:, m, c * 2 * P:(c + 1) * 2 * P])

            def turn_mixed(c):
                if c % 2 == 0:
                    pe.wait_ge(mixed_ready, t.nth(mixed_ready))
                turn_x(c, acc)

            def turn_h(c):
                if c % 2 == 0:
                    pe.wait_ge(h_ready, t.nth(h_ready))
                turn_x(c, h)

            def turn_xs(c):
                if c % 2 == 0:
                    pe.wait_ge(xs_ready, t.nth(xs_ready))
                turn_x(c, acc)

            def turn_probs(b, src):
                turn_batch(b, *[(src[:, n * P:(n + 1) * P], n * P) for n in range(3)])

            def open_score(b):
                pe.wait_ge(score_taken[b], t.nth(score_taken[b]))

            def scores_of(b, parts):
                open_score(b)
                for at, n, q in ((0, P, slice(0, P)), (P, 2 * P, slice(P, 2 * P))):
                    for i, (qT, kT) in enumerate(parts):
                        done = pe.matmul(score[b][:, at:at + n], qT[:, q], kT[:, 0:n], start=i == 0,
                                         stop=i == len(parts) - 1)
                done.then_inc(scored[b], 1)
                t.nth(scored[b])

            def weighted(out0, out1, pT3, v0, v1):
                pe.matmul(out0, pT3[:, 0:P], v0, start=True, stop=True)
                pe.matmul(out1, pT3[:, P:2 * P], v0, start=True, stop=False)
                return pe.matmul(out1, pT3[:, 2 * P:3 * P], v1, start=False, stop=True)

            def turned_panel(s, b, turn_piece):
                if s < 6:
                    turn_piece(s + 2)
                else:
                    turn_closed(s % 2)
                wide_chunk(s, b, XT)

            def four_panels(turn_piece):
                for s in range(32):
                    if s < 8:
                        turned_panel(s, 0, turn_piece)
                    else:
                        wide_chunk(s % 8, s // 8 % 2, XT)

            def turn_input(c):
                if c % 2 == 0:
                    pe.wait_ge(x_landed[c // 2], 16)
                turn_x(c, h)

            pe.wait_ge(first_landed, 16 * 2)
            open_score(0)
            pe.transpose(score[0][:, 0:KT], vec_mix[0:KT, :], ident[0:KT, 0:KT]).then_inc(scored[0], 1)
            t.nth(scored[0])
            turn_input(0)
            turn_input(1)

            def turn_heads(j):
                turn_batch(j % 2, *[(qk[:, m, (4 * c + j) * HEAD:(4 * c + j + 1) * HEAD], (2 * c + m) * P)
                                    for c in range(2) for m in range(TILES)])

            def head_scores(j):
                scores_of(j % 2, [(qkT[:, j, 0:2 * P], qkT[:, j, 2 * P:4 * P])])

            for s in range(8):
                turned_panel(s, 0, turn_input)
            pe.wait_ge(vec_landed, 16 * N_VECTORS)
            open_score(1)
            pe.transpose(score[1][:, KT:VEC_ROWS], vec[0:VEC_ROWS - KT, :], ident[0:VEC_ROWS - KT, 0:VEC_ROWS - KT])
            pe.transpose(score[1][:, COL_GN:COLS], vec_gn[0:COLS - COL_GN, :],
                         ident[0:COLS - COL_GN, 0:COLS - COL_GN]).then_inc(scored[1], 1)
            t.nth(scored[1])
            with t.rounds(2, ATTENTION) as g:
                for s in range(48):
                    if s in (10, 26):
                        pe.wait_ge(roped, t.nth(roped))
                        turn_heads(0)
                        turn_heads(1)
                    if s in (11, 27):
                        turn_heads(2)
                        turn_heads(3)
                    if s in (13, 29):
                        head_scores(0)
                        head_scores(1)
                    if s in (14, 30):
                        turn_closed(0)
                        turn_closed(1)
                        head_scores(2)
                        head_scores(3)
                    if s == 20:
                        pe.wait_ge(probs_ready, t.nth(probs_ready))
                        for hh in range(2):
                            turn_probs(hh, pr[:, 2 * hh, :])
                    if s == 34:
                        panel_closed(0)
                        turn_closed(0)
                        turn_closed(1)
                        for hh in range(2):
                            open_score(hh)
                            vs = [v_sb[:, m, hh * DIFF_V:(hh + 1) * DIFF_V] for m in range(TILES)]
                            weighted(score[hh][:, 0:DIFF_V], score[hh][:, DIFF_V:2 * DIFF_V], pT[:, hh, :],
                                     *vs).then_inc(scored[hh], 1)
                            t.nth(scored[hh])
                    if s in (35, 36):
                        pe.wait_ge(probs_ready, t.nth(probs_ready))
                        for j in range(2):
                            turn_probs(j, pr[:, 2 * (s - 35) + j, :])
                    if s == 39:
                        score_closed(0)
                        score_closed(1)
                        for hh in range(2):
                            turn_tokens(hh, lambda m: ob[:, m, hh, :])
                    if s == 42:
                        panel_closed(1)
                        for b in range(2):
                            open_score(b)
                            for j in (2 * b, 2 * b + 1):
                                at = (j % 2) * TOKENS
                                o = [score[b][:, at + m * P:at + (m + 1) * P] for m in range(TILES)]
                                v0, v1 = (v_sb[:, m, j * HEAD:(j + 1) * HEAD] for m in range(TILES))
                                pe.matmul(o[0], v0, pT[:, j, 0:P], start=True, stop=True)
                                pe.matmul(o[1], v0, pT[:, j, P:2 * P], start=True, stop=False)
                                done = pe.matmul(o[1], v1, pT[:, j, 2 * P:3 * P], start=False, stop=True)
                            done.then_inc(scored[b], 1)
                            t.nth(scored[b])
                    wide_chunk(s % 8, (1 + s // 8) % 2, XT)

            def mix_chunk(s):
                if s < 4:
                    if s == 0:
                        score_closed(0)
                        score_closed(1)
                    wide_chunk(s, 1, YT[0], 4)
                elif s < 12:
                    wide_chunk(s - 4, 0, XT)
                elif s < 16:
                    if s == 12:
                        turn_closed(0)
                        turn_closed(1)
                    wide_chunk(s - 12, 1, YT[1], 4)
                else:
                    wide_chunk(s - 16, 0, XT)

            with t.rounds(3, MIX) as n:
                for s in range(24):
                    mix_chunk(s)
            for s in range(16):
                if s >= 14:
                    turn_mixed(s - 14)
                mix_chunk(s)

            for s in range(32):
                if s < 8:
                    turned_panel(s, 0, turn_mixed)
                else:
                    wide_chunk(s % 8, s // 8 % 2, XT)

            def up_turns(b):
                panel_closed(b)
                for j in range(2):
                    turn_tokens(j, lambda m: relu[:, m, j * 2 * P:(j + 1) * 2 * P])

            def down_chunk(s, k):
                wide_chunk(s % 4, s // 4 % 2, YT[k], 4)

            pe.wait_ge(late_landed, 16 * (N_EARLY + N_LATE))
            open_score(1)
            for k in range(2):
                for m in range(TILES):
                    done = pe.transpose(score[1][:, k * TOKENS + m * P:k * TOKENS + (m + 1) * P],
                                        p_in[:, m, k * P:(k + 1) * P], ident[:])
            done.then_inc(scored[1], 1)
            t.nth(scored[1])
            turn_h(0)
            turn_h(1)
            for s in range(32):
                if s in (10, 18, 26):
                    up_turns(s // 8 % 2 ^ 1)
                if s < 8:
                    turned_panel(s, 0, turn_h)
                else:
                    wide_chunk(s % 8, s // 8 % 2, XT)
            with t.rounds(3, FEED) as i:
                for s in range(64):
                    if s in (2, 34):
                        up_turns(1)
                    if s in (26, 58):
                        up_turns(0)
                    if s % 32 < 16:
                        down_chunk(s, s // 32)
                    else:
                        wide_chunk(s % 8, s // 8 % 2, XT)
            for s in range(32):
                if s == 2:
                    up_turns(1)
                down_chunk(s, s // 16)

            for s in range(8):
                if s >= 6:
                    turn_h(s - 6)
                if s % 2 == 0:
                    open_panel(s // 2 % 2)
                chunk(s // 2 % 2, PT_X, s % 2, s % 2 == 0, s % 2 == 1, N, 1)
            four_panels(turn_h)

            def mod_sums(layer, parts):
                open_score(0)
                pe.wait_ge(ada_taken, ADA_SLOTS + ADA_STEPS * (layer + 1))
                for n in range(parts * KT):
                    done = pe.matmul(score[0][:, n:n + 1], ada_acc[:, n * P:(n + 1) * P], ones[:, 0:1], start=True, stop=True)
                done.then_inc(scored[0], 1)
                t.nth(scored[0])

            def gate_row(n, layer):
                open_score(n % 2)
                if layer == 0:
                    for k in range(4):
                        gate = mods[:, 2, 4 * n + k:4 * n + k + 1].broadcast_to([P, P])
                        done = pe.matmul(score[n % 2][:, k * P:(k + 1) * P], gate, ident[:], start=True, stop=True)
                else:
                    done = pe.matmul(score[n % 2], ones[:], ada_acc[:, 2 * D + n * N:2 * D + (n + 1) * N], start=True, stop=True)
                done.then_inc(scored[n % 2], 1)
                t.nth(scored[n % 2])

            mod_sums(0, 3)

            def ret_y_turns():
                pe.wait_ge(yg_ready, t.nth(yg_ready))
                for j in range(2):
                    turn_tokens(j, lambda m: ret_sg[:, m, j * 2 * P:(j + 1) * 2 * P])

            def ret_out_chunk(s):
                if s == 0:
                    turn_closed(0)
                    turn_closed(1)
                wide_chunk(s % 2, (1 + s // 2) % 2, YT[0], 2)

            def ret_qk_turns():
                pe.wait_ge(roped, t.nth(roped))
                for c in range(2):
                    turn_tokens(c, lambda m: ret_qk[:, m, c * RET_DK:(c + 1) * RET_DK])

            def ret_scores():
                turn_closed(0)
                turn_closed(1)
                open_score(0)
                for at, n, k0, q0 in ((0, 2 * P, 0, 0), (2 * P, P, P, P)):
                    for d in range(2):
                        done = pe.matmul(score[0][:, at:at + n], ret_qkT[:, 1, d, k0:k0 + P], ret_qkT[:, 0, d, q0:q0 + n],
                                         start=d == 0, stop=d == 1)
                done.then_inc(scored[0], 1)
                t.nth(scored[0])

            def ret_y():
                score_closed(0)
                panel_closed(1)
                open_score(0)
                pe.matmul(score[0], ret_sT[:, 0:P], ret_v[:, 0, :], start=True, stop=True).then_inc(scored[0], 1)
                t.nth(scored[0])
                open_score(1)
                pe.matmul(score[1], ret_sT[:, P:2 * P], ret_v[:, 0, :], start=True, stop=False)
                pe.matmul(score[1], ret_sT[:, 2 * P:3 * P], ret_v[:, 1, :], start=False, stop=True).then_inc(scored[1], 1)
                t.nth(scored[1])

            turn_xs(0)
            turn_xs(1)
            for s in range(24):
                if s == 11:
                    ret_qk_turns()
                if s == 14:
                    ret_scores()
                if s == 18:
                    ret_y()
                if s < 8:
                    turned_panel(s, 0, turn_xs)
                else:
                    wide_chunk(s % 8, s // 8, XT)
            with t.rounds(RET_HEADS - 1, RETAIN) as i:
                for s in range(32):
                    if s == 2:
                        ret_y_turns()
                    if s == 11:
                        ret_qk_turns()
                    if s == 14:
                        ret_scores()
                    if s == 26:
                        ret_y()
                    if s < 8:
                        wide_chunk(s, 0, XT)
                    elif s < 16:
                        ret_out_chunk(s - 8)
                    elif s < 24:
                        wide_chunk(s - 16, 1, XT)
                    else:
                        wide_chunk(s - 24, 2, XT)
            gate_row(2, 0)
            gate_row(3, 0)
            ret_y_turns()
            gate_row(0, 0)
            gate_row(1, 0)
            for s in range(8):
                ret_out_chunk(s)

            mod_sums(1, 2)
            turn_xs(0)
            turn_xs(1)
            def kr_chunk(s):
                if s == 0:
                    open_panel(1)
                slot = t.count(lo_ready) % HI_CHUNKS
                pe.wait_ge(lo_ready, t.nth(lo_ready))
                o = panel[1][0:MLA_ROPE, 0, 0:TOKENS]
                for j in range(8):
                    w_hi, w_lo = (w[:, slot, j * MLA_ROPE:(j + 1) * MLA_ROPE] for w in (hi, lo))
                    k = 8 * s + j
                    pe.matmul(o, w_hi, xT_hi[:, k, :], start=k == 0, stop=False)
                    pe.matmul(o, w_hi, xT_lo[:, k, :], start=False, stop=False)
                    done = pe.matmul(o, w_lo, xT_hi[:, k, :], start=False, stop=k == KT - 1)
                done.then_inc(multiplied, 1)
                t.nth(multiplied)

            for s in range(18):
                if s == 11:
                    panel_closed(1)
                    turn_batch(0, *[(krF[:, m * P:(m + 1) * P], m * MLA_ROPE) for m in range(TILES)])
                if s == 13:
                    for j in range(2):
                        turn_tokens(j, lambda m: lat[:, m, j * 2 * P:(j + 1) * 2 * P])
                if s == 10:
                    gate_row(0, 1)
                    gate_row(1, 1)
                if s == 16:
                    pe.wait_ge(roped, t.nth(roped))
                    turn_batch(0, *[(kr[:, m, :], m * P) for m in range(TILES)])
                if s < 8:
                    turned_panel(s, 0, turn_xs)
                elif s < 10:
                    kr_chunk(s - 8)
                else:
                    wide_chunk(s - 10, 0, XT)
            with t.rounds(2, WIDE) as n:
                for s in range(16):
                    wide_chunk(s % 8, (1 + s // 8) % 2, XT)
            for j in range(2):
                turn_tokens(j, lambda m: lat[:, m, j * 2 * P:(j + 1) * 2 * P])
            gate_row(2, 1)
            gate_row(3, 1)
            turn_closed(0)
            turn_closed(1)

            def pair_chunk(s):
                if s < 2:
                    if s == 0:
                        open_panel(0)
                    chunk(0, YT[0], 2 * s, s == 0, s == 1, MLA_QW)
                else:
                    wide_chunk(s - 2, 1, (yT_hi[0][:, 4:8, :], yT_lo[0][:, 4:8, :]), 2)

            def pair_step(s, q, r):
                if s == 1 and q is not None:
                    pe.wait_ge(roped, t.nth(roped))
                    panel_closed(1)
                    for hh in range(2):
                        k0 = hh * 2 * MLA_NOPE
                        q0 = hh * (MLA_NOPE + MLA_ROPE)
                        turn_batch(hh, *[(q_sb[q][:, m, q0:q0 + MLA_NOPE], m * P) for m in range(TILES)],
                                   *[(kv_sb[q][:, m, k0:k0 + MLA_NOPE], (2 + m) * P) for m in range(TILES)])
                if s == 2 and r is not None:
                    pe.wait_ge(pair_exps_ready, t.nth(pair_exps_ready))
                    for hh in range(2):
                        turn_probs(hh, m_exps[:, hh, :])
                if s == 3:
                    if r is not None:
                        turn_closed(0)
                        turn_closed(1)
                    if q is not None:
                        q1 = MLA_NOPE
                        turn_batch(0, *[(q_sb[q][:, m, hh * (MLA_NOPE + MLA_ROPE) + q1:(hh + 1) * (MLA_NOPE + MLA_ROPE)],
                                         hh * TOKENS + m * P) for hh in range(2) for m in range(TILES)])
                    if r is not None:
                        open_score(0)
                        for hh in range(2):
                            vs = [kv_sb[r][:, m, (2 * hh + 1) * P:(2 * hh + 2) * P] for m in range(TILES)]
                            done = weighted(score[0][:, hh * P:(hh + 1) * P], score[0][:, (2 + hh) * P:(3 + hh) * P],
                                            m_pT[:, hh, :], *vs)
                        done.then_inc(scored[0], 1)
                        t.nth(scored[0])
                if s == 4:
                    if q is not None:
                        turn_closed(0)
                        turn_closed(1)
                        scores_of(1, [(nT[:, 0, 0:2 * P], nT[:, 0, 2 * P:4 * P]), (rT[:, 0, :], krT)])
                    if r is not None:
                        score_closed(0)
                        turn_batch(1, *[(og[:, m, hh * P:(hh + 1) * P], hh * TOKENS + m * P)
                                        for hh in range(2) for m in range(TILES)])
                    if q is not None:
                        scores_of(0, [(nT[:, 1, 0:2 * P], nT[:, 1, 2 * P:4 * P]), (rT[:, 1, :], krT)])

            for p in range(2):
                for s in range(5):
                    pair_step(s, 0 if p else None, None)
                    if s < 4:
                        pair_chunk(s)
            with t.rounds(3, LATENT) as i:
                for p in range(2):
                    for s in range(5):
                        pair_step(s, 1 - p, p)
                        if s < 4:
                            pair_chunk(s)
            for s in range(5):
                pair_step(s, 1, 0)
                if s < 4:
                    wide_chunk(s, 0, XT)
            for s in range(5):
                pair_step(s, None, 1)
                if s < 2:
                    wide_chunk(4 + s, 0, XT)
                elif s < 4:
                    wide_chunk(s - 2, 1, XT)
            wide_chunk(6, 0, XT)
            turn_closed(1)
            wide_chunk(7, 0, XT)
            for s in range(10, 32):
                wide_chunk(s % 8, s // 8 % 2, XT)

        @block.scalar
        def _(act):
            t = Tally(act)
            copy = ACT.Copy

            def split_hi(words=CHUNK):
                k = t.count(hi_ready)
                slot = k // 2 % RAW_SLOTS
                if k % 2 == 0:
                    act.wait_ge(raw_landed[slot], t.nth(raw_landed[slot], LANDED))
                act.wait_ge(multiplied, t.nth(multiplied) + RAW_CHUNKS - HI_CHUNKS)
                act.activation(hi[:, k % HI_CHUNKS, 0:words], raw[:, slot, k % 2 * CHUNK:k % 2 * CHUNK + words],
                               copy).then_inc(hi_ready, 1)
                t.nth(hi_ready)

            def chunks_done():
                act.wait_ge(multiplied, t.now(multiplied, RAW_CHUNKS - AHEAD))

            def wait_turned(b):
                act.wait_ge(turned[b], t.nth(turned[b]))

            def squares(junk, src):
                for m in range(TILES):
                    done = act.activation(junk(m), src(m), ACT.Square, accum_out=st_sum[:, m:m + 1])
                done.then_inc(sums_ready, 1)

            def square_part(n, junk, src):
                for m in range(TILES):
                    done = act.activation(junk(m), src(m), ACT.Square, accum_out=st_parts[:, m, n:n + 1])
                done.then_inc(squares_done, 1)

            def h_squares(n):
                act.wait_ge(h_ready, t.nth(h_ready))
                at = slice(n * N, (n + 1) * N)
                square_part(n, lambda m: acc[:, m, at], lambda m: h[:, m, at])

            def wait_rstd():
                act.wait_ge(rstd_ready, t.nth(rstd_ready))

            def each_tile(dst, b, func):
                for m in range(TILES):
                    done = act.activation(dst[:, m, :], panel[b][:, m, :], func, scale=st_rstd[:, m:m + 1])
                return done

            def two(bank):
                return bank.rearrange("p (k t) -> p k t", t=TOKENS)

            def hi_plain(c, dst, kt):
                wait_turned(c % 2)
                act.activation(dst[:, kt, :], two(turn[c % 2]), copy).then_inc(turn_hi, 1)

            def hi_scaled(b, dst, kt, gains, shifts=None):
                wait_turned(b)
                for k in range(2):
                    src = turn[b][:, k * TOKENS:(k + 1) * TOKENS]
                    if shifts:
                        done = act.activation(dst[:, kt + k, :], src, ACT.Identity, scale=gains(k), bias=shifts(k))
                    else:
                        done = act.activation(dst(k) if callable(dst) else dst[:, kt + k, :], src, copy, scale=gains(k))
                done.then_inc(turn_hi, 1)

            def hi_norm(c, col):
                hi_scaled(c % 2, xT_hi, 2 * c, lambda k: cols[:, col + 2 * c + k:col + 2 * c + k + 1])

            def hi_mod(c):
                hi_scaled(c % 2, xT_hi, 2 * c, lambda k: mods[:, 1, 2 * c + k:2 * c + k + 1],
                          lambda k: mods[:, 0, 2 * c + k:2 * c + k + 1])

            def copy_turned(b, dst, src=None):
                wait_turned(b)
                act.activation(dst, turn[b] if src is None else src, copy).then_inc(turn_taken[b], 1)

            def load_row(name):
                act.dma_start(row[:], a[name].partition_broadcast(P)).then_inc(row_landed, 16)

            def ada_load(layer, kt, c):
                slot = t.count(ada_taken) % ADA_SLOTS
                act.wait_ge(ada_taken, t.nth(ada_taken))
                act.dma_start(ada_ring[:, slot, :], ada_w[layer][kt, c * ADA_CHUNK:(c + 1) * ADA_CHUNK]).then_inc(ada_landed[slot], ADA_LANDED)

            def ada_loads(s, at, layer, k0):
                for n in range(2 * ADA_CHUNKS):
                    if at[n] == s:
                        ada_load(layer, k0(n // ADA_CHUNKS), n % ADA_CHUNKS)

            def exps(sm, pr, heads, ready):
                act.wait_ge(max_ready, t.nth(max_ready))
                for j in heads:
                    act.activation(pr[:, j, 0:P], sm[:, j, 0:P], ACT.Exp, bias=st_neg[:, j, 0:1], accum_out=st_den[:, j, 0:1])
                    done = act.activation(pr[:, j, P:3 * P], sm[:, j, P:3 * P], ACT.Exp, bias=st_neg[:, j, 1:2],
                                          accum_out=st_den[:, j, 1:2])
                done.then_inc(ready, 1)

            def late(dst, src):
                act.dma_start(dst, src).then_inc(late_landed, 16)

            act.wait_ge(ones_set, 1)
            act.activation(stats[:, 2:3], ones[:, 0:1], copy)
            for at, name, n in ((COL_MLP, "g_mlp_pre", KT), (COL_PLE, "g_ple_pre", KT), (COL_NORM, "norm_g_2", 2 * KT),
                                (COL_C, "c_2", KT), (COL_Q, "mla_q_norm_g_2", 4), (COL_KV, "mla_kv_norm_g_2", 4),
                                (COL_SUB, "diff_subln_g", 2)):
                act.dma_start(vec[at - KT:at - KT + n, :], a[name].rearrange("l (k p) -> (l k) p", p=P)).then_inc(vec_landed, 16)
            act.dma_start(vec_gn[0:COLS - COL_GN, :], a["ret_gn_g_2"].rearrange("l (k p) -> (l k) p", p=P)).then_inc(vec_landed, 16)
            for b in range(2):
                t.nth(scored[b])
            act.wait_ge(score_taken[0], 1 + 1)
            hi_norm(0, COL_MIX)
            hi_norm(1, COL_MIX)
            for _ in range(AHEAD):
                split_hi()
            for s in range(8):
                if s < 6:
                    hi_norm(s + 2, COL_MIX)
                if s == 4:
                    for landed in x_landed:
                        act.wait_ge(landed, 16)
                    late(mask[:], a["k_mask"])
                    late(rope1[:], a["k_rope1"])
                    for n, name in enumerate(("lambda_q1", "lambda_k1", "lambda_q2", "lambda_k2")):
                        late(lambdas[:, n // 2, n % 2, :], a[name][0].partition_broadcast(P))
                    load_row("g_mix_post")
                if s == 5:
                    squares(lambda m: x_squares[:, m, :], lambda m: h[:, m, :])
                split_hi()
            t.nth(rstd_ready)
            act.wait_ge(lam_sums, 1)
            act.activation(st_lam, st_lam, ACT.Exp).then_inc(lam_exps, 1)

            with t.rounds(2, ATTENTION) as g:
                for s in range(48):
                    if s in (11, 12, 27, 28):
                        first = 0 if s in (11, 27) else 2
                        for j in (first, first + 1):
                            copy_turned(j % 2, qkT[:, j, :])
                    if s in (15, 16, 31, 32):
                        first = 0 if s in (15, 31) else 2
                        for b in range(2):
                            t.nth(scored[b])
                        exps(sm, pr, (first, first + 1), exp_ready)
                    if s == 21:
                        for hh in range(2):
                            copy_turned(hh, pT[:, hh, :], turn[hh][:, 0:3 * P])
                    if s == 35:
                        for hh in range(2):
                            act.wait_ge(scored[hh], t.nth(scored[hh]))
                            for m in range(TILES):
                                done = act.activation(ob_squares[:, hh, m, :], score[hh][:, m * DIFF_V:(m + 1) * DIFF_V], ACT.Square,
                                                      scale=DIFF_V ** -0.5, accum_out=st_dsum[:, hh, m:m + 1])
                        done.then_inc(sums_ready, 1)
                        t.nth(rstd_ready)
                    if s in (36, 37):
                        for j in range(2):
                            copy_turned(j, pT[:, 2 * (s - 36) + j, :], turn[j][:, 0:3 * P])
                    if s == 40:
                        for hh in range(2):
                            hi_scaled(hh, lambda k: yT_hi[1][:, bass.ds(g * 4 + (hh * 2 + k), 1), :].rearrange("p a t -> p (a t)"), 0,
                                      lambda k: cols[:, COL_SUB + k:COL_SUB + k + 1])
                    if s == 43:
                        for b in range(2):
                            act.wait_ge(scored[b], t.nth(scored[b]))
                            act.activation(yT_hi[0][:, bass.ds(g * 4 + 2 * b, 2), :], two(score[b]), copy).then_inc(turn_hi, 1)
                    split_hi()

            def sigmoid(b, dst):
                chunks_done()
                each_tile(dst, b, ACT.Sigmoid).then_inc(panel_taken[b], 1)
                t.nth(panel_taken[b])

            for b in range(2):
                t.nth(panel_taken[b], 1 + 3 * 2)
            def mix_step(s):
                if s == 0:
                    act.wait_ge(panel_taken[1], t.now(panel_taken[1]))
                    sigmoid(0, sig[0])
                if s in (4, 16):
                    t.nth(panel_taken[1])
                if s == 12:
                    act.wait_ge(panel_taken[1], t.now(panel_taken[1]))
                    sigmoid(0, sig[1])

            def hi_mixed(c):
                hi_plain(c, xT_hi, slice(2 * c, 2 * c + 2))

            with t.rounds(3, MIX) as n:
                for s in range(24):
                    mix_step(s)
                    split_hi()
            for s in range(17):
                mix_step(s)
                if s >= 15:
                    hi_mixed(s - 15)
                if s < 16:
                    split_hi()

            late(freq, a["k_freq"].partition_broadcast(P))
            for m in range(TILES):
                late(st_ipos[:, m:m + 1], a["positions_2"][0, m * P:(m + 1) * P].rearrange("(p o) -> p o", o=1))
            late(p_in, a["p"][0, 0].rearrange("(m p) d -> p m d", p=P))

            def ada_bias(layer):
                act.wait_ge(ada_set, layer + 1)
                act.dma_start(ada_acc[0:1, :], a["ada_b_2"][layer:layer + 1, :]).then_inc(ada_row, 16)

            for s in range(33):
                if s < 6:
                    hi_mixed(s + 2)
                if s == 20:
                    ada_bias(0)
                    act.activation(c_act[:], cols[:, COL_C:COL_C + KT], ACT.Silu).then_inc(c_ready, 1)
                if s in (8, 16, 24, 32):
                    n = s // 8 - 1
                    chunks_done()
                    square_part(n, lambda m: turn[m], lambda m: panel[n % 2][:, m, :])
                    t.nth(panel_taken[n % 2])
                if s < 32:
                    split_hi()
            t.nth(rstd_ready)
            act.wait_ge(scored[1], t.nth(scored[1]))
            act.activation(pT_hi[:], two(score[1]), copy).then_inc(turn_hi, 1)

            def up_panel(b):
                chunks_done()
                each_tile(relu, b, ACT.Relu).then_inc(act_step, 1)
                act.wait_ge(act_step, t.nth(act_step))
                act.activation(relu, relu, ACT.Square).then_inc(panel_taken[b], 1)
                t.nth(panel_taken[b])

            def up_hi(b, k):
                for j in range(2):
                    hi_plain(j, yT_hi[k], slice(b * 4 + 2 * j, b * 4 + 2 * j + 2))

            def by_dve(s):
                if s in (4, 8, 12, 16):
                    t.nth(panel_taken[s // 4 % 2 ^ 1])

            hi_norm(0, COL_MLP)
            hi_norm(1, COL_MLP)
            for s in range(32):
                if s < 6:
                    hi_norm(s + 2, COL_MLP)
                if s < 4:
                    h_squares(s)
                if s == 4:
                    load_row("g_mlp_post")
                ada_loads(s, ada_at(32), 0, lambda k: slice(k * P, (k + 1) * P))
                if s == 8:
                    wait_rstd()
                if s in (8, 16, 24):
                    up_panel(s // 8 % 2 ^ 1)
                if s in (11, 19, 27):
                    up_hi(s // 8 % 2 ^ 1, s // 20)
                if s == 13:
                    act.wait_ge(angles_ready, 1)
                    act.activation(trig[:], trig[:], ACT.Sin).then_inc(trig_ready, 1)
                split_hi()
            with t.rounds(3, FEED) as i:
                for s in range(64):
                    ada_loads(s % 32, ada_at(32), 0, lambda k: bass.ds(i * 4 * P + (2 + s // 32 * 2 + k) * P, P))
                    if s in (0, 32):
                        up_panel(1)
                    if s in (24, 56):
                        up_panel(0)
                    if s in (3, 27, 35, 59):
                        up_hi(1 if s in (3, 35) else 0, 1 if s in (3, 59) else 0)
                    by_dve(s % 32)
                    split_hi()
            for s in range(32):
                ada_loads(s, ada_at(32), 0, lambda k: slice((14 + k) * P, (15 + k) * P))
                if s == 0:
                    up_panel(1)
                if s == 3:
                    up_hi(1, 1)
                by_dve(s if s <= 16 else s - 16)
                if s in (20, 24, 28):
                    n = s // 4 - 5
                    act.wait_ge(panel_taken[n % 2], t.now(panel_taken[n % 2]))
                    square_part(n, lambda m: relu[:, m, :], lambda m: acc[:, m, n * N:(n + 1) * N])
                split_hi(CHUNK if s + AHEAD < 32 else N)
            split_hi(N)
            by_dve(16)
            act.wait_ge(panel_taken[1], t.now(panel_taken[1]))
            square_part(3, lambda m: relu[:, m, :], lambda m: acc[:, m, 3 * N:4 * N])
            t.nth(rstd_ready)

            def e_copy(n):
                chunks_done()
                act.activation(e_sb[:, :, n * N:(n + 1) * N], panel[n % 2], copy).then_inc(panel_taken[n % 2], 1)
                t.nth(panel_taken[n % 2])

            act.wait_ge(ada_taken, ADA_SLOTS + ADA_STEPS)
            act.wait_ge(squares_done, 2 * 4 + 4)
            for s in range(8):
                if s in (2, 4, 6):
                    e_copy(s // 2 - 1)
                if s >= 6:
                    hi_norm(s - 6, COL_PLE)
                if s:
                    split_hi(N if s + AHEAD < 8 else CHUNK)
            for s in range(33):
                if s == 0:
                    e_copy(3)
                if s < 6:
                    hi_norm(s + 2, COL_PLE)
                if s < 4:
                    h_squares(s)
                if s == 4:
                    load_row("g_ple_post")
                if s == 8:
                    wait_rstd()
                if s in (8, 16, 24, 32):
                    n = s // 8 - 1
                    at = slice(n * N, (n + 1) * N)
                    sigmoid(n % 2, acc[:, :, at])
                    act.wait_ge(ple_ready, t.nth(ple_ready))
                    square_part(n, lambda m: turn[m], lambda m: acc[:, m, at])
                if s < 32:
                    split_hi()

            for n in range(4):
                h_squares(n)
            act.wait_ge(mods_ready, 1)

            def load_decay(head):
                act.dma_start(ret_dm, a["k_decay"][head].rearrange("h p n -> p (h n)")).then_inc(dm_landed, 16)

            def ret_y_hi(head):
                for j in range(2):
                    hi_scaled(j, yT_hi[0], 2 * j, lambda k: cols[:, bass.ds(head * 4 + (COL_GN + 2 * j + k), 1)])

            def ret_copies():
                for c in range(2):
                    copy_turned(c, ret_qkT[:, c, :, :], turn[c].rearrange("p (d t) -> p d t", t=TOKENS))

            def ret_gate():
                chunks_done()
                act.activation(ret_sg, panel[2], ACT.Silu).then_inc(silu_ready, 1)

            load_decay(slice(0, 1))
            hi_mod(0)
            hi_mod(1)
            for s in range(24):
                if s < 6:
                    hi_mod(s + 2)
                if s == 5:
                    ada_bias(1)
                ada_loads(s, ADA_FIRST, 1, lambda k: slice(k * P, (k + 1) * P))
                if s == 8:
                    t.nth(panel_taken[0])
                if s == 12:
                    ret_copies()
                if s == 16:
                    t.nth(panel_taken[1])
                split_hi()
            ret_gate()
            with t.rounds(RET_HEADS - 1, RETAIN) as i:
                for s in range(32):
                    ada_loads(s, ada_at(32), 1, lambda k: bass.ds(i * 2 * P + (2 + k) * P, P))
                    if s == 3:
                        ret_y_hi(i)
                        load_decay(bass.ds(i + 1, 1))
                    if s == 8:
                        t.nth(panel_taken[0])
                    if s == 12:
                        ret_copies()
                    if s in (10, 14, 24):
                        t.nth(panel_taken[1])
                    if s in (12, 16):
                        t.nth(panel_taken[0])
                    split_hi()
                ret_gate()
            for j in range(2):
                kt = (RET_HEADS - 1) * 4 + 2 * j
                hi_scaled(j, yT_hi[0], 2 * j, lambda k: cols[:, COL_GN + kt + k:COL_GN + kt + k + 1])
            for s in range(8):
                split_hi()
                if s in (3, 5, 7):
                    h_squares(s // 2 - 1)

            h_squares(3)
            act.wait_ge(mods_ready, 2)
            for b in range(2):
                t.nth(panel_taken[b], 2)

            def lat_sums():
                chunks_done()
                squares(lambda m: lat_squares[m], lambda m: panel[0][:, m, :])

            def lat_hi(kt, col):
                for j in range(2):
                    hi_scaled(j, yT_hi[0], kt + 2 * j, lambda k: cols[:, col + 2 * j + k:col + 2 * j + k + 1])

            hi_mod(0)
            hi_mod(1)
            for s in range(18):
                if s < 6:
                    hi_mod(s + 2)
                if s == 8:
                    lat_sums()
                if s == 14:
                    lat_hi(4, COL_KV)
                if s == 10:
                    chunks_done()
                    act.activation(krF, panel[1][0:MLA_ROPE, 0, 0:TOKENS], copy).then_inc(panel_taken[1], 1)
                    t.nth(panel_taken[1])
                if s == 12:
                    copy_turned(0, kr_in, turn[0][:, 0:TILES * MLA_ROPE].rearrange("p (m d) -> p m d", m=TILES))
                if s == 17:
                    copy_turned(0, krT, turn[0][0:MLA_ROPE, 0:TOKENS])
                split_hi(N if s + AHEAD in (8, 9) else CHUNK)
            lat_sums()
            with t.rounds(2, WIDE) as n:
                for s in range(17):
                    if s in (8, 16):
                        j = s // 16
                        chunks_done()
                        act.activation(sgm[:, :, bass.ds(n * 2 * N + j * N, N)], panel[1 - j], ACT.Silu).then_inc(panel_taken[1 - j], 1)
                        t.nth(panel_taken[1 - j])
                    if s < 16:
                        split_hi()
            lat_hi(0, COL_Q)

            def pair_step(s, q, r, kt=None):
                if s == 1 and r is not None:
                    exps(m_sm, m_exps, range(2), pair_exps_ready)
                if s == 1 and q is not None:
                    for hh in range(2):
                        copy_turned(hh, nT[:, hh, :])
                if s == 3 and r is not None:
                    for hh in range(2):
                        copy_turned(hh, m_pT[:, hh, :], turn[hh][:, 0:3 * P])
                if s == 4:
                    if q is not None:
                        copy_turned(0, rT, turn[0][0:MLA_ROPE, :].rearrange("p (h t) -> p h t", t=TOKENS))
                    if r is not None:
                        wait_turned(1)
                        act.activation(xT_hi[:, kt, :], turn[1].rearrange("p (k t) -> p k t", t=TOKENS), copy).then_inc(turn_hi, 1)

            for p in range(2):
                for s in range(5):
                    pair_step(s, 0 if p else None, None)
                    if s < 4:
                        split_hi()
            with t.rounds(3, LATENT) as i:
                for p in range(2):
                    for s in range(5):
                        pair_step(s, 1 - p, p, bass.ds(i * 4 + 2 * p, 2))
                        if s < 4:
                            split_hi()
            for s in range(5):
                pair_step(s, 1, 0, slice(12, 14))
                if s < 4:
                    split_hi()
            for s in range(5):
                pair_step(s, None, 1, slice(14, 16))
                if s < 4:
                    split_hi()
            act.dma_start(final_row, a["final_norm_g_2"].partition_broadcast(P)).then_inc(row_landed, 16)

            for s in range(8, 33):
                if s in (20, 28):
                    h_squares(s // 8 - 2)
                if s < 32 - AHEAD:
                    split_hi()
            for n in (2, 3):
                h_squares(n)

        @block.vector
        def _(dve):
            t = Tally(dve)
            dve.sem_inc(ada_taken, ADA_SLOTS)
            t.nth(ada_taken, ADA_SLOTS)
            for b in range(2):
                t.nth(panel_taken[b])
                t.nth(score_taken[b])

            def split_lo(words=CHUNK):
                k = t.count(lo_ready)
                dve.wait_ge(hi_ready, t.nth(hi_ready))
                t.nth(multiplied)
                dve.tensor_tensor(lo[:, k % HI_CHUNKS, 0:words], raw[:, k // 2 % RAW_SLOTS, k % 2 * CHUNK:k % 2 * CHUNK + words],
                                  hi[:, k % HI_CHUNKS, 0:words].bitcast(F32), ALU.subtract).then_inc(lo_ready, 1)
                t.nth(lo_ready)

            def chunks_done(ahead=AHEAD):
                dve.wait_ge(multiplied, t.now(multiplied, RAW_CHUNKS - ahead))

            def panel_done(b):
                dve.wait_ge(panel_taken[b], t.now(panel_taken[b]))

            def panel_by_act(b):
                dve.wait_ge(panel_taken[b], t.nth(panel_taken[b]))

            def steps_done():
                dve.wait_ge(dve_step, t.now(dve_step))

            def wait_rstd():
                dve.wait_ge(rstd_ready, t.nth(rstd_ready))

            def wait_scored(b):
                dve.wait_ge(scored[b], t.nth(scored[b]))

            def normalised(n):
                at = slice(n * N, (n + 1) * N)
                for m in range(TILES):
                    done = dve.tensor_scalar(acc[:, m, at], h[:, m, at], st_rstd[:, m:m + 1], None, ALU.mult)
                done.then_inc(xs_ready, 1)

            def turned_hi():
                dve.wait_ge(turn_hi, t.nth(turn_hi))

            def two(bank):
                return bank.rearrange("p (k t) -> p k t", t=TOKENS)

            def lo_plain(c, y_hi, y_lo, kt):
                turned_hi()
                dve.tensor_tensor(y_lo[:, kt, :], two(turn[c % 2]), y_hi[:, kt, :].bitcast(F32),
                                  ALU.subtract).then_inc(turn_taken[c % 2], 1)

            def lo_scaled(b, y_hi, y_lo, gains):
                turned_hi()
                for k in range(2):
                    done = dve.scalar_tensor_tensor(y_lo(k), turn[b][:, k * TOKENS:(k + 1) * TOKENS], gains(k),
                                                    y_hi(k).bitcast(F32), ALU.mult, ALU.subtract)
                done.then_inc(turn_taken[b], 1)

            def lo_norm(c, col):
                lo_scaled(c % 2, lambda k: xT_hi[:, 2 * c + k, :], lambda k: xT_lo[:, 2 * c + k, :],
                          lambda k: cols[:, col + 2 * c + k:col + 2 * c + k + 1])

            def lo_mod(c):
                turned_hi()
                b, kt = c % 2, slice(2 * c, 2 * c + 2)
                for k in range(2):
                    done = dve.tensor_scalar(shift_tmp[:, b, k * TOKENS:(k + 1) * TOKENS], turn[b][:, k * TOKENS:(k + 1) * TOKENS],
                                             mods[:, 1, 2 * c + k:2 * c + k + 1], mods[:, 0, 2 * c + k:2 * c + k + 1],
                                             ALU.mult, ALU.add)
                done.then_inc(dve_step, 1)
                dve.wait_ge(dve_step, t.nth(dve_step))
                dve.tensor_tensor(xT_lo[:, kt, :], two(shift_tmp[:, b, :]), xT_hi[:, kt, :].bitcast(F32),
                                  ALU.subtract).then_inc(turn_taken[b], 1)

            def residual(n):
                at = slice(n * N, (n + 1) * N)
                for m in range(TILES):
                    done = dve.scalar_tensor_tensor(h[:, m, at], acc[:, m, at], st_rstd[:, m:m + 1], h[:, m, at],
                                                    ALU.mult, ALU.add)
                done.then_inc(h_ready, 1)

            def by_rms(dst, src):
                for m in range(TILES):
                    done = dve.tensor_scalar(dst(m), src(m), st_rstd[:, m:m + 1], None, ALU.mult)
                return done

            def row_of(ap):
                return ap.unsqueeze(1).broadcast_to([P, TILES, ap.shape[1]])

            def ada_step(kt, c):
                slot = t.count(ada_taken) % ADA_SLOTS
                dve.wait_ge(ada_landed[slot], t.nth(ada_landed[slot], ADA_LANDED))
                dve.wait_ge(ada_taken, t.now(ada_taken))
                piece = ada_acc[:, c * ADA_CHUNK:(c + 1) * ADA_CHUNK]
                dve.scalar_tensor_tensor(piece, ada_ring[:, slot, :], c_act[:, kt], piece, ALU.mult, ALU.add).then_inc(ada_taken, 1)
                t.nth(ada_taken)

            def ada_steps(s, at, late, k0):
                for n in range(2 * ADA_CHUNKS):
                    if min(at[n] + late, at[-1] + 1) == s:
                        ada_step(k0(n // ADA_CHUNKS), n % ADA_CHUNKS)

            def rotate(x1, x2, y1, y2, cos, sin, tmp, taken):
                dve.tensor_tensor(y1, x1, cos, ALU.mult)
                dve.tensor_tensor(y2, x2, cos, ALU.mult)
                dve.tensor_tensor(tmp[0], x2, sin, ALU.mult)
                dve.tensor_tensor(tmp[1], x1, sin, ALU.mult).then_inc(taken, 1)
                dve.wait_ge(taken, t.nth(taken))
                dve.tensor_tensor(y1, y1, tmp[0], ALU.subtract)
                dve.tensor_tensor(y2, y2, tmp[1], ALU.add).then_inc(roped, 1)

            def masked_scores(j0, banks, sm, scale):
                for n, b in enumerate(banks):
                    wait_scored(b)
                    dve.scalar_tensor_tensor(sm[:, j0 + n, :], score[b][:, 0:3 * P], scale, mask[:], ALU.mult,
                                             ALU.add).then_inc(score_taken[b], 1)
                    t.nth(score_taken[b])
                for b in banks:
                    dve.wait_ge(score_taken[b], t.now(score_taken[b]))
                pair = slice(j0, j0 + 2)
                dve.tensor_reduce(st_max[:, pair, 0], sm[:, pair, 0:P], AXIS_X, ALU.max)
                dve.tensor_reduce(st_max[:, pair, 1], sm[:, pair, P:3 * P], AXIS_X, ALU.max).then_inc(dve_step, 1)
                dve.wait_ge(dve_step, t.nth(dve_step))
                dve.tensor_scalar(st_neg[:, pair, :], st_max[:, pair, :], -1.0, None, ALU.mult).then_inc(max_ready, 1)

            def normalise(j0, pr, ready):
                dve.wait_ge(exp_ready, t.nth(exp_ready))
                pair = slice(j0, j0 + 2)
                dve.reciprocal(st_inv[:, pair, :], st_den[:, pair, :]).then_inc(dve_step, 1)
                dve.wait_ge(dve_step, t.nth(dve_step))
                for q, at in ((0, slice(0, P)), (1, slice(P, 3 * P))):
                    part = pr[:, pair, at]
                    done = dve.tensor_tensor(part, part, st_inv[:, pair, q:q + 1].broadcast_to([P, 2, at.stop - at.start]), ALU.mult)
                done.then_inc(ready, 1)
                t.nth(ready)

            wait_scored(0)
            dve.tensor_copy(cols[:, 0:KT], score[0][:, 0:KT]).then_inc(score_taken[0], 1)
            dve.wait_ge(score_taken[0], t.nth(score_taken[0]))
            lo_norm(0, COL_MIX)
            lo_norm(1, COL_MIX)
            for _ in range(AHEAD):
                split_lo()
            for s in range(8):
                if s < 6:
                    lo_norm(s + 2, COL_MIX)
                split_lo()
            wait_scored(1)
            dve.tensor_copy(cols[:, KT:COLS], score[1][:, KT:COLS]).then_inc(score_taken[1], 1)
            dve.wait_ge(score_taken[1], t.nth(score_taken[1]))
            dve.tensor_scalar(cols[:, COL_SUB:COL_SUB + 2], cols[:, COL_SUB:COL_SUB + 2], 1.0 - LAMBDA_INIT, None, ALU.mult)
            dve.wait_ge(late_landed, 16 * N_EARLY)
            dve.tensor_tensor(lam_prods, lambdas[:, :, 0, :], lambdas[:, :, 1, :], ALU.mult).then_inc(dve_step, 1)
            dve.wait_ge(dve_step, t.nth(dve_step))
            dve.tensor_reduce(st_lam, lam_prods, AXIS_X, ALU.add).then_inc(lam_sums, 1)
            dve.wait_ge(lam_exps, 1)
            dve.scalar_tensor_tensor(neg_lam, st_lam[:, 1:2], -LAMBDA_INIT, st_lam[:, 0:1], ALU.add, ALU.subtract)
            wait_rstd()

            def q_copy():
                chunks_done()
                by_rms(lambda m: qk[:, m, 0:N], lambda m: panel[0][:, m, :]).then_inc(panel_taken[0], 1)
                t.nth(panel_taken[0])

            def k_copy_and_rotate():
                chunks_done()
                src = panel[1].rearrange("p m (h d) -> p m h d", d=HEAD)
                dst = qk[:, :, N:2 * N].rearrange("p m (h d) -> p m h d", d=HEAD)
                rot = 2 * ROT_HALF
                by_rms(lambda m: dst[:, m, :, 0:rot], lambda m: src[:, m, :, 0:rot]).then_inc(dve_step, 1)
                by_rms(lambda m: dst[:, m, :, rot:HEAD], lambda m: src[:, m, :, rot:HEAD]).then_inc(panel_taken[1], 1)
                t.nth(panel_taken[1])
                dve.wait_ge(dve_step, t.nth(dve_step))
                heads = qk.rearrange("p m (h d) -> p (m h) d", d=HEAD)
                x1, x2 = heads[:, :, 0:ROT_HALF], heads[:, :, ROT_HALF:rot]
                cos, sin = (rope1[:, i, :].rearrange("p (h r) -> p h r", r=ROT_HALF) for i in range(2))
                for n, (x, y) in enumerate(((x1, cos), (x2, sin), (x2, cos), (x1, sin))):
                    done = dve.tensor_tensor(rope_tmp[:, n], x, y, ALU.mult)
                done.then_inc(dve_step, 1)
                dve.wait_ge(dve_step, t.nth(dve_step))
                dve.tensor_tensor(x1, rope_tmp[:, 0], rope_tmp[:, 1], ALU.subtract)
                dve.tensor_tensor(x2, rope_tmp[:, 2], rope_tmp[:, 3], ALU.add).then_inc(roped, 1)

            def v_copy(b):
                chunks_done()
                by_rms(lambda m: v_sb[:, m, :], lambda m: panel[b][:, m, :]).then_inc(panel_taken[b], 1)
                t.nth(panel_taken[b])

            with t.rounds(2, ATTENTION) as g:
                for s in range(48):
                    if s in (0, 16):
                        q_copy()
                    if s in (8, 24):
                        k_copy_and_rotate()
                    if s in (14, 15, 30, 31):
                        masked_scores(0 if s in (14, 30) else 2, (0, 1), sm, HEAD ** -0.5)
                    if s == 18:
                        for j0 in (0, 2):
                            normalise(j0, pr, dve_step)
                        steps_done()
                        maps = pr.rearrange("p (h c) n -> p h c n", c=2)
                        dve.scalar_tensor_tensor(maps[:, :, 0, :], maps[:, :, 1, :], neg_lam, maps[:, :, 0, :], ALU.mult,
                                                 ALU.add).then_inc(probs_ready, 1)
                        t.nth(probs_ready)
                    if s == 32:
                        v_copy(0)
                    if s in (33, 34):
                        normalise(2 * (s - 33), pr, probs_ready)
                    if s == 36:
                        wait_rstd()
                        for hh in range(2):
                            wait_scored(hh)
                            dve.tensor_tensor(ob[:, :, hh, :], score[hh].rearrange("p (m d) -> p m d", d=DIFF_V),
                                              st_drstd[:, hh, :].unsqueeze(2).broadcast_to([P, TILES, DIFF_V]),
                                              ALU.mult).then_inc(score_taken[hh], 1)
                            t.nth(score_taken[hh])
                    if s == 40:
                        v_copy(1)
                        for hh in range(2):
                            def kt(k):
                                return bass.ds(g * 4 + (hh * 2 + k), 1)
                            lo_scaled(hh, lambda k: yT_hi[1][:, kt(k), :].rearrange("p a t -> p (a t)"),
                                      lambda k: yT_lo[1][:, kt(k), :].rearrange("p a t -> p (a t)"),
                                      lambda k: cols[:, COL_SUB + k:COL_SUB + k + 1])
                    if s == 43:
                        for b in range(2):
                            turned_hi()
                            wait_scored(b)
                            pair = bass.ds(g * 4 + 2 * b, 2)
                            dve.tensor_tensor(yT_lo[0][:, pair, :], two(score[b]), yT_hi[0][:, pair, :].bitcast(F32),
                                              ALU.subtract).then_inc(score_taken[b], 1)
                            t.nth(score_taken[b])
                    split_lo()

            def mix_step(s, at):
                if s == 4:
                    panel_by_act(0)
                    chunks_done()
                    dve.tensor_tensor(gated, panel[1], sig[0], ALU.mult).then_inc(panel_taken[1], 1)
                    t.nth(panel_taken[1])
                if s == 16:
                    panel_by_act(0)
                    chunks_done()
                    dve.tensor_tensor(sig[1], panel[1], sig[1], ALU.mult).then_inc(panel_taken[1], 1)
                    t.nth(panel_taken[1])
                    panel_done(1)
                    dve.tensor_tensor(acc[:, :, at], gated, sig[1], ALU.add).then_inc(mixed_ready, 1)

            def lo_mixed(c):
                lo_plain(c, xT_hi, xT_lo, slice(2 * c, 2 * c + 2))

            with t.rounds(3, MIX) as n:
                for s in range(24):
                    mix_step(s, bass.ds(n * N, N))
                    split_lo()
            for s in range(17):
                mix_step(s, slice(3 * N, 4 * N))
                if s >= 15:
                    lo_mixed(s - 15)
                if s < 16:
                    split_lo()

            angle, cos_in = trig[:, 1, :], trig[:, 0, :]

            def angle_step(i):
                if i:
                    steps_done()
                if i == 0:
                    dve.wait_ge(late_landed, 16 * (N_EARLY + N_LATE))
                    done = dve.tensor_copy(st_pos, st_ipos)
                elif i == 1:
                    for m in range(TILES):
                        for at, n in ((0, RET_DK), (2 * RET_DK, MLA_ROPE)):
                            part = slice(at + m * n, at + (m + 1) * n)
                            done = dve.tensor_scalar(angle[:, part], freq[:, part], st_pos[:, m:m + 1], None, ALU.mult)
                elif i == 2:
                    done = dve.tensor_scalar(turns_all, angle, 1.0 / TURN, ROUND, ALU.mult, ALU.add)
                elif i == 3:
                    done = dve.tensor_scalar(turns_all, turns_all, -ROUND, None, ALU.add)
                elif i == 4:
                    done = dve.tensor_scalar(turns_hi, turns_all, 1.0 / MANY, ROUND, ALU.mult, ALU.add)
                elif i == 5:
                    done = dve.tensor_scalar(turns_hi, turns_hi, -ROUND, MANY, ALU.add, ALU.mult)
                elif i == 6:
                    done = dve.tensor_tensor(turns_all, turns_all, turns_hi, ALU.subtract)
                elif i < 13:
                    turns = (turns_hi, turns_all)[(i - 7) % 2]
                    done = dve.scalar_tensor_tensor(angle, turns, -TURN_PARTS[(i - 7) // 2], angle, ALU.mult, ALU.add)
                elif i == 13:
                    done = dve.tensor_scalar(angle, angle, HALF_TURN, -HALF_TURN, ALU.min, ALU.max)
                elif i == 14:
                    done = dve.scalar_tensor_tensor(cos_in, angle, -1.0, angle, ALU.mult, ALU.max)
                elif i == 15:
                    dve.tensor_scalar(cos_in, cos_in, -1.0, TURN / 4, ALU.mult, ALU.add).then_inc(angles_ready, 1)
                if i < 15:
                    done.then_inc(dve_step, 1)
                    t.nth(dve_step)

            dve.wait_ge(row_landed, 16)
            for s in range(33):
                if s < 6:
                    lo_mixed(s + 2)
                if s in (8, 16, 24, 32):
                    n = s // 8 - 1
                    at = slice(n * N, (n + 1) * N)
                    dve.wait_ge(squares_done, t.nth(squares_done))
                    dve.tensor_tensor(acc[:, :, at], panel[n % 2], row_of(row[:, at]), ALU.mult).then_inc(panel_taken[n % 2], 1)
                    t.nth(panel_taken[n % 2])
                elif 9 <= s < 27:
                    angle_step(s - 9 - s // 17 - s // 25)
                if s < 32:
                    split_lo()
            for b in range(2):
                panel_done(b)
            wait_rstd()
            residual(0)
            residual(1)
            turned_hi()
            wait_scored(1)
            dve.tensor_tensor(pT_lo[:], two(score[1]), pT_hi[:].bitcast(F32), ALU.subtract).then_inc(score_taken[1], 1)
            t.nth(score_taken[1])
            lo_norm(0, COL_MLP)
            residual(2)
            lo_norm(1, COL_MLP)
            residual(3)

            def up_lo(b, k):
                for j in range(2):
                    lo_plain(j, yT_hi[k], yT_lo[k], slice(b * 4 + 2 * j, b * 4 + 2 * j + 2))

            def by_act(b):
                t.nth(panel_taken[b])

            def down_panel(s):
                if s in (4, 8, 12, 16):
                    n = s // 4 - 1
                    chunks_done()
                    part = acc[:, :, n * N:(n + 1) * N]
                    dve.tensor_tensor(part, panel[n % 2], part, ALU.add).then_inc(panel_taken[n % 2], 1)
                    t.nth(panel_taken[n % 2])

            def times_row(n):
                dve.wait_ge(squares_done, t.nth(squares_done))
                at = slice(n * N, (n + 1) * N)
                dve.tensor_tensor(acc[:, :, at], acc[:, :, at], row_of(row[:, at]), ALU.mult).then_inc(dve_step, 1)
                t.nth(dve_step)

            for s in range(32):
                if s < 6:
                    lo_norm(s + 2, COL_MLP)
                if s == 2:
                    dve.wait_ge(c_ready, 1)
                    dve.wait_ge(ada_row, 16)
                ada_steps(s, ada_at(32), 2, lambda k: slice(k, k + 1))
                if s in (8, 16, 24):
                    by_act(s // 8 % 2 ^ 1)
                if s == 8:
                    wait_rstd()
                    t.nth(squares_done, 4)
                    dve.memset(acc[:], 0.0)
                if s in (11, 19, 27):
                    up_lo(s // 8 % 2 ^ 1, s // 20)
                split_lo()
            with t.rounds(3, FEED) as i:
                for s in range(64):
                    ada_steps(s % 32, ada_at(32), 2, lambda k: bass.ds(i * 4 + (2 + s // 32 * 2 + k), 1))
                    if s in (0, 32):
                        by_act(1)
                    if s in (24, 56):
                        by_act(0)
                    if s in (3, 27, 35, 59):
                        up_lo(1 if s in (3, 35) else 0, 1 if s in (3, 59) else 0)
                    down_panel(s % 32)
                    split_lo()
            for s in range(32):
                ada_steps(s, ada_at(32), 2, lambda k: slice(14 + k, 15 + k))
                if s == 0:
                    by_act(1)
                if s == 3:
                    up_lo(1, 1)
                down_panel(s if s <= 16 else s - 16)
                if s == 21:
                    dve.wait_ge(row_landed, 16 * 2)
                if s in (22, 26, 30):
                    times_row((s - 22) // 4)
                split_lo(CHUNK if s + AHEAD < 32 else N)
            down_panel(16)
            split_lo(N)
            times_row(3)
            split_lo(N)
            steps_done()
            wait_rstd()
            for s in range(2, 8):
                if s < 5:
                    residual(s - 2)
                elif s < 7:
                    lo_norm(s - 5, COL_PLE)
                else:
                    residual(3)
                split_lo(N if s + AHEAD < 8 else CHUNK)
            for b in range(2):
                t.nth(panel_taken[b], 2)

            for s in range(33):
                if s < 6:
                    lo_norm(s + 2, COL_PLE)
                if s == 8:
                    for b in range(2):
                        panel_done(b)
                    wait_rstd()
                    t.nth(squares_done, 4)
                    dve.wait_ge(row_landed, 16 * 3)
                if s in (8, 16, 24, 32):
                    n = s // 8 - 1
                    at = slice(n * N, (n + 1) * N)
                    panel_by_act(n % 2)
                    dve.tensor_tensor(acc[:, :, at], acc[:, :, at], e_sb[:, :, at], ALU.mult).then_inc(ple_ready, 1)
                if s in (10, 18, 26):
                    times_row(s // 8 - 1)
                if s < 32:
                    split_lo()
            times_row(3)
            steps_done()
            wait_rstd()
            for n in range(4):
                residual(n)

            def modulation(layer, parts):
                wait_scored(0)
                dve.tensor_copy(mods[:, 0:parts, :], score[0][:, 0:parts * KT].rearrange("p (a k) -> p a k", k=KT)).then_inc(score_taken[0], 1)
                dve.wait_ge(score_taken[0], t.nth(score_taken[0]))
                gain = cols[:, COL_NORM + layer * KT:COL_NORM + (layer + 1) * KT]
                dve.scalar_tensor_tensor(mods[:, 1, :], mods[:, 1, :], 1.0, gain, ALU.add, ALU.mult).then_inc(mods_ready, 1)

            def gate_row(n):
                wait_scored(n % 2)
                dve.tensor_copy(row[:, n * N:(n + 1) * N], score[n % 2]).then_inc(score_taken[n % 2], 1)
                t.nth(score_taken[n % 2])

            def ret_rotate():
                chunks_done()
                src, dst = (x.rearrange("p m (c x f) -> p (m c) x f", c=2, x=2) for x in (panel[0], ret_qk))
                cos, sin = (trig[:, i, 0:2 * RET_DK].rearrange("p (n f) -> p n f", f=RET_DK // 2) for i in range(2))
                tmp = [ret_sg[:, i, :].rearrange("p (n f) -> p n f", f=RET_DK // 2) for i in range(2)]
                rotate(src[:, :, 0, :], src[:, :, 1, :], dst[:, :, 0, :], dst[:, :, 1, :], cos, sin, tmp, panel_taken[0])

            def ret_decay():
                wait_scored(0)
                dve.wait_ge(dm_landed, t.nth(dm_landed, 16))
                dve.tensor_tensor(ret_sT, score[0][:, 0:3 * P], ret_dm, ALU.mult).then_inc(score_taken[0], 1)
                t.nth(score_taken[0])

            def ret_v_copy():
                chunks_done()
                dve.tensor_copy(ret_v, panel[1]).then_inc(panel_taken[1], 1)
                t.nth(panel_taken[1])

            def ret_moments():
                for m in range(TILES):
                    wait_scored(m)
                    done = dve.bn_stats(st_bn[:, m, :], score[m])
                done.then_inc(dve_step, 1)
                dve.wait_ge(dve_step, t.nth(dve_step))
                if t.i is not None:
                    dve.sem_inc(dve_waited, 1)
                dve.bn_aggr(st_mv[:, 0, :], st_bn[:, 0, :])
                dve.bn_aggr(st_mv[:, 1, :], st_bn[:, 1, :]).then_inc(sums_ready, 1)

            def ret_group_norm():
                wait_rstd()
                for m in range(TILES):
                    dve.tensor_scalar(ret_yn[:, m, :], score[m], st_mv[:, m, 0:1], st_rstd[:, m:m + 1], ALU.subtract,
                                      ALU.mult).then_inc(score_taken[m], 1)
                    t.nth(score_taken[m])

            def ret_gated():
                dve.wait_ge(silu_ready, t.nth(silu_ready))
                for b in range(2):
                    dve.wait_ge(score_taken[b], t.now(score_taken[b]))
                dve.tensor_tensor(ret_sg, ret_sg, ret_yn, ALU.mult).then_inc(yg_ready, 1)

            def ret_out_panel(n, ahead=AHEAD):
                chunks_done(ahead)
                b = (1 + n) % 2
                part = acc[:, :, n * N:(n + 1) * N]
                dve.tensor_tensor(part, panel[b], part, ALU.add).then_inc(panel_taken[b], 1)
                t.nth(panel_taken[b])

            def ret_y_lo(gains):
                for j in range(2):
                    lo_scaled(j, lambda k: yT_hi[0][:, 2 * j + k, :], lambda k: yT_lo[0][:, 2 * j + k, :],
                              lambda k: gains(2 * j + k))

            wait_rstd()
            normalised(0)
            normalised(1)
            modulation(0, 3)
            lo_mod(0)
            normalised(2)
            lo_mod(1)
            normalised(3)
            for s in range(24):
                if s < 6:
                    lo_mod(s + 2)
                if s == ADA_FIRST[0] + 2:
                    dve.wait_ge(ada_row, 16 * 2)
                ada_steps(s, ADA_FIRST, 2, lambda k: slice(k, k + 1))
                if s == 8:
                    dve.wait_ge(trig_ready, 1)
                    ret_rotate()
                if s == 15:
                    ret_decay()
                if s == 16:
                    ret_v_copy()
                if s == 19:
                    ret_moments()
                if s == 21:
                    ret_group_norm()
                split_lo()
            ret_gated()
            dve.wait_ge(acc_zeroed, 1)
            with t.rounds(RET_HEADS - 1, RETAIN) as i:
                for s in range(32):
                    ada_steps(s, ada_at(32), 2, lambda k: bass.ds(i * 2 + (2 + k), 1))
                    if s == 3:
                        ret_y_lo(lambda kt: cols[:, bass.ds(i * 4 + (COL_GN + kt), 1)])
                    if s == 8:
                        ret_rotate()
                    if s in (10, 12, 14, 16):
                        ret_out_panel((s - 10) // 2)
                    if s == 15:
                        ret_decay()
                    if s == 24:
                        ret_v_copy()
                    if s == 27:
                        ret_moments()
                    if s == 29:
                        ret_group_norm()
                    split_lo()
                ret_gated()
            gate_row(2)
            gate_row(3)
            ret_y_lo(lambda kt: cols[:, COL_GN + (RET_HEADS - 1) * 4 + kt:COL_GN + (RET_HEADS - 1) * 4 + kt + 1])
            gate_row(0)
            gate_row(1)
            for s in range(9):
                if s in (2, 4, 6, 8):
                    n = s // 2 - 1
                    ret_out_panel(n, min(AHEAD, 8 - s))
                    for b in range(2):
                        panel_done(b)
                        dve.wait_ge(score_taken[b], t.now(score_taken[b]))
                    at = slice(n * N, (n + 1) * N)
                    dve.tensor_tensor(acc[:, :, at], acc[:, :, at], row_of(row[:, at]), ALU.mult).then_inc(dve_step, 1)
                    dve.wait_ge(dve_step, t.nth(dve_step))
                    dve.tensor_tensor(h[:, :, at], h[:, :, at], acc[:, :, at], ALU.add).then_inc(h_ready, 1)
                if s < 8 - AHEAD:
                    split_lo()
            def latent():
                wait_rstd()
                for m in range(TILES):
                    done = dve.tensor_scalar(lat[:, m, :], panel[0][:, m, :], st_rstd[:, m:m + 1], None, ALU.mult)
                done.then_inc(panel_taken[0], 1)
                t.nth(panel_taken[0])

            def lat_lo(kt, col):
                for j in range(2):
                    lo_scaled(j, lambda k: yT_hi[0][:, kt + 2 * j + k, :], lambda k: yT_lo[0][:, kt + 2 * j + k, :],
                              lambda k: cols[:, col + 2 * j + k:col + 2 * j + k + 1])

            mla_cos, mla_sin = (trig[:, i, 2 * RET_DK:640].rearrange("p (m h f) -> p m h f", m=TILES, h=2) for i in range(2))
            half = MLA_ROPE // 2
            split_lo()
            split_lo()
            wait_rstd()
            normalised(0)
            normalised(1)
            modulation(1, 2)
            lo_mod(0)
            normalised(2)
            lo_mod(1)
            normalised(3)
            split_lo()
            for s in range(18):
                if s < 6:
                    lo_mod(s + 2)
                if s == 8:
                    latent()
                if s == 11:
                    gate_row(0)
                    gate_row(1)
                if s == 10:
                    by_act(1)
                if s == 14:
                    lat_lo(4, COL_KV)
                    tmp = [mla_tmp[:, i, 0:TILES * half].rearrange("p (m f) -> p m f", f=half) for i in range(2)]
                    rotate(kr_in[:, :, 0:half], kr_in[:, :, half:2 * half], kr[:, :, 0:half], kr[:, :, half:2 * half],
                           mla_cos[:, :, 0, :], mla_sin[:, :, 0, :], tmp, dve_step)
                split_lo(N if s + AHEAD in (8, 9) else CHUNK)
            latent()
            with t.rounds(2, WIDE) as n:
                for s in range(16):
                    split_lo()
                for b in range(2):
                    t.nth(panel_taken[b])
            lat_lo(0, COL_Q)
            gate_row(2)
            gate_row(3)

            def q_copy_and_rotate(p):
                chunks_done()
                src, dst = (x.rearrange("p m (h d) -> p m h d", h=2) for x in (panel[0][:, :, 0:MLA_QW], q_sb[p]))
                dve.tensor_copy(dst[:, :, :, 0:MLA_NOPE], src[:, :, :, 0:MLA_NOPE])
                x1, x2 = slice(MLA_NOPE, MLA_NOPE + half), slice(MLA_NOPE + half, MLA_NOPE + 2 * half)
                tmp = [mla_tmp[:, i, :].rearrange("p (m h f) -> p m h f", m=TILES, h=2) for i in range(2)]
                rotate(src[:, :, :, x1], src[:, :, :, x2], dst[:, :, :, x1], dst[:, :, :, x2], mla_cos, mla_sin, tmp, panel_taken[0])

            def pair_step(s, p, r, cols_r=None, kt=None):
                if s == 0 and r is not None:
                    masked_scores(0, (1, 0), m_sm, (MLA_NOPE + MLA_ROPE) ** -0.5)
                if s == 1 and r is not None:
                    dve.wait_ge(pair_exps_ready, t.nth(pair_exps_ready))
                    dve.reciprocal(st_inv[:, 0:2, :], st_den[:, 0:2, :]).then_inc(dve_step, 1)
                if s == 2 and p is not None:
                    q_copy_and_rotate(p)
                if s == 4:
                    if r is not None:
                        dve.wait_ge(dve_step, t.nth(dve_step))
                        wait_scored(0)
                        for hh in range(2):
                            for m in range(TILES):
                                done = dve.scalar_tensor_tensor(
                                    og[:, m, hh * P:(hh + 1) * P], score[0][:, (2 * m + hh) * P:(2 * m + hh + 1) * P],
                                    st_inv[:, hh, m:m + 1], sgm[:, m, cols_r(hh)], ALU.mult, ALU.mult)
                        done.then_inc(score_taken[0], 1)
                        t.nth(score_taken[0])
                    if p is not None:
                        chunks_done()
                        dve.tensor_copy(kv_sb[p], panel[1]).then_inc(panel_taken[1], 1)
                        t.nth(panel_taken[1])
                    if r is not None:
                        lo_plain(1, xT_hi, xT_lo, kt)

            for p in range(2):
                for s in range(5):
                    pair_step(s, p, None)
                    if s < 4:
                        split_lo()
            for b in range(2):
                panel_done(b)
            with t.rounds(3, LATENT) as i:
                for p in range(2):
                    for s in range(5):
                        pair_step(s, p, p, lambda hh: bass.ds(i * 4 * P + (2 * p + hh) * P, P), bass.ds(i * 4 + 2 * p, 2))
                        if s < 4:
                            split_lo()
            for p in range(2):
                pair = 6 + p
                for s in range(5):
                    pair_step(s, None, p, lambda hh: slice((2 * pair + hh) * P, (2 * pair + hh + 1) * P), slice(2 * pair, 2 * pair + 2))
                    if s < 4:
                        split_lo()

            for s in range(8, 33):
                if s in (10, 16, 24, 32):
                    n = s // 8 - 1
                    dve.wait_ge(multiplied, t.now(multiplied, RAW_CHUNKS - (AHEAD if n < 3 else 0)))
                    at, b = slice(n * N, (n + 1) * N), n % 2
                    dve.tensor_tensor(acc[:, :, at], panel[b], row_of(row[:, at]), ALU.mult).then_inc(panel_taken[b], 1)
                    t.nth(panel_taken[b])
                    panel_done(b)
                    dve.tensor_tensor(h[:, :, at], h[:, :, at], acc[:, :, at], ALU.add).then_inc(h_ready, 1)
                if s < 32 - AHEAD:
                    split_lo()
            dve.wait_ge(row_landed, 16 * 4)
            wait_rstd()
            for m in range(TILES):
                for at in (slice(0, D // 2), slice(D // 2, D)):
                    dve.scalar_tensor_tensor(acc[:, m, at], h[:, m, at], st_rstd[:, m:m + 1], final_row[:, at], ALU.mult,
                                             ALU.mult).then_inc(out_ready, 1)

        @block.gpsimd
        def _(pool):
            t = Tally(pool)
            pool.memset(ones[:], 1.0).then_inc(ones_set, 1)
            pool.memset(eps[:], EPS)
            pool.memset(neg_half[:], -0.5).then_inc(pool_step, 1)
            pool.wait_ge(pool_step, t.nth(pool_step))

            def rstd_of(dst, mean):
                pool.tensor_tensor(dst, mean, eps[:, 0:dst.shape[1]], ALU.add).then_inc(pool_step, 1)
                pool.wait_ge(pool_step, t.nth(pool_step))
                pool.tensor_tensor(dst, dst, neg_half[:, 0:dst.shape[1]], ALU.pow).then_inc(rstd_ready, 1)

            def rstd_of_sum(width):
                pool.tensor_scalar(st_rstd, st_sum, 1.0 / width, EPS, ALU.mult, ALU.add).then_inc(pool_step, 1)
                pool.wait_ge(pool_step, t.nth(pool_step))
                pool.tensor_tensor(st_rstd, st_rstd, neg_half[:, 0:TILES], ALU.pow).then_inc(rstd_ready, 1)

            def rstd(width):
                pool.wait_ge(sums_ready, t.nth(sums_ready))
                rstd_of_sum(width)

            def rstd_parts():
                pool.wait_ge(squares_done, t.nth(squares_done, 4))
                pool.tensor_tensor(st_parts[:, :, 0:2], st_parts[:, :, 0:2], st_parts[:, :, 2:4], ALU.add).then_inc(pool_step, 1)
                pool.wait_ge(pool_step, t.nth(pool_step))
                pool.tensor_tensor(st_sum, st_parts[:, :, 0], st_parts[:, :, 1], ALU.add).then_inc(pool_step, 1)
                pool.wait_ge(pool_step, t.nth(pool_step))
                rstd_of_sum(D)

            rstd(D)
            with t.rounds(2, ATTENTION):
                pool.wait_ge(sums_ready, t.nth(sums_ready))
                rstd_of(stats[:, 80:84], stats[:, 76:80])
            pool.wait_ge(mixed_ready, 4)
            pool.memset(ada_acc, 0.0).then_inc(ada_set, 1)
            for _ in range(6):
                rstd_parts()
            pool.wait_ge(mods_ready, 1)
            pool.memset(ada_acc, 0.0).then_inc(ada_set, 1)

            def group_rstd():
                pool.wait_ge(sums_ready, t.nth(sums_ready))
                rstd_of(st_rstd, st_mv[:, :, 1])

            t.nth(roped, 4)
            pool.wait_ge(roped, t.nth(roped))
            pool.memset(acc[:], 0.0).then_inc(acc_zeroed, 1)
            group_rstd()
            with t.rounds(RET_HEADS - 1, RETAIN):
                group_rstd()
            rstd_parts()
            rstd(MLA_RANK)
            rstd(MLA_RANK)
            rstd_parts()


def constants():
    import numpy as np

    i = np.arange(P)
    causal = np.where(i[None, :] <= i[:, None], 0.0, -3e38)
    mask = np.concatenate([causal, np.zeros((P, P)), causal], 1)
    theta = 1.0 / 500000.0 ** (np.arange(ROT_HALF) * 2.0 / (2 * ROT_HALF))
    angle = (np.arange(TOKENS, dtype=np.float32)[:, None] * theta.astype(np.float32)[None, :]).astype(np.float64)
    rope1 = np.stack([np.cos(angle), np.sin(angle)])
    rope1 = np.broadcast_to(rope1.reshape(2, TILES, P, 1, ROT_HALF), (2, TILES, P, 8, ROT_HALF))
    rope1 = rope1.transpose(2, 0, 1, 3, 4).reshape(P, 2, TILES * 8 * ROT_HALF)
    freq = [10000.0 ** (-np.arange(0, d, 2) / d) for d in (RET_DK, MLA_ROPE)]
    freq = np.concatenate([np.tile(f, 2 * TILES) for f in freq])
    log_gamma = np.log1p(-np.exp2(-5.0 - np.arange(RET_HEADS)))
    n, m = np.arange(TOKENS)[None, :], np.arange(TOKENS)[:, None]
    decay = np.where(n >= m, np.exp(log_gamma[:, None, None] * np.maximum(n - m, 0)), 0.0) * RET_DK ** -0.5
    decay = np.concatenate([decay[:, 0:P, :], decay[:, P:2 * P, P:2 * P]], 2)
    made = {"k_ident": np.eye(P), "k_mask": mask, "k_rope1": rope1, "k_freq": freq, "k_decay": decay}
    return {name: np.ascontiguousarray(x.astype(np.float32)) for name, x in made.items()}


INPUTS = ["x", "p", "w_in", "w_br_moba", "w_br_diff", "w_out", "lambda_q1", "lambda_k1", "lambda_q2", "lambda_k2",
          "diff_subln_g", "g_mix_pre", "g_mix_post", "w_up", "w_down", "g_mlp_pre", "g_mlp_post", "w_ple_proj",
          "w_ple_gate", "g_ple_pre", "g_ple_post", "c_2", "positions_2", "ada_w_2", "ada_b_2", "norm_g_2", "ret_w_in_2",
          "ret_gn_g_2", "ret_w_out_2", "mla_w_in_2", "mla_q_norm_g_2", "mla_w_uq_2", "mla_kv_norm_g_2",
          "mla_w_ukv_2", "mla_w_out_2", "final_norm_g_2"]


def kernel(**inputs):
    import concourse.bacc as bacc
    import numpy as np
    from concourse.bass_utils import run_bass_kernel_spmd

    nc = bacc.Bacc("TRN2", target_bir_lowering=False, num_devices=1, dynamic_dma_scratch_size=1024)
    arrays = {name: np.ascontiguousarray(inputs[name]) for name in INPUTS}
    arrays.update(constants())
    aps = {name: nc.dram_tensor(name, x.shape, mybir.dt.from_np(x.dtype), kind="ExternalInput").ap()
           for name, x in arrays.items()}
    out = nc.dram_tensor("out_0", (1, TOKENS, D), F32, kind="ExternalOutput").ap()
    build(nc, aps, out)
    r = run_bass_kernel_spmd(nc, [arrays], core_ids=[0])
    return r.results[0]["out_0"]
```
